# Optimizing a Trainium2 kernel written in Bass

```python
import math
import jax, jax.numpy as jnp
from jax import lax
import numpy as np

D_MODEL = 1024
BATCH = 1
SEQ = 512
DEPTH = 2

CHUNK = 64
N_MIXERS = 2
EPS = 1e-6
A_HEADS = 16
A_KV_HEADS = 4
A_GROUP = A_HEADS // A_KV_HEADS
A_HEAD_DIM = 64
A_WINDOW = 128
A_WIN_CHUNKS = A_WINDOW // CHUNK
A_BAND = A_WIN_CHUNKS * CHUNK
A_QKV_DIM = (A_HEADS + 2 * A_KV_HEADS) * A_HEAD_DIM
REL_BUCKETS = 32
REL_MAX_DIST = 128
B_HEADS = 4
B_KEY_DIM = D_MODEL // 2
B_VAL_DIM = D_MODEL
B_HK = B_KEY_DIM // B_HEADS
B_HV = B_VAL_DIM // B_HEADS
B_GATE_RANK = 16
B_GATE_NORM = 16.0
B_IN_DIM = 2 * B_KEY_DIM + 2 * B_VAL_DIM + B_GATE_RANK
D_FF = 2816
CONV_W = 3
N_A_LAYERS = (DEPTH + 1) // 2
N_B_LAYERS = DEPTH // 2
NEG = -1e30

kernel_name = "hybrid_swa_sink_gla_convffn"

def rmsnorm(x, g):
    xf = x.astype(jnp.float32)
    xf = xf * lax.rsqrt(jnp.mean(xf * xf, axis=-1, keepdims=True) + EPS)
    return (xf * g.astype(jnp.float32)).astype(x.dtype)

def t5_bucket(rel):
    nb = REL_BUCKETS // 2
    ret = np.where(rel > 0, nb, 0)
    n = np.abs(rel)
    max_exact = nb // 2
    n_f = np.maximum(n, 1).astype(np.float32)
    large = max_exact + (np.log(n_f / max_exact) / math.log(REL_MAX_DIST / max_exact)
                         * (nb - max_exact)).astype(np.int32)
    large = np.minimum(large, nb - 1)
    return (ret + np.where(n < max_exact, n, large)).astype(np.int32)

def swa_sink_attention(h, w_qkv, sinks, rel_bias, w_o):
    B, S, _ = h.shape
    nC = S // CHUNK
    qkv = h @ w_qkv
    q = qkv[..., :A_HEADS * A_HEAD_DIM]
    k = qkv[..., A_HEADS * A_HEAD_DIM:(A_HEADS + A_KV_HEADS) * A_HEAD_DIM]
    v = qkv[..., (A_HEADS + A_KV_HEADS) * A_HEAD_DIM:]
    q = q.reshape(B, nC, CHUNK, A_KV_HEADS, A_GROUP, A_HEAD_DIM)
    k = k.reshape(B, S, A_KV_HEADS, A_HEAD_DIM)
    v = v.reshape(B, S, A_KV_HEADS, A_HEAD_DIM)
    pad = (A_WIN_CHUNKS - 1) * CHUNK
    k_pad = jnp.pad(k, ((0, 0), (pad, 0), (0, 0), (0, 0)))
    v_pad = jnp.pad(v, ((0, 0), (pad, 0), (0, 0), (0, 0)))
    k_band = jnp.concatenate(
        [k_pad[:, i * CHUNK:i * CHUNK + S].reshape(B, nC, CHUNK, A_KV_HEADS, A_HEAD_DIM)
         for i in range(A_WIN_CHUNKS)], axis=2)
    v_band = jnp.concatenate(
        [v_pad[:, i * CHUNK:i * CHUNK + S].reshape(B, nC, CHUNK, A_KV_HEADS, A_HEAD_DIM)
         for i in range(A_WIN_CHUNKS)], axis=2)
    jj = np.arange(A_BAND)
    key_chunk = np.arange(nC)[:, None] - (A_WIN_CHUNKS - 1) + jj[None, :] // CHUNK
    valid = jnp.asarray(key_chunk >= 0)
    rel = jj[None, :] - pad - np.arange(CHUNK)[:, None]
    bias = rel_bias.astype(jnp.float32)[jnp.asarray(t5_bucket(rel))]
    bias = jnp.transpose(bias, (2, 0, 1)).reshape(A_KV_HEADS, A_GROUP, 1, CHUNK, A_BAND)
    scores = jnp.einsum('bnqhgd,bnjhd->bhgnqj', q, k_band).astype(jnp.float32)
    scores = scores * (A_HEAD_DIM ** -0.5) + bias
    scores = jnp.where(valid[None, None, None, :, None, :], scores, NEG)
    sink = sinks.astype(jnp.float32).reshape(A_KV_HEADS, A_GROUP, 1, 1)
    m = jnp.maximum(scores.max(axis=-1), sink)
    p = jnp.exp(scores - m[..., None])
    p = p / (p.sum(axis=-1) + jnp.exp(sink - m))[..., None]
    out = jnp.einsum('bhgnqj,bnjhd->bnqhgd', p.astype(v.dtype), v_band)
    return out.reshape(B, S, A_HEADS * A_HEAD_DIM) @ w_o

def gla(h, w_in, w_gate, b_gate, norm_w, w_o):
    B, S, _ = h.shape
    nC = S // CHUNK
    proj = h @ w_in
    o0, o1, o2, o3 = B_KEY_DIM, 2 * B_KEY_DIM, 2 * B_KEY_DIM + B_VAL_DIM, 2 * B_KEY_DIM + 2 * B_VAL_DIM
    q, k, v, g, ga = proj[..., :o0], proj[..., o0:o1], proj[..., o1:o2], proj[..., o2:o3], proj[..., o3:]
    gk = jax.nn.log_sigmoid((ga @ w_gate + b_gate).astype(jnp.float32)) / B_GATE_NORM
    shp_k = (B, nC, CHUNK, B_HEADS, B_HK)
    q = q.astype(jnp.float32).reshape(shp_k) * (B_HK ** -0.5)
    k = k.astype(jnp.float32).reshape(shp_k)
    v = v.astype(jnp.float32).reshape(B, nC, CHUNK, B_HEADS, B_HV)
    bcum = jnp.cumsum(gk.reshape(shp_k), axis=2)
    blast = bcum[:, :, -1]
    q_dec = q * jnp.exp(bcum)
    attn = jnp.einsum('bnihd,bnjhd->bnhij', q_dec, k * jnp.exp(-bcum))
    tril = jnp.asarray(np.tril(np.ones((CHUNK, CHUNK), dtype=bool)))
    attn = jnp.where(tril, attn, 0.0)
    o_intra = jnp.einsum('bnhij,bnjhv->bnihv', attn, v)
    u = jnp.einsum('bnjhd,bnjhv->bnhdv', k * jnp.exp(blast[:, :, None] - bcum), v)

    def step(state, inp):
        u_n, dec_n = inp
        return state * dec_n[..., None] + u_n, state

    s0 = jnp.zeros((B, B_HEADS, B_HK, B_HV), jnp.float32)
    _, s_prev = lax.scan(step, s0, (jnp.moveaxis(u, 1, 0), jnp.moveaxis(jnp.exp(blast), 1, 0)))
    s_prev = jnp.moveaxis(s_prev, 0, 1)
    o_inter = jnp.einsum('bnihd,bnhdv->bnihv', q_dec, s_prev)
    o = (o_intra + o_inter).reshape(B, S, B_HEADS, B_HV)
    o = o * lax.rsqrt(jnp.mean(o * o, axis=-1, keepdims=True) + EPS) * norm_w.astype(jnp.float32)
    o = o * jax.nn.silu(g.astype(jnp.float32).reshape(B, S, B_HEADS, B_HV))
    return o.reshape(B, S, B_VAL_DIM).astype(h.dtype) @ w_o

def conv_ffn(h, w_up, conv_w, conv_b, w_down):
    S = h.shape[1]
    u = h @ w_up
    gate, up = u[..., :D_FF], u[..., D_FF:]
    gp = jnp.pad(gate, ((0, 0), (CONV_W - 1, 0), (0, 0)))
    conv = conv_b + conv_w[0] * gp[:, 0:S]
    for i in range(1, CONV_W):
        conv = conv + conv_w[i] * gp[:, i:i + S]
    return (jax.nn.silu(conv) * up) @ w_down

def setup_inputs(seed: int = 0) -> dict:
    key = jax.random.key(seed)
    ks = jax.random.split(key, 20)
    f32 = jnp.float32
    nrm = lambda k, shape, scale: jax.random.normal(k, shape, f32) * scale
    return {
        "x": nrm(ks[0], (BATCH, SEQ, D_MODEL), 1.0),
        "mix_norm": 1.0 + nrm(ks[1], (DEPTH, D_MODEL), 0.05),
        "ffn_norm": 1.0 + nrm(ks[2], (DEPTH, D_MODEL), 0.05),
        "final_norm": 1.0 + nrm(ks[3], (D_MODEL,), 0.05),
        "rel_bias": nrm(ks[4], (REL_BUCKETS, A_HEADS), 0.5),
        "a_w_qkv": nrm(ks[5], (N_A_LAYERS, D_MODEL, A_QKV_DIM), D_MODEL ** -0.5),
        "a_sinks": nrm(ks[6], (N_A_LAYERS, A_HEADS), 0.5),
        "a_w_o": nrm(ks[7], (N_A_LAYERS, A_HEADS * A_HEAD_DIM, D_MODEL), (A_HEADS * A_HEAD_DIM) ** -0.5),
        "b_w_in": nrm(ks[8], (N_B_LAYERS, D_MODEL, B_IN_DIM), D_MODEL ** -0.5),
        "b_w_gate": nrm(ks[9], (N_B_LAYERS, B_GATE_RANK, B_KEY_DIM), B_GATE_RANK ** -0.5),
        "b_gate_bias": nrm(ks[10], (N_B_LAYERS, B_KEY_DIM), 0.1),
        "b_norm": 1.0 + nrm(ks[11], (N_B_LAYERS, B_HV), 0.05),
        "b_w_o": nrm(ks[12], (N_B_LAYERS, B_VAL_DIM, D_MODEL), B_VAL_DIM ** -0.5),
        "f_w_up": nrm(ks[13], (DEPTH, D_MODEL, 2 * D_FF), D_MODEL ** -0.5),
        "f_conv_w": nrm(ks[14], (DEPTH, CONV_W, D_FF), CONV_W ** -0.5),
        "f_conv_b": nrm(ks[15], (DEPTH, D_FF), 0.02),
        "f_w_down": nrm(ks[16], (DEPTH, D_FF, D_MODEL), D_FF ** -0.5),
    }

def reference(x, mix_norm, ffn_norm, final_norm, rel_bias, a_w_qkv, a_sinks, a_w_o,
              b_w_in, b_w_gate, b_gate_bias, b_norm, b_w_o,
              f_w_up, f_conv_w, f_conv_b, f_w_down):
    for i in range(DEPTH):
        h = rmsnorm(x, mix_norm[i])
        j = i // N_MIXERS
        if i % N_MIXERS == 0:
            y = swa_sink_attention(h, a_w_qkv[j], a_sinks[j], rel_bias, a_w_o[j])
        else:
            y = gla(h, b_w_in[j], b_w_gate[j], b_gate_bias[j], b_norm[j], b_w_o[j])
        x = x + y
        x = x + conv_ffn(rmsnorm(x, ffn_norm[i]), f_w_up[i], f_conv_w[i], f_conv_b[i], f_w_down[i])
    return rmsnorm(x, final_norm)


_drawn_inputs = setup_inputs


def setup_inputs(seed=0):
    import zlib

    import numpy as np

    out = dict(_drawn_inputs(seed))
    spreads = {}
    factors = {'a_sinks': 8.0, 'f_conv_b': 3.413}
    for name, (base, spread) in spreads.items():
        noise = np.random.default_rng([zlib.crc32(name.encode()), seed]).standard_normal(out[name].shape)
        drawn = base * np.exp(spread * noise) if base else spread * noise
        out[name] = __import__('jax').numpy.asarray(drawn.astype(out[name].dtype))
    for name, factor in factors.items():
        out[name] = (out[name] * factor).astype(out[name].dtype)
    return out
```

```python
from contextlib import ExitStack

import numpy as np

import concourse.bass as bass
from concourse import mybir

F32, F32R, U32 = mybir.dt.float32, mybir.dt.float32r, mybir.dt.uint32
ALU, ACT, AX = mybir.AluOpType, mybir.ActivationFunctionType, mybir.AxisListType

P = 128
T = 512
D = 1024
KT_D = D // P
FF = 2816
FT = FF // P
HALF = FT // 2
CHUNK = 64
NCH = T // CHUNK
EPS = 1e-6
NEG = -1e30
A_HEADS, KV, HD = 16, 4, 64
A_SCALE = HD ** -0.5
BH, HK, HV = 4, 128, 256
B_SCALE = HK ** -0.5
RANK = 16
GATE_NORM = 16.0
REL = 2 * P - 64
SLOTS = 4

A_K, A_V, A_Q, A_O = 0, 2, 4, 12
UP0, DOWN0 = 20, 64
B_V, B_Q, B_K, B_G, B_O = 80, 88, 92, 96, 104
UP1, DOWN1 = 112, 156
UP, DOWN = (UP0, UP1), (DOWN0, DOWN1)

B4, B5, B6, B7 = 4, 5, 6, 7


def trunk(nc, xT, gains, w_qkv, sinks, rel_bias, w_o, w_bin, w_ga, w_gate, b_norm, w_bo, w_up, conv_w, conv_b,
          w_down, onehot, ident, causal, out, bias_rows):
    with ExitStack() as ctx:
        place_at = [-(-nc.sbuf_base // 64) * 64]

        def place(name, shape, dt=F32, at=None):
            size = 4 * int(np.prod(shape[1:]))
            offset = place_at[0] if at is None else at
            if at is None:
                place_at[0] += -(-size // 64) * 64
            return nc.alloc_sbuf_tensor_at(name, shape, dt, offset=offset)

        def sem(name):
            return ctx.enter_context(nc.semaphore(name))

        X = place("X", [P, KT_D, T])
        XH = place("XH", [P, KT_D, T], F32R)
        XL = place("XL", [P, KT_D, T], F32R)
        WH = place("WH", [P, SLOTS, HALF * P], F32R)
        slots_at = place_at[0]
        WRAW = place("WRAW", [P, SLOTS, HALF * P])
        WL = place("WL", [P, SLOTS, HALF * P], F32R, at=slots_at)
        R = place("R", [P, T])
        STD = place("STD", [P, T])
        SS = place("SS", [P, T])
        SQ = place("SQ", [P, 2, T])
        ONES = place("ONES", [P, P])
        IDENT = place("IDENT", [P, P])
        CAUSAL = place("CAUSAL", [P, P])
        GAIN = place("GAIN", [P, 5, KT_D])
        CONVW = place("CONVW", [P, 2, FT, 3])
        CONVB = place("CONVB", [P, 2, FT])
        BNORM = place("BNORM", [P, 2])
        SINK = place("SINK", [P, KV, 2])
        EPSC = place("EPSC", [P, 1])
        WG = place("WG", [P, BH * HK])
        GARAW = place("GARAW", [P, KT_D, RANK])
        MX = place("MX", [P, 2, 4])
        NM = place("NM", [P, 2, 4])
        SM = place("SM", [P, 2, 4])
        ES = place("ES", [P, 2, 4])
        SUM = place("SUM", [P, 2, 4])
        RD = place("RD", [P, 2, 4])
        CL = place("CL", [P, BH, NCH])
        DEC = place("DEC", [P, BH, NCH])
        region = place_at[0]

        AH = place("AH", [P, FT, T], F32R)
        AL = place("AL", [P, FT, T], F32R)
        GS = place("GS", [P, 2, T + 2])
        CV = place("CV", [P, 2, T])
        AC = place("AC", [P, 2, T])
        end_ffn = place_at[0]

        place_at[0] = region
        KT = place("KT", [P, KV, T])
        VT = place("VT", [P, 2, T])
        V = place("V", [P, 2, 4, KV * HD])
        QT = place("QT", [P, 2, 2, NCH, 2 * CHUNK])
        SB = place("SB", [P, 2, 4, P])
        PB = place("PB", [P, 2, 4, P])
        PT = place("PT", [P, 2, 4, P])
        BIAS = place("BIAS", [P, KV, 2, 4, P])
        TB = place("TB", [P, REL])
        HOT = place("HOT", [P, REL])
        RB = place("RB", [P, A_HEADS])
        OH = place("OH", [P, KT_D, T], F32R)
        OL = place("OL", [P, KT_D, T], F32R)
        end_a = place_at[0]

        place_at[0] = region
        EP = place("EP", [P, BH, T])
        EN = place("EN", [P, BH, T])
        EU = place("EU", [P, BH, T])
        VV = place("VV", [P, 4, BH * HV])
        S = place("S", [P, NCH, HV])
        SG = place("SG", [P, KT_D, T])
        y_at = place_at[0]
        YH = place("YH", [P, KT_D, T], F32R)
        YL = place("YL", [P, KT_D, T], F32R)
        GT = place("GT", [P, 4, 2, T], at=y_at)
        GK = place("GK", [P, 4, T], at=y_at + 16 * T * 2)
        VTT = place("VTT", [P, 2, T])
        KS = place("KS", [P, 2, T])
        GAT = place("GAT", [P, T])
        ga_at = max(end_a, end_ffn, place_at[0])
        GAH = place("GAH", [P, KT_D, P], F32R, at=ga_at)
        GAL = place("GAL", [P, KT_D, P], F32R, at=ga_at + 4 * KT_D * P)
        AM = place("AM", [P, 2, 4, P], at=ga_at)
        KUT = place("KUT", [P, 2, 4, P], at=ga_at + 4 * 2 * 4 * P)
        assert ga_at + 8 * KT_D * P <= nc.sbuf_usable_end

        PS = ctx.enter_context(nc.psum_tensor("PS", [P, 8, T], F32))

        raw_landed = [sem(f"raw_landed{s}") for s in range(SLOTS)]
        hi_ready, lo_ready = sem("hi_ready"), sem("lo_ready")
        unit_done = sem("unit_done")
        unit_evac = sem("unit_evac")
        x_landed = [sem(f"x_landed{i}") for i in range(4)]
        consts = sem("consts")
        small_set = sem("small_set")
        xh_ready, xl_ready = sem("xh_ready"), sem("xl_ready")
        sq_ready, ss_ready = sem("sq_ready"), sem("ss_ready")
        ms_done, std_ready, r_ready = sem("ms_done"), sem("std_ready"), sem("r_ready")
        tb_done, tb_ready, rows_out, bias_in = sem("tb_done"), sem("tb_ready"), sem("rows_out"), sem("bias_in")
        bias_ready, k_dup = sem("bias_ready"), sem("k_dup")
        vt_done, v_copied, v_ready = sem("vt_done"), sem("v_copied"), sem("v_ready")
        scores_done, s_ready, max_ready = sem("scores_done"), sem("s_ready"), sem("max_ready")
        exp_done, p_ready, pt_done, pt_ready = sem("exp_done"), sem("p_ready"), sem("pt_done"), sem("pt_ready")
        pv_done, oh_ready, ol_ready = sem("pv_done"), sem("oh_ready"), sem("ol_ready")
        dve_step = sem("dve_step")
        pool_step = sem("pool_step")
        c0_ready, c1_ready, conv_ready = sem("c0_ready"), sem("c1_ready"), sem("conv_ready")
        silu_ready, slr_ready, ah_ready, al_ready = sem("silu_ready"), sem("slr_ready"), sem("ah_ready"), sem("al_ready")
        gah_ready, gal_ready, ga_done, ga_ready = sem("gah_ready"), sem("gal_ready"), sem("ga_done"), sem("ga_ready")
        z_done, ln_ready, gk_ready, cum_done = sem("z_done"), sem("ln_ready"), sem("gk_ready"), sem("cum_done")
        act_step = sem("act_step")
        c_copied, d_ready, e_ready, epr_ready = sem("c_copied"), sem("d_ready"), sem("e_ready"), sem("epr_ready")
        vtt_done, vv_ready = sem("vtt_done"), sem("vv_ready")
        ks_ready, kd_ready, ku_ready, am_zero = sem("ks_ready"), sem("kd_ready"), sem("ku_ready"), sem("am_zero")
        a_done, am_ready, kut_done, kut_ready = sem("a_done"), sem("am_ready"), sem("kut_done"), sem("kut_ready")
        u_done, st_ready, o_done, o_ready = sem("u_done"), sem("st_ready"), sem("o_done"), sem("o_ready")
        hms_done, hstd_ready = sem("hms_done"), sem("hstd_ready")
        sg_ready, y_ready, yh_ready, yl_ready = sem("sg_ready"), sem("y_ready"), sem("yh_ready"), sem("yl_ready")
        fin_ready, out_written = sem("fin_ready"), sem("out_written")

        block = ctx.enter_context(nc.Block())

        def ksize(u):
            return HALF if DOWN0 <= u < B_V or u >= DOWN1 else KT_D

        @block.sync
        def _(sp):
            def load(u, src, k, first=False):
                s = u % SLOTS if isinstance(u, int) else first
                if not isinstance(u, int) or u >= SLOTS:
                    sp.wait_ge(unit_done, u - SLOTS + 1)
                sp.dma_start(WRAW[:, s, 0:k * P], src).then_inc(raw_landed[s], 16)

            def load_all(u0, src, n, k):
                with sp.Fori(0, n - SLOTS + 1, SLOTS) as i:
                    for s in range(SLOTS):
                        sp.wait_ge(unit_done, i + (u0 + s - SLOTS + 1))
                        sp.dma_start(WRAW[:, s, 0:k * P], src[bass.ds(i + s, 1)].rearrange("a p c -> p (a c)"))\
                          .then_inc(raw_landed[s], 16)

            sp.dma_start(X[:, 0:2], xT[:, 0:2]).then_inc(x_landed[0], 16)
            sp.dma_start(X[:, 2:4], xT[:, 2:4]).then_inc(x_landed[1], 16)
            load(0, w_qkv[0], KT_D)
            sp.dma_start(X[:, 4:6], xT[:, 4:6]).then_inc(x_landed[2], 16)
            sp.dma_start(X[:, 6:8], xT[:, 6:8]).then_inc(x_landed[3], 16)
            for u in range(1, A_O):
                load(u, w_qkv[u], KT_D)
            load_all(A_O, w_o, D // P, KT_D)
            load_all(UP0, w_up[0], 2 * FT, KT_D)
            load_all(DOWN0, w_down[0], 2 * KT_D, HALF)
            load_all(B_V, w_bin, 24, KT_D)
            load_all(B_O, w_bo, D // P, KT_D)
            load_all(UP1, w_up[1], 2 * FT, KT_D)
            load_all(DOWN1, w_down[1], 2 * KT_D, HALF)
            for m in range(KT_D):
                sp.wait_ge(fin_ready, m + 1)
                sp.dma_start(out[:, m], X[:, m]).then_inc(out_written, 16)
            sp.wait_ge(out_written, 16 * KT_D)

        @block.tensor
        def _(pe):
            mm = nc.tensor.matmul

            def product(s, bank, hi, lo, kbs, wkb, start=True, stop=True, part_ready=None):
                last = None
                for n, kb in enumerate(kbs):
                    if part_ready is not None:
                        pe.wait_ge(part_ready[0], part_ready[1] + kb + 1)
                    c = (wkb + n) * P
                    for w, x in ((WH, hi), (WH, lo), (WL, hi)):
                        last = mm(PS[:, bank], w[:, s, c:c + P], x[:, kb],
                                  start=start and n == 0 and w is WH and x is hi,
                                  stop=stop and n == len(kbs) - 1 and w is WL)
                return last

            def unit(u, s, hi, lo, bank=None, banks=4, **kw):
                pe.wait_ge(lo_ready, u + 1)
                if not isinstance(u, int) or u >= 4:
                    pe.wait_ge(unit_evac, u - banks + 1)
                product(s, s if bank is None else bank, hi, lo, range(KT_D), 0, **kw).then_inc(unit_done, 1)

            def mean_square(st):
                pe.wait_ge(ss_ready, KT_D * (st + 1))
                mm(PS[:, B4], ONES[:], SS[:], start=True, stop=True).then_inc(ms_done, 1)

            def up_phase(layer, st):
                u0 = UP[layer]
                for j in range(4):
                    unit(u0 + j, j, XH, XL, part_ready=(xl_ready, KT_D * st))
                    if j == 0:
                        mean_square(st)
                with pe.Fori(4, 2 * FT, 4) as i:
                    for s in range(SLOTS):
                        unit(i + (u0 + s), s, XH, XL)

            def down_unit(u, s, half):
                pe.wait_ge(lo_ready, u + 1)
                if half == 0:
                    pe.wait_ge(unit_evac, u - 3)
                return product(s, s & 2, AH, AL, range(half * HALF, half * HALF + HALF), 0,
                               start=half == 0, stop=half == 1)

            def down_phase(layer):
                u0 = DOWN[layer]
                for s in range(SLOTS):
                    if s == 0:
                        pe.wait_ge(al_ready, FT * layer + HALF)
                    if s == 1:
                        pe.wait_ge(lo_ready, u0 + 2)
                        last = None
                        for n in range(HALF):
                            kb = HALF + n
                            pe.wait_ge(al_ready, FT * layer + kb + 1)
                            for w, x in ((WH, AH), (WH, AL), (WL, AH)):
                                last = mm(PS[:, 0], w[:, 1, n * P:(n + 1) * P], x[:, kb], start=False,
                                          stop=n == HALF - 1 and w is WL)
                        last.then_inc(unit_done, 1)
                    else:
                        down_unit(u0 + s, s, s % 2).then_inc(unit_done, 1)
                with pe.Fori(4, 2 * KT_D, 4) as i:
                    for s in range(SLOTS):
                        down_unit(i + (u0 + s), s, s % 2).then_inc(unit_done, 1)

            pe.wait_ge(consts, 16 * 13)
            mm(PS[0:A_HEADS, B5, 0:REL], RB[0:32, :], HOT[0:32, :], start=True, stop=True).then_inc(tb_done, 1)
            pe.wait_ge(small_set, 1)
            unit(0, 0, XH, XL, part_ready=(xl_ready, 0))
            mean_square(0)
            for u in range(1, 5):
                unit(u, u % 4, XH, XL)
            pe.wait_ge(unit_evac, A_V + 2)
            pe.wait_ge(tb_ready, 1)
            for t in range(4):
                for f in range(2):
                    last = nc.tensor.transpose(PS[:, B5 + t // 2, (t % 2) * 256 + f * P:(t % 2) * 256 + (f + 1) * P],
                                               VT[:, f, t * P:(t + 1) * P], IDENT[:])
            last.then_inc(vt_done, 1)
            unit(5, 1, XH, XL)

            def scores(k):
                g, p = divmod(k, 4)
                if k == 0:
                    pe.wait_ge(std_ready, 1)
                    pe.wait_ge(v_copied, 2)
                    pe.wait_ge(k_dup, 64)
                if k >= 2:
                    pe.wait_ge(s_ready, k - 1)
                if p == 0:
                    pe.wait_ge(unit_evac, A_Q + 2 * g + 2)
                for j in range(2):
                    for half in range(2):
                        q = QT[:, g % 2, half, 2 * p + j]
                        c = (2 * j + half) * P
                        o = PS[:, B4 + k % 2]
                        if j == 1:
                            last = mm(o[:, c:c + P], q, KT[:, g, 2 * p * 64:2 * p * 64 + P], start=True, stop=True)
                        else:
                            before = max(2 * p - 1, 0) * 64
                            mm(o[:, c:c + 64], q, KT[:, g, 2 * p * 64:2 * p * 64 + 64], start=True, stop=True)
                            last = mm(o[:, c + 64:c + P], q, KT[:, g, before:before + 64], start=True, stop=True)
                last.then_inc(scores_done, 1)

            def turn_probs(k):
                pe.wait_ge(p_ready, k + 1)
                if k >= 1:
                    pe.wait_ge(pt_ready, k)
                for i in range(4):
                    last = nc.tensor.transpose(PS[:, B6, i * P:(i + 1) * P], PB[:, k % 2, i], IDENT[:])
                last.then_inc(pt_done, 1)

            def values(k):
                g, p = divmod(k, 4)
                pe.wait_ge(pt_ready, k + 1)
                if k == 0:
                    pe.wait_ge(v_ready, 1)
                if k >= 1:
                    pe.wait_ge(ol_ready, k)
                for j in range(2):
                    for half in range(2):
                        last = mm(PS[64 * half:64 * half + 64, B7, j * P:(j + 1) * P],
                                  V[:, 1 - j, p, g * HD:(g + 1) * HD], PT[:, k % 2, 2 * j + half],
                                  start=True, stop=True)
                last.then_inc(pv_done, 1)

            def out_part(u, kbs, hi, lo, start, stop):
                return product(u % 4, u % 4, hi, lo, kbs, kbs[0], start=start, stop=stop)

            for k in range(16):
                g, p = divmod(k, 4)
                scores(k)
                if k >= 1:
                    turn_probs(k - 1)
                if k >= 2:
                    values(k - 2)
                if g < 3 and p % 2 == 0:
                    u = A_Q + 2 * (g + 1) + p // 2
                    unit(u, u % 4, XH, XL)
                if g == 3:
                    u = A_O + p
                    pe.wait_ge(lo_ready, u + 1)
                    pe.wait_ge(unit_evac, u - 3)
                    pe.wait_ge(ol_ready, 8)
                    out_part(u, range(0, 4), OH, OL, True, False)
            turn_probs(15)
            values(14)
            pe.wait_ge(ol_ready, 12)
            for u in range(A_O, A_O + 2):
                out_part(u, range(4, 6), OH, OL, False, False)
            values(15)
            for u in range(A_O + 2, A_O + 4):
                out_part(u, range(4, 6), OH, OL, False, False)
            pe.wait_ge(ol_ready, 16)
            for u in range(A_O, A_O + 4):
                out_part(u, range(6, 8), OH, OL, False, True).then_inc(unit_done, 1)
            for u in range(A_O + 4, A_O + 8):
                unit(u, u % 4, OH, OL)

            up_phase(0, 1)
            down_phase(0)

            pe.wait_ge(gal_ready, 1)
            for kb in range(KT_D):
                pe.wait_ge(xl_ready, 2 * KT_D + kb + 1)
                for w, x in ((GAH, XH), (GAH, XL), (GAL, XH)):
                    last = mm(PS[:, B5], w[:, kb], x[:, kb], start=kb == 0 and w is GAH and x is XH,
                              stop=kb == KT_D - 1 and w is GAL)
            last.then_inc(ga_done, 1)
            mean_square(2)

            def gate_logits(t):
                if t == 0:
                    pe.wait_ge(ga_ready, 1)
                if t >= 2:
                    pe.wait_ge(gk_ready, t - 1)
                mm(PS[:, B6 + t % 2], GAT[0:RANK + 1, t * P:(t + 1) * P], WG[0:RANK + 1, :],
                   start=True, stop=True).then_inc(z_done, 1)

            def cumulate(h):
                pe.wait_ge(gk_ready, 4)
                if h >= 2:
                    pe.wait_ge(e_ready, h - 1)
                for t in range(4):
                    last = mm(PS[:, B6 + h % 2, t * P:(t + 1) * P], GK[:, t, h * HK:(h + 1) * HK], CAUSAL[:],
                              start=True, stop=True)
                last.then_inc(cum_done, 1)

            def turn_values(j):
                pe.wait_ge(unit_evac, B_V + j + 1)
                if j == 0:
                    pe.wait_ge(std_ready, 3)
                if j == 1:
                    pe.wait_ge(ga_ready, 1)
                if j >= 2:
                    pe.wait_ge(vv_ready, j - 1)
                for t in range(4):
                    last = nc.tensor.transpose(PS[:, B4 + j % 2, t * P:(t + 1) * P],
                                               VTT[:, j % 2, t * P:(t + 1) * P], IDENT[:])
                last.then_inc(vtt_done, 1)

            for j in range(16):
                unit(B_V + j, j % 4, XH, XL)
                if 1 <= j <= 2:
                    gate_logits(2 * j - 2)
                    gate_logits(2 * j - 1)
                if j in (4, 6):
                    cumulate(j - 4)
                    cumulate(j - 3)
                if 2 <= j <= 9:
                    turn_values(j - 2)

            def head_start(h):
                pe.wait_ge(kd_ready, h + 1)
                pe.wait_ge(ku_ready, h + 1)
                if h == 0:
                    pe.wait_ge(vv_ready, 8)
                if h >= 2:
                    pe.wait_ge(hstd_ready, h - 1)
                for p in range(4):
                    c = slice(p * P, (p + 1) * P)
                    last = mm(PS[:, B4, c], EN[:, h, c], EP[:, h, c], start=True, stop=True)
                last.then_inc(a_done, 1)
                for p in range(4):
                    c = slice(p * P, (p + 1) * P)
                    last = nc.tensor.transpose(PS[:, B5, c], EU[:, h, c], IDENT[:])
                last.then_inc(kut_done, 1)

            def state_updates(h):
                pe.wait_ge(kut_ready, h + 1)
                if h == 0:
                    pe.wait_ge(e_ready, 4)
                for c in range(NCH - 1):
                    if c % 2 == 0 and (c >= 4 or h >= 1):
                        pe.wait_ge(st_ready, (NCH - 1) * h + (c - 2 if c >= 4 else c + 4 - (NCH - 1) if c == 0 else 0))
                    mm(PS[:, B6 + (c // 2) % 2, (c % 2) * HV:(c % 2 + 1) * HV], KUT[:, c % 2, c // 2],
                       VV[:, c // 2, h * HV:(h + 1) * HV], start=True, stop=True).then_inc(u_done, 1)

            def outputs(h):
                pe.wait_ge(am_ready, h + 1)
                pe.wait_ge(st_ready, (NCH - 1) * (h + 1))
                for vt in range(2):
                    v0 = h * HV + vt * P
                    if h >= 1:
                        pe.wait_ge(o_ready, 2 * (h - 1) + vt + 1)
                    for p in range(4):
                        c0 = p * P
                        mm(PS[:, 2 + vt, c0:c0 + P], VV[:, p, v0:v0 + P], AM[:, h % 2, p], start=True, stop=False,
                           skip_group_check=True)
                        for c in ((1,) if p == 0 else (2 * p, 2 * p + 1)):
                            last = mm(PS[:, 2 + vt, c * 64:c * 64 + 64], S[:, c, vt * P:(vt + 1) * P],
                                      EP[:, h, c * 64:c * 64 + 64], start=False, stop=c % 2 == 1, skip_group_check=True)
                    last.then_inc(o_done, 1)

            def head_square(h):
                pe.wait_ge(o_ready, 2 * h + 2)
                if h < 3:
                    pe.wait_ge(am_ready, h + 2)
                mm(PS[:, B4], ONES[:], SQ[:, 0], start=True, stop=False)
                mm(PS[:, B4], ONES[:], SQ[:, 1], start=False, stop=True).then_inc(hms_done, 1)

            for h in range(BH):
                head_start(h)
                u = B_G + 2 * h
                if h == 0:
                    pe.wait_ge(unit_evac, B_G)
                unit(u, u % 4, XH, XL, bank=0, banks=2)
                if h >= 1:
                    head_square(h - 1)
                state_updates(h)
                unit(u + 1, (u + 1) % 4, XH, XL, bank=1, banks=2)
                outputs(h)
            for u in range(B_O, B_O + 4):
                pe.wait_ge(lo_ready, u + 1)
                if u == B_O:
                    pe.wait_ge(unit_evac, B_O)
                if u == B_O + 1:
                    head_square(3)
                if u == B_O + 2:
                    pe.wait_ge(o_ready, 8)
                pe.wait_ge(yl_ready, 6)
                out_part(u, range(0, 6), YH, YL, True, False)
            for u in range(B_O, B_O + 4):
                pe.wait_ge(yl_ready, 8)
                out_part(u, range(6, 8), YH, YL, False, True).then_inc(unit_done, 1)
            for u in range(B_O + 4, B_O + 8):
                unit(u, u % 4, YH, YL)

            up_phase(1, 3)
            down_phase(1)
            mean_square(4)

        @block.scalar
        def _(act):
            A = nc.scalar.activation

            def hi(u, s, turn, k):
                act.wait_ge(raw_landed[s], 16 * turn + 16)
                nc.scalar.copy(WH[:, s, 0:k * P], WRAW[:, s, 0:k * P]).then_inc(hi_ready, 1)

            def hi_unit(u):
                hi(u, u % 4, u // 4, ksize(u))

            def after_wait(m):
                return slice(m, m + 1) if isinstance(m, int) else bass.ds(act.snap(m), 1)

            def x_tile(st, m, m_even=None):
                par = m % 2 if m_even is None else m_even
                if not isinstance(m, int) or KT_D * st + m >= 2:
                    act.wait_ge(ss_ready, m + (KT_D * st - 1))
                tile = after_wait(m)
                if st < 4:
                    A(XH[:, tile, :], X[:, tile, :], ACT.Copy, scale=GAIN[:, st, tile]).then_inc(xh_ready, 1)
                A(SQ[:, par:par + 1, :], X[:, tile, :], ACT.Square).then_inc(sq_ready, 1)

            def std(st):
                act.wait_ge(ms_done, st + 1)
                A(STD[:], PS[:, B4], ACT.Sqrt, bias=EPSC[:], scale=1.0 / D).then_inc(std_ready, 1)

            def ffn_step(layer, m, par, before=None, after=None):
                u, f = UP[layer] + 2 * m, FT * layer + m
                act.wait_ge(unit_evac, u + 1)
                tile = after_wait(m)
                A(CV[:, par], GS[:, par, 2:T + 2], ACT.Identity, bias=CONVB[:, layer, tile],
                  scale=CONVW[:, layer, tile, 2]).then_inc(c0_ready, 1)
                if after:
                    after()
                act.wait_ge(conv_ready, f + 1)
                A(CV[:, par], CV[:, par], ACT.Silu).then_inc(silu_ready, 1)
                act.wait_ge(unit_evac, u + 2)
                tile = after_wait(m)
                nc.scalar.copy(AH[:, tile, :], AC[:, par:par + 1, :]).then_inc(ah_ready, 1)

            def ffn(layer, st):
                u0, d0 = UP[layer], DOWN[layer]
                for j in range(2):
                    act.wait_ge(unit_evac, u0 - 1 + j)
                    x_tile(st, 6 + j)
                    hi_unit(u0 + 2 + j)
                std(st)
                with act.Fori(1, FT - 1, 2) as i:
                    for j in range(2):
                        s, landed = 2 * j, 8 * i + (4 * u0 + 24)
                        act.wait_ge(raw_landed[s], landed)
                        nc.scalar.copy(WH[:, s, 0:D], WRAW[:, s, 0:D]).then_inc(hi_ready, 1)

                        def second(s=s, landed=landed):
                            act.wait_ge(raw_landed[s + 1], landed)
                            nc.scalar.copy(WH[:, s + 1, 0:D], WRAW[:, s + 1, 0:D]).then_inc(hi_ready, 1)
                        ffn_step(layer, i + (j - 1), j, after=second)
                hi_unit(d0)
                ffn_step(layer, FT - 2, 0, after=lambda: hi_unit(d0 + 1))
                hi_unit(d0 + 2)
                ffn_step(layer, FT - 1, 1, after=lambda: hi_unit(d0 + 3))
                with act.Fori(1, KT_D - 1, 2) as i:
                    for j in range(2):
                        s, landed = 2 * j, 8 * i + (4 * d0 + 24)
                        act.wait_ge(raw_landed[s], landed)
                        nc.scalar.copy(WH[:, s], WRAW[:, s]).then_inc(hi_ready, 1)
                        act.wait_ge(unit_evac, 2 * i + (d0 + 2 * j))
                        x_tile(st + 1, i + (j - 1), j)
                        act.wait_ge(raw_landed[s + 1], landed)
                        nc.scalar.copy(WH[:, s + 1], WRAW[:, s + 1]).then_inc(hi_ready, 1)
                if d0 + 16 < DOWN1:
                    hi_unit(d0 + 16)
                act.wait_ge(unit_evac, d0 + 14)
                x_tile(st + 1, 6)
                if d0 + 16 < DOWN1:
                    hi_unit(d0 + 17)
                    hi_unit(d0 + 18)
                act.wait_ge(unit_evac, d0 + 16)
                x_tile(st + 1, 7)

            for dst, src in ((GAIN[:], gains), (RB[0:32, :], rel_bias), (HOT[0:32, :], onehot), (IDENT[:], ident),
                             (CAUSAL[:], causal), (SINK[:], sinks), (CONVW[:], conv_w), (CONVB[:], conv_b),
                             (BNORM[:], b_norm), (WG[0:RANK, :], w_gate[0:RANK]), (WG[RANK:RANK + 1, :], w_gate[RANK:RANK + 1]),
                             (GARAW[:, 0:4], w_ga[:, 0:4]), (GARAW[:, 4:8], w_ga[:, 4:8])):
                act.dma_start(dst, src).then_inc(consts, 16)
            act.wait_ge(consts, 16 * 13)
            act.wait_ge(tb_done, 1)
            nc.scalar.copy(TB[0:A_HEADS, :], PS[0:A_HEADS, B5, 0:REL]).then_inc(tb_ready, 1)
            act.wait_ge(tb_ready, 1)
            act.dma_start(bias_rows.rearrange("h (q r) -> h q r", q=64),
                          TB[0:A_HEADS, :].rearrange("h (o r) -> h o r", o=1).to_broadcast([A_HEADS, 64, REL]))\
               .then_inc(rows_out, 16)
            act.wait_ge(small_set, 1)
            for m in range(KT_D):
                if m % 2 == 0:
                    act.wait_ge(x_landed[m // 2], 16)
                x_tile(0, m)
                if m == 3:
                    hi_unit(0)
            hi_unit(1)
            hi_unit(2)
            act.wait_ge(rows_out, 16)
            for hh in range(2):
                for half in range(2):
                    def stretch(first, n, hh=hh, half=half):
                        return bass.AP(tensor=bias_rows.tensor,
                                       offset=bias_rows.offset + (2 * hh + half) * 64 * REL + 63 + first,
                                       ap=[[REL - 1, 64], [4 * 64 * REL, KV], [1, n]])
                    rows = slice(64 * hh, 64 * hh + 64)
                    act.dma_start(BIAS[rows, :, 1, half, 0:64], stretch(64, 64)).then_inc(bias_in, 16)
                    act.dma_start(BIAS[rows, :, 1, half, 64:P], stretch(0, 64)).then_inc(bias_in, 16)
                    act.dma_start(BIAS[rows, :, 1, 2 + half], stretch(0, P)).then_inc(bias_in, 16)
            std(0)
            hi_unit(3)
            for g in range(KV):
                if g % 2 == 0:
                    act.wait_ge(unit_evac, g // 2 + 1)
                here, there = slice(64 * (g % 2), 64 * (g % 2) + 64), slice(64 - 64 * (g % 2), 128 - 64 * (g % 2))
                act.dma_start(KT[there, g], KT[here, g]).then_inc(k_dup, 16)
                if g % 2 == 1:
                    hi_unit(4 + g // 2)
            hi_unit(6)
            act.wait_ge(vt_done, 1)
            for b in range(2):
                nc.scalar.copy(V[:, 0, 2 * b:2 * b + 2], PS[:, B5 + b].rearrange("p (t f) -> p t f", t=2)).then_inc(v_copied, 1)
            hi_unit(7)

            def softmax_exp(k):
                act.wait_ge(max_ready, k + 1)
                for i in range(4):
                    A(PB[:, k % 2, i], SB[:, k % 2, i], ACT.Exp, bias=NM[:, k % 2, i:i + 1],
                      accum_out=SUM[:, k % 2, i:i + 1])
                A(ES[:, k % 2], SM[:, k % 2], ACT.Exp).then_inc(exp_done, 1)

            def probs_copy(k):
                act.wait_ge(pt_done, k + 1)
                if k >= 2:
                    act.wait_ge(pv_done, k - 1)
                nc.scalar.copy(PT[:, k % 2], PS[:, B6].rearrange("p (i c) -> p i c", i=4)).then_inc(pt_ready, 1)

            def o_view(k):
                return PS[:, B7, 0:2 * P].rearrange("p (j a q) -> p a j q", j=2, a=2)

            def o_tiles(t, k):
                g, p = divmod(k, 4)
                return t[:, 2 * g:2 * g + 2, p * P:(p + 1) * P].rearrange("p a (j q) -> p a j q", j=2)

            def o_hi(k):
                act.wait_ge(pv_done, k + 1)
                nc.scalar.copy(o_tiles(OH, k), o_view(k)).then_inc(oh_ready, 1)

            for k in range(16):
                g, p = divmod(k, 4)
                if k >= 3:
                    o_hi(k - 3)
                softmax_exp(k)
                if k >= 1:
                    probs_copy(k - 1)
                if p % 2 == 0:
                    hi_unit(8 + 2 * g + p // 2)
            probs_copy(15)
            for k in range(13, 16):
                o_hi(k)
            for m in range(6):
                act.wait_ge(unit_evac, A_O + m + 1)
                x_tile(1, m)
                if m >= 1:
                    hi_unit(A_O + 3 + m)
            hi_unit(A_O + 9)
            ffn(0, 1)

            std(2)

            def decays(h):
                act.wait_ge(cum_done, h + 1)
                nc.scalar.copy(EU[:, h], PS[:, B6 + h % 2]).then_inc(c_copied, 1)
                A(EP[:, h], PS[:, B6 + h % 2], ACT.Exp, scale=1.0 / GATE_NORM)
                A(EN[:, h], PS[:, B6 + h % 2], ACT.Exp, scale=-1.0 / GATE_NORM).then_inc(e_ready, 1)
                act.wait_ge(d_ready, h + 1)
                A(EU[:, h], EU[:, h], ACT.Exp, scale=1.0 / GATE_NORM)
                A(DEC[:, h], CL[:, h], ACT.Exp, scale=1.0 / GATE_NORM).then_inc(ln_ready, 1)

            def values_copy(j):
                act.wait_ge(vtt_done, j + 1)
                nc.scalar.copy(VV[:, :, j * P:(j + 1) * P], PS[:, B4 + j % 2].rearrange("p (t f) -> p t f", t=4))\
                   .then_inc(vv_ready, 1)

            def gates(t):
                act.wait_ge(z_done, t + 1)
                A(GT[:, t, 0], PS[:, B6 + t % 2], ACT.Abs).then_inc(act_step, 1)
                act.wait_ge(act_step, 3 * t + 1)
                A(GT[:, t, 0], GT[:, t, 0], ACT.Exp, scale=-1.0).then_inc(act_step, 1)
                act.wait_ge(act_step, 3 * t + 2)
                A(GT[:, t, 1], GT[:, t, 0], ACT.Ln, bias=1.0).then_inc(act_step, 1)

            for j in range(16):
                hi_unit(B_V + j + 3)
                if 1 <= j <= 2:
                    gates(2 * j - 2)
                    gates(2 * j - 1)
                if j in (4, 6):
                    decays(j - 4)
                    decays(j - 3)
                if 2 <= j <= 9:
                    values_copy(j - 2)

            def head_keys(h):
                act.wait_ge(kut_done, h + 1)
                if h == 0:
                    act.wait_ge(am_zero, 1)
                for half in range(2):
                    rows = slice(64 * half, 64 * half + 64)
                    last = nc.scalar.copy(KUT[rows, half], PS[rows, B5].rearrange("p (i c) -> p i c", i=4))
                last.then_inc(kut_ready, 1)

            def head_outputs(h):
                for vt, o in ((0, EN), (1, EU)):
                    act.wait_ge(o_done, 2 * h + vt + 1)
                    nc.scalar.copy(o[:, h], PS[:, 2 + vt]).then_inc(act_step, 1)
                    if h >= 1 and vt == 0:
                        act.wait_ge(hms_done, h)
                    A(SQ[:, vt], PS[:, 2 + vt], ACT.Square).then_inc(o_ready, 1)

            def head_std(h):
                act.wait_ge(hms_done, h + 1)
                if h >= 1:
                    act.wait_ge(y_ready, 2 * h)
                A(STD[:], PS[:, B4], ACT.Sqrt, bias=EPSC[:], scale=1.0 / HV).then_inc(hstd_ready, 1)

            def silu(j):
                act.wait_ge(unit_evac, B_G + j + 1)
                A(SG[:, j], SG[:, j], ACT.Silu).then_inc(sg_ready, 1)

            def head_hi(h):
                for vt in range(2):
                    act.wait_ge(y_ready, 2 * h + vt + 1)
                    nc.scalar.copy(YH[:, 2 * h + vt], (EN if vt == 0 else EU)[:, h]).then_inc(yh_ready, 1)

            for h in range(BH):
                head_keys(h)
                u = B_G + 2 * h
                hi_unit(u + 3)
                if h >= 1:
                    head_std(h - 1)
                silu(2 * h)
                if h >= 1:
                    head_hi(h - 1)
                if h < 3:
                    hi_unit(u + 4)
                silu(2 * h + 1)
                head_outputs(h)
            hi_unit(B_O + 2)
            hi_unit(B_O + 3)
            head_std(3)
            head_hi(3)
            for m in range(6):
                act.wait_ge(unit_evac, B_O + m + 1)
                x_tile(3, m)
                if m >= 1:
                    hi_unit(B_O + 3 + m)
            hi_unit(B_O + 9)
            ffn(1, 3)
            std(4)

        @block.vector
        def _(dve):
            tt, stt, ts = nc.vector.tensor_tensor, nc.vector.scalar_tensor_tensor, nc.vector.tensor_scalar
            steps = [0]

            def link(instruction):
                steps[0] += 1
                instruction.then_inc(dve_step, 1)
                dve.wait_ge(dve_step, steps[0])

            def lo(u, s, k):
                dve.wait_ge(hi_ready, u + 1)
                tt(WL[:, s, 0:k * P], WRAW[:, s, 0:k * P], WH[:, s, 0:k * P].bitcast(F32), ALU.subtract).then_inc(lo_ready, 1)

            def lo_unit(u):
                lo(u, u % 4, ksize(u))

            def tile_of(m):
                return slice(m, m + 1) if isinstance(m, int) else bass.ds(m, 1)

            def x_lo(st, m):
                tile = tile_of(m)
                dve.wait_ge(xh_ready, m + (KT_D * st + 1))
                stt(XL[:, tile, :], X[:, tile, :], GAIN[:, st, tile], XH[:, tile, :].bitcast(F32),
                    ALU.mult, ALU.subtract).then_inc(xl_ready, 1)

            def x_add(u_last, m, bank, n=1):
                tile = tile_of(m)
                dve.wait_ge(unit_done, u_last + 1)
                tt(X[:, tile, :], PS[:, bank:bank + 1], X[:, tile, :], ALU.add).then_inc(unit_evac, n)

            def inverse_rms(st):
                dve.wait_ge(std_ready, st + 1)
                nc.vector.reciprocal(R[:], STD[:]).then_inc(r_ready, 1)
                dve.wait_ge(r_ready, st + 1)

            def ffn_step(layer, m, par, mid=None, after=None):
                u, f = UP[layer] + 2 * m, FT * layer + m
                tile = tile_of(m)
                gate, up = (0, 1) if par == 0 else (2, 3)
                dve.wait_ge(unit_done, u + 1)
                tt(GS[:, par, 2:T + 2], PS[:, gate], R[:], ALU.mult).then_inc(unit_evac, 1)
                if mid:
                    mid()
                dve.wait_ge(c0_ready, f + 1)
                stt(CV[:, par], GS[:, par, 1:T + 1], CONVW[:, layer, tile, 1], CV[:, par], ALU.mult, ALU.add)\
                    .then_inc(c1_ready, 1)
                dve.wait_ge(c1_ready, f + 1)
                stt(CV[:, par], GS[:, par, 0:T], CONVW[:, layer, tile, 0], CV[:, par], ALU.mult, ALU.add)\
                    .then_inc(conv_ready, 1)
                if after:
                    after()
                dve.wait_ge(unit_done, u + 2)
                dve.wait_ge(slr_ready, f + 1)
                tt(AC[:, par], PS[:, up], CV[:, par], ALU.mult).then_inc(unit_evac, 1)
                dve.wait_ge(ah_ready, f + 1)
                tt(AL[:, tile, :], AC[:, par:par + 1, :], AH[:, tile, :].bitcast(F32), ALU.subtract).then_inc(al_ready, 1)

            def ffn(layer, st):
                u0, d0 = UP[layer], DOWN[layer]
                for j in range(2):
                    x_add(u0 - 2 + j, 6 + j, 2 + j)
                    x_lo(st, 6 + j)
                    lo_unit(u0 + 2 + j)
                nc.vector.memset(GS[:, :, 0:2], 0.0)
                inverse_rms(st)
                with dve.Fori(1, FT - 1, 2) as i:
                    for j in range(2):
                        s = 2 * j
                        ffn_step(layer, i + (j - 1), j,
                                 mid=lambda: lo(2 * i + (u0 + 2 * j + 2), s, KT_D),
                                 after=lambda: lo(2 * i + (u0 + 2 * j + 3), s + 1, KT_D))
                ffn_step(layer, FT - 2, 0, mid=lambda: lo_unit(d0), after=lambda: lo_unit(d0 + 1))
                ffn_step(layer, FT - 1, 1, mid=lambda: lo_unit(d0 + 2), after=lambda: lo_unit(d0 + 3))
                with dve.Fori(1, KT_D - 1, 2) as i:
                    for j in range(2):
                        s = 2 * j
                        lo(2 * i + (d0 + 2 * j + 2), s, HALF)
                        x_add(2 * i + (d0 + 2 * j - 1), i + (j - 1), 2 * j, 2)
                        if st + 1 < 4:
                            x_lo(st + 1, i + (j - 1))
                        lo(2 * i + (d0 + 2 * j + 3), s + 1, HALF)
                for m in (6, 7):
                    if m == 6 and st + 1 < 4:
                        lo_unit(d0 + 16)
                    x_add(d0 + 2 * m + 1, m, 2 * (m % 2), 2)
                    if st + 1 < 4:
                        x_lo(st + 1, m)
                        lo_unit(d0 + 17 + (m - 6))

            for m in range(KT_D):
                if m % 2 == 0:
                    dve.wait_ge(x_landed[m // 2], 16)
                x_lo(0, m)
                if m == 4:
                    lo_unit(0)
            lo_unit(1)
            lo_unit(2)
            inverse_rms(0)

            for t in range(2):
                dve.wait_ge(unit_done, A_K + t + 1)
                for half in range(2):
                    rows = slice(64 * half, 64 * half + 64)
                    last = tt(KT[rows, 2 * t + half], PS[rows, t], R[rows], ALU.mult)
                last.then_inc(unit_evac, 1)
                lo_unit(3 + t)
            for t in range(2):
                dve.wait_ge(unit_done, A_V + t + 1)
                tt(VT[:, t], PS[:, 2 + t], R[:], ALU.mult).then_inc(unit_evac, 1)
                lo_unit(5 + t)

            def queries(u):
                dve.wait_ge(unit_done, u + 1)
                by_chunk = lambda t: t.rearrange("p (c q) -> p c q", q=CHUNK)
                a = CHUNK * (u % 2)
                for half in range(2):
                    rows = slice(64 * half, 64 * half + 64)
                    last = tt(QT[rows, (u - A_Q) // 2 % 2, half, :, a:a + CHUNK], by_chunk(PS[rows, u % 4]),
                              by_chunk(R[rows]), ALU.mult)
                last.then_inc(unit_evac, 1)

            dve.wait_ge(small_set, 1)
            queries(A_Q)
            lo_unit(7)
            queries(A_Q + 1)

            def softmax_max(k):
                g, p = divmod(k, 4)
                if k == 0:
                    dve.wait_ge(bias_ready, 1)
                dve.wait_ge(scores_done, k + 1)
                b = k % 2
                stt(SB[:, b].rearrange("p i c -> p (i c)"), PS[:, B4 + b], A_SCALE,
                    BIAS[:, g, min(p, 1)].rearrange("p i c -> p (i c)"), ALU.mult, ALU.add).then_inc(s_ready, 1)
                dve.wait_ge(s_ready, k + 1)
                link(nc.vector.tensor_reduce(MX[:, b], SB[:, b], AX.X, ALU.max))
                sink = SINK[:, g:g + 1, :].to_broadcast([P, 2, 2])
                two = lambda t: t[:, b].rearrange("p (j h) -> p j h", j=2)
                link(tt(two(MX), two(MX), sink, ALU.max))
                tt(two(SM), sink, two(MX), ALU.subtract)
                ts(NM[:, b], MX[:, b], -1.0, None, ALU.mult).then_inc(max_ready, 1)

            def softmax_divide(k):
                b = k % 2
                dve.wait_ge(exp_done, k + 1)
                link(tt(RD[:, b], SUM[:, b], ES[:, b], ALU.add))
                link(nc.vector.reciprocal(RD[:, b], RD[:, b]))
                tt(PB[:, b], PB[:, b], RD[:, b].unsqueeze(2).to_broadcast([P, 4, P]), ALU.mult).then_inc(p_ready, 1)

            def o_lo(k):
                g, p = divmod(k, 4)
                dve.wait_ge(oh_ready, k + 1)
                view = lambda t: t[:, 2 * g:2 * g + 2, p * P:(p + 1) * P].rearrange("p a (j q) -> p a j q", j=2)
                tt(view(OL), PS[:, B7, 0:2 * P].rearrange("p (j a q) -> p a j q", j=2, a=2), view(OH).bitcast(F32),
                   ALU.subtract).then_inc(ol_ready, 1)

            for k in range(16):
                g, p = divmod(k, 4)
                if k >= 3:
                    o_lo(k - 3)
                softmax_max(k)
                if k >= 1:
                    softmax_divide(k - 1)
                if p % 2 == 0:
                    lo_unit(8 + 2 * g + p // 2)
                elif g < 3:
                    queries(A_Q + 2 * (g + 1) + p // 2)
            softmax_divide(15)
            for k in range(13, 16):
                o_lo(k)
            for m in range(6):
                x_add(A_O + m, m, m % 4)
                x_lo(1, m)
                if m >= 1:
                    lo_unit(A_O + 3 + m)
            lo_unit(A_O + 9)
            ffn(0, 1)

            inverse_rms(2)
            dve.wait_ge(ga_done, 1)
            dve.wait_ge(small_set, 3)
            tt(GAT[0:RANK, :], PS[0:RANK, B5], R[0:RANK], ALU.mult).then_inc(ga_ready, 1)

            def log_gates(t):
                dve.wait_ge(act_step, 3 * t + 3)
                stt(GK[:, t], PS[:, B6 + t % 2], 0.0, GT[:, t, 1], ALU.min, ALU.subtract).then_inc(gk_ready, 1)

            def to_last(h):
                dve.wait_ge(c_copied, h + 1)
                chunks = EU[:, h].rearrange("p (c t) -> p c t", t=CHUNK)
                link(nc.vector.tensor_copy(CL[:, h], chunks[:, :, CHUNK - 1]))
                tt(chunks, CL[:, h].unsqueeze(2).to_broadcast([P, NCH, CHUNK]), chunks, ALU.subtract).then_inc(d_ready, 1)

            for j in range(16):
                u = B_V + j
                dve.wait_ge(unit_done, u + 1)
                if j < 8:
                    if j >= 2:
                        dve.wait_ge(vtt_done, j - 1)
                    tt(VTT[:, j % 2], PS[:, j % 4], R[:], ALU.mult).then_inc(unit_evac, 1)
                elif j < 12:
                    h = j - 8
                    dve.wait_ge(epr_ready, h + 1)
                    stt(EP[:, h], PS[:, j % 4], B_SCALE, EP[:, h], ALU.mult, ALU.mult).then_inc(unit_evac, 1)
                else:
                    h = j - 12
                    if h >= 2:
                        dve.wait_ge(ku_ready, h - 1)
                    tt(KS[:, h % 2], PS[:, j % 4], R[:], ALU.mult).then_inc(unit_evac, 1)
                    dve.wait_ge(unit_evac, u + 1)
                    dve.wait_ge(ln_ready, h + 1)
                    tt(EN[:, h], KS[:, h % 2], EN[:, h], ALU.mult).then_inc(kd_ready, 1)
                lo_unit(u + 3)
                if 1 <= j <= 2:
                    log_gates(2 * j - 2)
                    log_gates(2 * j - 1)
                if j in (4, 6):
                    to_last(j - 4)
                    to_last(j - 3)

            def mask(h):
                if h == 0:
                    dve.wait_ge(am_zero, 1)
                dve.wait_ge(a_done, h + 1)
                nc.vector.copy_predicated(AM[:, h % 2], CAUSAL[:].bitcast(U32).unsqueeze(1).to_broadcast([P, 4, P]),
                                          PS[:, B4].rearrange("p (i c) -> p i c", i=4)).then_inc(am_ready, 1)

            def states(h):
                for c in range(NCH - 1):
                    dve.wait_ge(u_done, (NCH - 1) * h + min(c | 1, NCH - 2) + 1)
                    u = PS[:, B6 + (c // 2) % 2, (c % 2) * HV:(c % 2 + 1) * HV]
                    if c == 0:
                        nc.vector.tensor_copy(S[:, 1], u).then_inc(st_ready, 1)
                    else:
                        dve.wait_ge(st_ready, (NCH - 1) * h + c)
                        stt(S[:, c + 1], S[:, c], DEC[:, h, c:c + 1], u, ALU.mult, ALU.add).then_inc(st_ready, 1)

            def head_norm(h):
                dve.wait_ge(hstd_ready, h + 1)
                link(nc.vector.reciprocal(STD[:], STD[:]))
                for vt, o in ((0, EN), (1, EU)):
                    link(stt(o[:, h], o[:, h], BNORM[:, vt:vt + 1], STD[:], ALU.mult, ALU.mult))
                    dve.wait_ge(sg_ready, 2 * h + vt + 1)
                    tt(o[:, h], o[:, h], SG[:, 2 * h + vt], ALU.mult).then_inc(y_ready, 1)

            def head_lo(h):
                for vt, o in ((0, EN), (1, EU)):
                    dve.wait_ge(yh_ready, 2 * h + vt + 1)
                    tt(YL[:, 2 * h + vt], o[:, h], YH[:, 2 * h + vt].bitcast(F32), ALU.subtract).then_inc(yl_ready, 1)

            for h in range(BH):
                u = B_G + 2 * h
                mask(h)
                lo_unit(u + 3)
                dve.wait_ge(unit_done, u + 1)
                tt(SG[:, 2 * h], PS[:, 0], R[:], ALU.mult).then_inc(unit_evac, 1)
                states(h)
                if h >= 1:
                    head_norm(h - 1)
                    head_lo(h - 1)
                if h < 3:
                    lo_unit(u + 4)
                dve.wait_ge(unit_done, u + 2)
                tt(SG[:, 2 * h + 1], PS[:, 1], R[:], ALU.mult).then_inc(unit_evac, 1)
            lo_unit(B_O + 2)
            lo_unit(B_O + 3)
            head_norm(3)
            head_lo(3)
            for m in range(6):
                x_add(B_O + m, m, m % 4)
                x_lo(3, m)
                if m >= 1:
                    lo_unit(B_O + 3 + m)
            lo_unit(B_O + 9)
            ffn(1, 3)
            inverse_rms(4)
            for m in range(KT_D):
                stt(X[:, m], X[:, m], GAIN[:, 4, m:m + 1], R[:], ALU.mult, ALU.mult).then_inc(fin_ready, 1)

        @block.gpsimd
        def _(pool):
            steps = [0]

            def link(instruction):
                steps[0] += 1
                instruction.then_inc(pool_step, 1)
                pool.wait_ge(pool_step, steps[0])

            def sum_square(st, m, par=None):
                par = m % 2 if par is None else par
                pool.wait_ge(sq_ready, m + (KT_D * st + 1))
                if isinstance(m, int) and m == 0:
                    if st:
                        pool.wait_ge(std_ready, st)
                    nc.gpsimd.tensor_copy(SS[:], SQ[:, 0]).then_inc(ss_ready, 1)
                    pool.wait_ge(ss_ready, KT_D * st + 1)
                else:
                    nc.gpsimd.tensor_tensor(SS[:], SS[:], SQ[:, par], ALU.add).then_inc(ss_ready, 1)
                    pool.wait_ge(ss_ready, m + (KT_D * st + 1))

            def ffn(layer, st):
                for j in range(2):
                    sum_square(st, 6 + j)
                pool.wait_ge(r_ready, st + 1)
                with pool.Fori(0, FT, 2) as i:
                    for j in range(2):
                        pool.wait_ge(silu_ready, i + (FT * layer + j + 1))
                        nc.gpsimd.tensor_tensor(CV[:, j], CV[:, j], R[:], ALU.mult).then_inc(slr_ready, 1)
                        pool.wait_ge(slr_ready, i + (FT * layer + j + 1))
                for m in range(KT_D):
                    sum_square(st + 1, m)

            link(nc.gpsimd.memset(EPSC[:], EPS))
            link(nc.gpsimd.memset(ONES[:], 1.0))
            for half in range(2):
                link(nc.gpsimd.memset(QT[64 - 64 * half:P - 64 * half, :, half], 0.0))
            nc.gpsimd.memset(V[64:P, 1, 0], 0.0).then_inc(small_set, 1)
            pool.wait_ge(small_set, 1)
            for m in range(KT_D):
                sum_square(0, m)
            pool.wait_ge(ss_ready, KT_D)
            pool.wait_ge(bias_in, 16 * 12)
            link(nc.gpsimd.tensor_copy(BIAS[:, :, 0], BIAS[:, :, 1]))
            nc.gpsimd.memset(BIAS[:, :, 0, 0:2, 64:P], NEG).then_inc(bias_ready, 1)
            pool.wait_ge(bias_ready, 1)
            pool.wait_ge(v_copied, 2)
            link(nc.gpsimd.tensor_copy(V[0:64, 1], V[0:64, 0]))
            nc.gpsimd.tensor_copy(V[64:P, 1, 1:4], V[64:P, 0, 0:3]).then_inc(v_ready, 1)
            pool.wait_ge(v_ready, 1)
            link(nc.gpsimd.memset(GAH[:].bitcast(F32), 0.0))
            link(nc.gpsimd.memset(GAL[:].bitcast(F32), 0.0))
            pool.wait_ge(consts, 16 * 13)
            link(nc.gpsimd.tensor_copy(GAH[:, :, 0:RANK], GARAW[:]))
            nc.gpsimd.tensor_tensor(GAL[:, :, 0:RANK], GARAW[:], GAH[:, :, 0:RANK].bitcast(F32), ALU.subtract)\
                .then_inc(gal_ready, 1)
            pool.wait_ge(gal_ready, 1)
            for m in range(6):
                sum_square(1, m)
            ffn(0, 1)
            pool.wait_ge(unit_done, B_V)
            nc.gpsimd.memset(GAT[0:32, :], 1.0).then_inc(small_set, 2)
            pool.wait_ge(small_set, 3)
            for h in range(BH):
                pool.wait_ge(e_ready, h + 1)
                if h == 0:
                    pool.wait_ge(r_ready, 3)
                nc.gpsimd.tensor_tensor(EP[:, h], EP[:, h], R[:], ALU.mult).then_inc(epr_ready, 1)
                pool.wait_ge(epr_ready, h + 1)
            pool.wait_ge(ga_done, 1)
            link(nc.gpsimd.memset(KUT[:], 0.0))
            nc.gpsimd.memset(AM[:], 0.0).then_inc(am_zero, 1)
            pool.wait_ge(am_zero, 1)
            for h in range(BH):
                pool.wait_ge(unit_evac, B_K + h + 1)
                pool.wait_ge(ln_ready, h + 1)
                nc.gpsimd.tensor_tensor(EU[:, h], EU[:, h], KS[:, h % 2], ALU.mult).then_inc(ku_ready, 1)
                pool.wait_ge(ku_ready, h + 1)
            for m in range(6):
                sum_square(3, m)
            ffn(1, 3)


def _one_hot():
    rel = np.arange(REL) - 127
    half, exact = 16, 8
    n = np.abs(rel)
    large = exact + (np.log(np.maximum(n, 1).astype(np.float32) / exact) / np.log(128 / exact)
                     * (half - exact)).astype(np.int32)
    bucket = np.where(rel > 0, half, 0) + np.where(n < exact, n, np.minimum(large, half - 1))
    return (bucket[None, :] == np.arange(32)[:, None]).astype(np.float32)


def _causal():
    s, t = np.arange(P)[:, None], np.arange(P)[None, :]
    return ((s <= t) & (s // CHUNK == t // CHUNK)).astype(np.float32)


def _units(w, k):
    K, N = w.shape
    w = w.reshape(K // (k * P), k, P, N // P, P)
    return np.ascontiguousarray(w.transpose(3, 0, 2, 1, 4)).reshape(-1, P, k * P)


def _rows(v):
    return np.ascontiguousarray(np.moveaxis(v.reshape(*v.shape[:-1], -1, P), -1, 0))


def kernel(x, mix_norm, ffn_norm, final_norm, rel_bias, a_w_qkv, a_sinks, a_w_o, b_w_in, b_w_gate, b_gate_bias,
           b_norm, b_w_o, f_w_up, f_conv_w, f_conv_b, f_w_down):
    import concourse.bacc as bacc
    from concourse.bass_utils import run_bass_kernel_spmd

    x, mix_norm, ffn_norm, final_norm, rel_bias, a_w_qkv, a_sinks, a_w_o, b_w_in, b_w_gate, b_gate_bias, \
        b_norm, b_w_o, f_w_up, f_conv_w, f_conv_b, f_w_down = (
            np.asarray(a) for a in (x, mix_norm, ffn_norm, final_norm, rel_bias, a_w_qkv, a_sinks, a_w_o, b_w_in,
                                    b_w_gate, b_gate_bias, b_norm, b_w_o, f_w_up, f_conv_w, f_conv_b, f_w_down))
    w = a_w_qkv[0]
    nq, nk = A_HEADS * HD, KV * HD
    w_qkv = np.concatenate([w[:, nq:], w[:, :nq]], axis=1)
    w, dk, dv = b_w_in[0], BH * HK, BH * HV
    w_bin = np.concatenate([w[:, 2 * dk:2 * dk + dv], w[:, :2 * dk], w[:, 2 * dk + dv:2 * dk + 2 * dv]], axis=1)
    w_ga = w[:, 2 * dk + 2 * dv:].reshape(KT_D, P, RANK).transpose(1, 0, 2)
    w_up = np.stack([_units(f_w_up[n].reshape(D, 2, FT, P).transpose(0, 2, 1, 3).reshape(D, 2 * FF), KT_D)
                     for n in range(2)])
    sinks = np.repeat(a_sinks[0].reshape(KV, 2, 2).transpose(1, 0, 2), 64, axis=0)
    arrays = {
        "xT": x[0].T.reshape(KT_D, P, T).transpose(1, 0, 2),
        "gains": _rows(np.stack([mix_norm[0], ffn_norm[0], mix_norm[1], ffn_norm[1], final_norm])),
        "w_qkv": _units(w_qkv, KT_D), "sinks": sinks, "rel_bias": rel_bias, "w_o": _units(a_w_o[0], KT_D),
        "w_bin": _units(w_bin, KT_D), "w_ga": w_ga, "w_gate": np.concatenate([b_w_gate[0], b_gate_bias], axis=0),
        "b_norm": _rows(b_norm[0]), "w_bo": _units(b_w_o[0], KT_D), "w_up": w_up,
        "conv_w": f_conv_w.reshape(2, 3, FT, P).transpose(3, 0, 2, 1), "conv_b": _rows(f_conv_b),
        "w_down": np.stack([_units(f_w_down[n], HALF) for n in range(2)]),
        "onehot": _one_hot(), "ident": np.eye(P, dtype=np.float32), "causal": _causal(),
    }
    arrays = {k: np.ascontiguousarray(v) for k, v in arrays.items()}
    nc = bacc.Bacc("TRN2", target_bir_lowering=False, num_devices=1, dynamic_dma_scratch_size=1024)
    args = [nc.dram_tensor(k, v.shape, mybir.dt.from_np(v.dtype), kind="ExternalInput").ap() for k, v in arrays.items()]
    out = nc.dram_tensor("out", (P, KT_D, T), F32, kind="ExternalOutput").ap()
    bias_rows = nc.dram_tensor("bias_rows", (A_HEADS, 64 * REL), F32, kind="Internal").ap()
    trunk(nc, *args, out, bias_rows)
    got = run_bass_kernel_spmd(nc, [arrays], core_ids=[0]).results[0]["out"]
    return np.ascontiguousarray(np.asarray(got).transpose(2, 1, 0)).reshape(1, T, D)
```

```python
from contextlib import ExitStack

import numpy as np

import concourse.bass as bass
from concourse import mybir

F32, F32R, U32 = mybir.dt.float32, mybir.dt.float32r, mybir.dt.uint32
ALU, ACT, AX = mybir.AluOpType, mybir.ActivationFunctionType, mybir.AxisListType

P = 128
T = 512
D = 1024
KT_D = D // P
FF = 2816
FT = FF // P
HALF = FT // 2
CHUNK = 64
NCH = T // CHUNK
EPS = 1e-6
NEG = -1e30
A_HEADS, KV, HD = 16, 4, 64
A_SCALE = HD ** -0.5
BH, HK, HV = 4, 128, 256
B_SCALE = HK ** -0.5
RANK = 16
GATE_NORM = 16.0
REL = 2 * P - 64
SLOTS = 4
POOL_TILES = 2

A_K, A_V, A_Q, A_O = 0, 2, 4, 12
UP0, DOWN0 = 20, 64
B_V, B_Q, B_K, B_G, B_O = 80, 88, 92, 96, 104
UP1, DOWN1 = 112, 156
UP, DOWN = (UP0, UP1), (DOWN0, DOWN1)

B4, B5, B6, B7 = 4, 5, 6, 7


def trunk(nc, xT, gains, w_qkv, sinks, rel_bias, w_o, w_bin, w_ga, w_gate, b_norm, w_bo, w_up, conv_w, conv_b,
          w_down, onehot, ident, causal, out, bias_rows):
    with ExitStack() as ctx:
        place_at = [-(-nc.sbuf_base // 64) * 64]

        def place(name, shape, dt=F32, at=None):
            size = 4 * int(np.prod(shape[1:]))
            offset = place_at[0] if at is None else at
            if at is None:
                place_at[0] += -(-size // 64) * 64
            return nc.alloc_sbuf_tensor_at(name, shape, dt, offset=offset)

        def sem(name):
            return ctx.enter_context(nc.semaphore(name))

        X = place("X", [P, KT_D, T])
        XH = place("XH", [P, KT_D, T], F32R)
        XL = place("XL", [P, KT_D, T], F32R)
        WH = place("WH", [P, SLOTS, HALF * P], F32R)
        slots_at = place_at[0]
        WRAW = place("WRAW", [P, SLOTS, HALF * P])
        WL = place("WL", [P, SLOTS, HALF * P], F32R, at=slots_at)
        R = place("R", [P, T])
        STD = place("STD", [P, T])
        SS = place("SS", [P, T])
        SQ = place("SQ", [P, 2, T])
        ONES = place("ONES", [P, P])
        CONSTS = 9
        IDENT = place("IDENT", [P, P])
        CAUSAL = place("CAUSAL", [P, P])
        GAIN = place("GAIN", [P, 5, KT_D])
        CONVW = place("CONVW", [P, 2, FT, 3])
        CONVB = place("CONVB", [P, 2, FT])
        BNORM = place("BNORM", [P, 2])
        SINK = place("SINK", [P, KV, 2])
        EPSC = place("EPSC", [P, 1])
        WG = place("WG", [P, BH * HK])
        GARAW = place("GARAW", [P, KT_D, RANK])
        MX = place("MX", [P, 2, 4])
        NM = place("NM", [P, 2, 4])
        SM = place("SM", [P, 2, 4])
        ES = place("ES", [P, 2, 4])
        SUM = place("SUM", [P, 2, 4])
        RD = place("RD", [P, 2, 4])
        WARM = place("WARM", [P, 2])
        RMS = place("RMS", [P, 4])
        CL = place("CL", [P, BH, NCH])
        DEC = place("DEC", [P, BH, NCH])
        region = place_at[0]

        AH = place("AH", [P, FT, T], F32R)
        AL = place("AL", [P, FT, T], F32R)
        GS = place("GS", [P, 2, T + 2])
        CV = place("CV", [P, 2, T])
        AC = place("AC", [P, 2, T])
        end_ffn = place_at[0]

        place_at[0] = region
        KT = place("KT", [P, KV, 2, T])
        VT = place("VT", [P, 2, T])
        V = place("V", [P, 2, 4, KV * HD])
        QT = place("QT", [P, 2, NCH, 2 * CHUNK])
        SB = place("SB", [P, 2, 4, P])
        PB = place("PB", [P, 2, 4, P])
        PT = place("PT", [P, 2, 4, P])
        BIAS = place("BIAS", [P, KV, 2, 4, P])
        TB = place("TB", [P, REL])
        HOT = place("HOT", [P, REL])
        RB = place("RB", [P, A_HEADS])
        OH = place("OH", [P, KT_D, T], F32R)
        OL = place("OL", [P, KT_D, T], F32R)
        fifth_raw_a = place("FIFTH_RAW_A", [P, D])
        fifth_lo_a = place("FIFTH_LO_A", [P, D], F32R, at=place_at[0] - 4 * D)
        fifth_hi_a = place("FIFTH_HI_A", [P, D], F32R)
        end_a = place_at[0]

        place_at[0] = region
        EP = place("EP", [P, BH, T])
        EN = place("EN", [P, BH, T])
        EU = place("EU", [P, BH, T])
        VV = place("VV", [P, 4, BH * HV])
        S = place("S", [P, NCH, HV])
        SG = place("SG", [P, KT_D, T])
        y_at = place_at[0]
        YH = place("YH", [P, KT_D, T], F32R)
        YL = place("YL", [P, KT_D, T], F32R)
        GT = place("GT", [P, 4, 2, T], at=y_at)
        GK = place("GK", [P, 4, T], at=y_at + 16 * T * 2)
        vtt_at = place_at[0]
        VTT = place("VTT", [P, 2, T])
        KS = place("KS", [P, 2, T])
        GAT = place("GAT", [P, T])
        fifth_raw_b = nc.alloc_sbuf_tensor_at("FIFTH_RAW_B", [P, D], F32, offset=vtt_at)
        fifth_lo_b = nc.alloc_sbuf_tensor_at("FIFTH_LO_B", [P, D], F32R, offset=vtt_at)
        fifth_hi_b = nc.alloc_sbuf_tensor_at("FIFTH_HI_B", [P, D], F32R, offset=vtt_at + 4 * D)
        fifth = {A_O + 4: (fifth_raw_a, fifth_hi_a, fifth_lo_a), B_O + 4: (fifth_raw_b, fifth_hi_b, fifth_lo_b)}
        ga_at = max(end_a, end_ffn, place_at[0])
        GAH = place("GAH", [P, KT_D, P], F32R, at=ga_at)
        GAL = place("GAL", [P, KT_D, P], F32R, at=ga_at + 4 * KT_D * P)
        AM = place("AM", [P, 2, 4, P], at=ga_at)
        KUT = place("KUT", [P, 2, 4, P], at=ga_at + 4 * 2 * 4 * P)
        assert ga_at + 8 * KT_D * P <= nc.sbuf_usable_end

        PS = ctx.enter_context(nc.psum_tensor("PS", [P, 8, T], F32))

        raw_landed = [sem(f"raw_landed{s}") for s in range(SLOTS)]
        hi_ready, lo_ready = sem("hi_ready"), sem("lo_ready")
        unit_done = sem("unit_done")
        unit_evac = sem("unit_evac")
        x_landed = [sem(f"x_landed{i}") for i in range(4)]
        gain_landed, rel_landed, consts = sem("gain_landed"), sem("rel_landed"), sem("consts")
        small_set = sem("small_set")
        xh_ready, xl_ready = sem("xh_ready"), sem("xl_ready")
        sq_ready, ss_ready = sem("sq_ready"), sem("ss_ready")
        ms_done, std_ready, r_ready = sem("ms_done"), sem("std_ready"), sem("r_ready")
        tb_done, tb_ready, rows_out, bias_in = sem("tb_done"), sem("tb_ready"), sem("rows_out"), sem("bias_in")
        bias_ready, k_dup = sem("bias_ready"), sem("k_dup")
        vt_done, v_copied, v_ready = sem("vt_done"), sem("v_copied"), sem("v_ready")
        scores_done, s_ready, max_ready = sem("scores_done"), sem("s_ready"), sem("max_ready")
        exp_done, p_ready, pt_done, pt_ready = sem("exp_done"), sem("p_ready"), sem("pt_done"), sem("pt_ready")
        pv_done, oh_ready, ol_ready = sem("pv_done"), sem("oh_ready"), sem("ol_ready")
        dve_step = sem("dve_step")
        pool_step = sem("pool_step")
        c0_ready, c1_ready, conv_ready = sem("c0_ready"), sem("c1_ready"), sem("conv_ready")
        silu_ready, slr_ready, ah_ready, al_ready = sem("silu_ready"), sem("slr_ready"), sem("ah_ready"), sem("al_ready")
        gah_ready, gal_ready, ga_done, ga_ready = sem("gah_ready"), sem("gal_ready"), sem("ga_done"), sem("ga_ready")
        z_done, ln_ready, gk_ready, cum_done = sem("z_done"), sem("ln_ready"), sem("gk_ready"), sem("cum_done")
        act_step = sem("act_step")
        c_copied, d_ready, e_ready, epr_ready = sem("c_copied"), sem("d_ready"), sem("e_ready"), sem("epr_ready")
        vtt_done, vv_ready = sem("vtt_done"), sem("vv_ready")
        ks_ready, kd_ready, ku_ready, am_zero = sem("ks_ready"), sem("kd_ready"), sem("ku_ready"), sem("am_zero")
        a_done, am_ready, kut_done, kut_ready = sem("a_done"), sem("am_ready"), sem("kut_done"), sem("kut_ready")
        u_done, st_ready, o_done, o_ready = sem("u_done"), sem("st_ready"), sem("o_done"), sem("o_ready")
        hms_done, hstd_ready = sem("hms_done"), sem("hstd_ready")
        sg_ready, y_ready, yh_ready, yl_ready = sem("sg_ready"), sem("y_ready"), sem("yh_ready"), sem("yl_ready")
        last_sq_ready, diag_ready, r_spread = sem("last_sq_ready"), sem("diag_ready"), sem("r_spread")
        gained, pool_fin = sem("gained"), sem("pool_fin")
        fin_ready, out_written = sem("fin_ready"), sem("out_written")

        block = ctx.enter_context(nc.Block())

        def ksize(u):
            return HALF if DOWN0 <= u < B_V or u >= DOWN1 else KT_D

        @block.sync
        def _(sp):
            def load(u, src, k, first=False):
                s = u % SLOTS if isinstance(u, int) else first
                if not isinstance(u, int) or u >= SLOTS:
                    sp.wait_ge(unit_done, u - SLOTS + 1)
                sp.dma_start(WRAW[:, s, 0:k * P], src).then_inc(raw_landed[s], 16)

            def load_fifth(u, src):
                sp.wait_ge(hi_ready, u - SLOTS + 1)
                sp.dma_start(fifth[u][0][:], src).then_inc(raw_landed[0], 16)

            def load_all(u0, src, n, k):
                with sp.Fori(0, n - SLOTS + 1, SLOTS) as i:
                    for s in range(SLOTS):
                        sp.wait_ge(unit_done, i + (u0 + s - SLOTS + 1))
                        sp.dma_start(WRAW[:, s, 0:k * P], src[bass.ds(i + s, 1)].rearrange("a p c -> p (a c)"))\
                          .then_inc(raw_landed[s], 16)

            load(0, w_qkv[0], KT_D)
            sp.dma_start(X[:, 0:2], xT[:, 0:2]).then_inc(x_landed[0], 16)
            sp.dma_start(X[:, 2:4], xT[:, 2:4]).then_inc(x_landed[1], 16)
            sp.dma_start(X[:, 4:6], xT[:, 4:6]).then_inc(x_landed[2], 16)
            sp.dma_start(X[:, 6:8], xT[:, 6:8]).then_inc(x_landed[3], 16)
            for u in range(1, A_O):
                load(u, w_qkv[u], KT_D)
            for u in range(A_O, A_O + 4):
                load(u, w_o[u - A_O], KT_D)
            load_fifth(A_O + 4, w_o[4])
            for u in range(A_O + 5, UP0):
                load(u, w_o[u - A_O], KT_D)
            load_all(UP0, w_up[0], 2 * FT, KT_D)
            load_all(DOWN0, w_down[0], 2 * KT_D, HALF)
            load_all(B_V, w_bin, 24, KT_D)
            for u in range(B_O, B_O + 4):
                load(u, w_bo[u - B_O], KT_D)
            sp.wait_ge(vtt_done, 8)
            sp.wait_ge(kd_ready, 4)
            sp.wait_ge(ku_ready, 4)
            load_fifth(B_O + 4, w_bo[4])
            for u in range(B_O + 5, UP1):
                load(u, w_bo[u - B_O], KT_D)
            load_all(UP1, w_up[1], 2 * FT, KT_D)
            load_all(DOWN1, w_down[1], 2 * KT_D, HALF)
            for m in range(KT_D - POOL_TILES - 1):
                sp.wait_ge(fin_ready, m + 1)
                sp.dma_start(out[:, m], X[:, m]).then_inc(out_written, 16)
            for i in range(POOL_TILES):
                m = KT_D - POOL_TILES + i
                sp.wait_ge(pool_fin, i + 1)
                sp.dma_start(out[:, m], X[:, m]).then_inc(out_written, 16)
            m = KT_D - POOL_TILES - 1
            sp.wait_ge(fin_ready, m + 1)
            sp.dma_start(out[:, m], X[:, m]).then_inc(out_written, 16)
            sp.wait_ge(out_written, 16 * KT_D)

        @block.tensor
        def _(pe):
            mm = nc.tensor.matmul

            def product(s, bank, hi, lo, kbs, wkb, start=True, stop=True, part_ready=None, wh=None, wl=None):
                wh, wl = wh or WH[:, s], wl or WL[:, s]
                last = None
                for n, kb in enumerate(kbs):
                    if part_ready is not None:
                        pe.wait_ge(part_ready[0], part_ready[1] + kb + 1)
                    c = (wkb + n) * P
                    for w, x in ((wh, hi), (wh, lo), (wl, hi)):
                        last = mm(PS[:, bank], w[:, c:c + P], x[:, kb],
                                  start=start and n == 0 and w is wh and x is hi,
                                  stop=stop and n == len(kbs) - 1 and w is wl)
                return last

            def unit(u, s, hi, lo, bank=None, banks=4, **kw):
                pe.wait_ge(lo_ready, u + 1)
                if not isinstance(u, int) or u >= 4:
                    pe.wait_ge(unit_evac, u - banks + 1)
                product(s, s if bank is None else bank, hi, lo, range(KT_D), 0, **kw).then_inc(unit_done, 1)

            def mean_square(st):
                pe.wait_ge(ss_ready, KT_D * (st + 1))
                mm(PS[:, B4], ONES[:], SS[:], start=True, stop=True).then_inc(ms_done, 1)

            def up_phase(layer, st):
                u0 = UP[layer]
                for j in range(4):
                    unit(u0 + j, j, XH, XL, part_ready=(xl_ready, KT_D * st))
                    if j == 0:
                        mean_square(st)
                with pe.Fori(4, 2 * FT, 4) as i:
                    for s in range(SLOTS):
                        unit(i + (u0 + s), s, XH, XL)

            def down_unit(u, s, half):
                pe.wait_ge(lo_ready, u + 1)
                if half == 0:
                    pe.wait_ge(unit_evac, u - 3)
                return product(s, s & 2, AH, AL, range(half * HALF, half * HALF + HALF), 0,
                               start=half == 0, stop=half == 1)

            def down_phase(layer):
                u0 = DOWN[layer]
                for s in range(SLOTS):
                    if s == 0:
                        pe.wait_ge(al_ready, FT * layer + HALF)
                    if s == 1:
                        pe.wait_ge(lo_ready, u0 + 2)
                        last = None
                        for n in range(HALF):
                            kb = HALF + n
                            pe.wait_ge(al_ready, FT * layer + kb + 1)
                            for w, x in ((WH, AH), (WH, AL), (WL, AH)):
                                last = mm(PS[:, 0], w[:, 1, n * P:(n + 1) * P], x[:, kb], start=False,
                                          stop=n == HALF - 1 and w is WL)
                        last.then_inc(unit_done, 1)
                    else:
                        down_unit(u0 + s, s, s % 2).then_inc(unit_done, 1)
                with pe.Fori(4, 2 * KT_D, 4) as i:
                    for s in range(SLOTS):
                        down_unit(i + (u0 + s), s, s % 2).then_inc(unit_done, 1)

            unit(0, 0, XH, XL, part_ready=(xl_ready, 0))
            pe.wait_ge(rel_landed, 32)
            mm(PS[0:A_HEADS, B5, 0:REL], RB[0:32, :], HOT[0:32, :], start=True, stop=True).then_inc(tb_done, 1)
            unit(1, 1, XH, XL)
            pe.wait_ge(lo_ready, 3)
            product(2, 2, XH, XL, range(0, 2), 0, stop=False)
            pe.wait_ge(small_set, 1)
            mean_square(0)
            product(2, 2, XH, XL, range(2, 8), 2, start=False).then_inc(unit_done, 1)
            unit(3, 3, XH, XL)
            unit(4, 0, XH, XL)
            pe.wait_ge(consts, 16 * CONSTS)
            pe.wait_ge(unit_evac, A_V + 2)
            pe.wait_ge(tb_ready, 1)
            for t in range(4):
                for f in range(2):
                    last = nc.tensor.transpose(PS[:, B5 + t // 2, (t % 2) * 256 + f * P:(t % 2) * 256 + (f + 1) * P],
                                               VT[:, f, t * P:(t + 1) * P], IDENT[:])
            last.then_inc(vt_done, 1)
            unit(5, 1, XH, XL)

            def scores(k):
                g, p = divmod(k, 4)
                if k == 0:
                    pe.wait_ge(std_ready, 1)
                    pe.wait_ge(v_copied, 2)
                    pe.wait_ge(k_dup, 64)
                if k >= 2:
                    pe.wait_ge(s_ready, k - 1)
                if p == 0:
                    pe.wait_ge(unit_evac, A_Q + 2 * g + 2)
                for j in range(2):
                    for half in range(2):
                        q, keys = QT[:, g % 2, 2 * p + j], KT[:, g, half]
                        c = (2 * j + half) * P
                        o = PS[:, B4 + k % 2]
                        if j == 1:
                            last = mm(o[:, c:c + P], q, keys[:, 2 * p * 64:2 * p * 64 + P], start=True, stop=True)
                        else:
                            before = max(2 * p - 1, 0) * 64
                            mm(o[:, c:c + 64], q, keys[:, 2 * p * 64:2 * p * 64 + 64], start=True, stop=True)
                            last = mm(o[:, c + 64:c + P], q, keys[:, before:before + 64], start=True, stop=True)
                last.then_inc(scores_done, 1)

            def turn_probs(k):
                pe.wait_ge(p_ready, k + 1)
                if k >= 1:
                    pe.wait_ge(pt_ready, k)
                for i in range(4):
                    last = nc.tensor.transpose(PS[:, B6, i * P:(i + 1) * P], PB[:, k % 2, i], IDENT[:])
                last.then_inc(pt_done, 1)

            def values(k):
                g, p = divmod(k, 4)
                pe.wait_ge(pt_ready, k + 1)
                if k == 0:
                    pe.wait_ge(v_ready, 1)
                if k >= 1:
                    pe.wait_ge(ol_ready, k)
                for j in range(2):
                    for half in range(2):
                        last = mm(PS[64 * half:64 * half + 64, B7, j * P:(j + 1) * P],
                                  V[:, 1 - j, p, g * HD:(g + 1) * HD], PT[:, k % 2, 2 * j + half],
                                  start=True, stop=True)
                last.then_inc(pv_done, 1)

            def out_part(u, kbs, hi, lo, start, stop):
                return product(u % 4, u % 4, hi, lo, kbs, kbs[0], start=start, stop=stop)

            for k in range(16):
                g, p = divmod(k, 4)
                if g < 3:
                    u = A_Q + 2 + k // 2
                    if k % 2 == 0:
                        pe.wait_ge(lo_ready, u + 1)
                        pe.wait_ge(unit_evac, u - 3)
                    last = out_part(u, range(4 * (k % 2), 4 * (k % 2) + 4), XH, XL, k % 2 == 0, k % 2 == 1)
                    if k % 2 == 1:
                        last.then_inc(unit_done, 1)
                else:
                    u = A_O + p
                    pe.wait_ge(lo_ready, u + 1)
                    pe.wait_ge(unit_evac, u - 3)
                    pe.wait_ge(ol_ready, 8)
                    out_part(u, range(0, 4), OH, OL, True, False)
                scores(k)
                if k >= 1:
                    turn_probs(k - 1)
                if k >= 2:
                    values(k - 2)
            pe.wait_ge(ol_ready, 12)
            for u in range(A_O, A_O + 3):
                out_part(u, range(4, 6), OH, OL, False, False)
            turn_probs(15)
            values(14)
            out_part(A_O + 3, range(4, 6), OH, OL, False, False)
            values(15)
            pe.wait_ge(ol_ready, 16)
            for u in range(A_O, A_O + 4):
                out_part(u, range(6, 8), OH, OL, False, True).then_inc(unit_done, 1)
            unit(A_O + 4, 0, OH, OL, wh=fifth[A_O + 4][1], wl=fifth[A_O + 4][2])
            for u in range(A_O + 5, A_O + 8):
                unit(u, u % 4, OH, OL)

            up_phase(0, 1)
            down_phase(0)

            pe.wait_ge(gal_ready, 1)
            for kb in range(KT_D):
                pe.wait_ge(xl_ready, 2 * KT_D + kb + 1)
                for w, x in ((GAH, XH), (GAH, XL), (GAL, XH)):
                    last = mm(PS[:, B5], w[:, kb], x[:, kb], start=kb == 0 and w is GAH and x is XH,
                              stop=kb == KT_D - 1 and w is GAL)
            last.then_inc(ga_done, 1)
            mean_square(2)

            def gate_logits(t):
                if t == 0:
                    pe.wait_ge(ga_ready, 1)
                if t >= 2:
                    pe.wait_ge(gk_ready, t - 1)
                mm(PS[:, B6 + t % 2], GAT[0:RANK + 1, t * P:(t + 1) * P], WG[0:RANK + 1, :],
                   start=True, stop=True).then_inc(z_done, 1)

            def cumulate(h):
                pe.wait_ge(gk_ready, 4)
                if h >= 2:
                    pe.wait_ge(e_ready, h - 1)
                for t in range(4):
                    last = mm(PS[:, B6 + h % 2, t * P:(t + 1) * P], GK[:, t, h * HK:(h + 1) * HK], CAUSAL[:],
                              start=True, stop=True)
                last.then_inc(cum_done, 1)

            def turn_values(j):
                pe.wait_ge(unit_evac, B_V + j + 1)
                if j == 0:
                    pe.wait_ge(std_ready, 3)
                if j == 1:
                    pe.wait_ge(ga_ready, 1)
                if j >= 2:
                    pe.wait_ge(vv_ready, j - 1)
                for t in range(4):
                    last = nc.tensor.transpose(PS[:, B4 + j % 2, t * P:(t + 1) * P],
                                               VTT[:, j % 2, t * P:(t + 1) * P], IDENT[:])
                last.then_inc(vtt_done, 1)

            for j in range(16):
                unit(B_V + j, j % 4, XH, XL)
                if 1 <= j <= 2:
                    gate_logits(2 * j - 2)
                    gate_logits(2 * j - 1)
                if j in (4, 6):
                    cumulate(j - 4)
                    cumulate(j - 3)
                if 2 <= j <= 9:
                    turn_values(j - 2)

            def head_start(h):
                pe.wait_ge(kd_ready, h + 1)
                pe.wait_ge(ku_ready, h + 1)
                if h == 0:
                    pe.wait_ge(vv_ready, 8)
                if h >= 2:
                    pe.wait_ge(hstd_ready, h - 1)
                for p in range(4):
                    c = slice(p * P, (p + 1) * P)
                    last = mm(PS[:, B4, c], EN[:, h, c], EP[:, h, c], start=True, stop=True)
                last.then_inc(a_done, 1)
                for p in range(4):
                    c = slice(p * P, (p + 1) * P)
                    last = nc.tensor.transpose(PS[:, B5, c], EU[:, h, c], IDENT[:])
                last.then_inc(kut_done, 1)

            def state_updates(h):
                pe.wait_ge(kut_ready, h + 1)
                if h == 0:
                    pe.wait_ge(e_ready, 4)
                for c in range(NCH - 1):
                    if c % 2 == 0 and (c >= 4 or h >= 1):
                        pe.wait_ge(st_ready, (NCH - 1) * h + (c - 2 if c >= 4 else c + 4 - (NCH - 1) if c == 0 else 0))
                    mm(PS[:, B6 + (c // 2) % 2, (c % 2) * HV:(c % 2 + 1) * HV], KUT[:, c % 2, c // 2],
                       VV[:, c // 2, h * HV:(h + 1) * HV], start=True, stop=True).then_inc(u_done, 1)

            def outputs(h):
                pe.wait_ge(am_ready, h + 1)
                pe.wait_ge(st_ready, (NCH - 1) * (h + 1))
                for vt in range(2):
                    v0 = h * HV + vt * P
                    if h >= 1:
                        pe.wait_ge(o_ready, 2 * (h - 1) + vt + 1)
                    for p in range(4):
                        c0 = p * P
                        mm(PS[:, 2 + vt, c0:c0 + P], VV[:, p, v0:v0 + P], AM[:, h % 2, p], start=True, stop=False,
                           skip_group_check=True)
                        for c in ((1,) if p == 0 else (2 * p, 2 * p + 1)):
                            last = mm(PS[:, 2 + vt, c * 64:c * 64 + 64], S[:, c, vt * P:(vt + 1) * P],
                                      EP[:, h, c * 64:c * 64 + 64], start=False, stop=c % 2 == 1, skip_group_check=True)
                    last.then_inc(o_done, 1)

            def head_square(h):
                pe.wait_ge(o_ready, 2 * h + 2)
                if h < 3:
                    pe.wait_ge(am_ready, h + 2)
                mm(PS[:, B4], ONES[:], SQ[:, 0], start=True, stop=False)
                mm(PS[:, B4], ONES[:], SQ[:, 1], start=False, stop=True).then_inc(hms_done, 1)

            for h in range(BH):
                head_start(h)
                u = B_G + 2 * h
                if h == 0:
                    pe.wait_ge(unit_evac, B_G)
                unit(u, u % 4, XH, XL, bank=0, banks=2)
                if h >= 1:
                    head_square(h - 1)
                state_updates(h)
                unit(u + 1, (u + 1) % 4, XH, XL, bank=1, banks=2)
                outputs(h)
            for u in range(B_O, B_O + 4):
                pe.wait_ge(lo_ready, u + 1)
                if u == B_O:
                    pe.wait_ge(unit_evac, B_O)
                if u == B_O + 1:
                    head_square(3)
                if u == B_O + 2:
                    pe.wait_ge(o_ready, 8)
                pe.wait_ge(yl_ready, 6)
                out_part(u, range(0, 6), YH, YL, True, False)
            for u in range(B_O, B_O + 4):
                pe.wait_ge(yl_ready, 8)
                out_part(u, range(6, 8), YH, YL, False, True).then_inc(unit_done, 1)
            unit(B_O + 4, 0, YH, YL, wh=fifth[B_O + 4][1], wl=fifth[B_O + 4][2])
            for u in range(B_O + 5, B_O + 8):
                unit(u, u % 4, YH, YL)

            up_phase(1, 3)
            down_phase(1)
            pe.wait_ge(ss_ready, KT_D * 5 - 1)
            pe.wait_ge(last_sq_ready, 1)
            for t in range(4):
                for squares in (SS, SQ[:, 1]):
                    last = mm(PS[:, B4, t:t + 1], squares[:, t * P:(t + 1) * P], ONES[:, 0:1], start=squares is SS,
                              stop=squares is not SS)
            last.then_inc(ms_done, 1)
            for t in range(4):
                pe.wait_ge(diag_ready, t + 1)
                last = mm(PS[:, B5, t * P:(t + 1) * P], ONES[:], STD[:, t * P:(t + 1) * P], start=True, stop=True)
            last.then_inc(r_spread, 1)

        @block.scalar
        def _(act):
            A = nc.scalar.activation

            def hi(u, s, turn, k):
                act.wait_ge(raw_landed[s], 16 * turn + 16)
                nc.scalar.copy(WH[:, s, 0:k * P], WRAW[:, s, 0:k * P]).then_inc(hi_ready, 1)

            def hi_unit(u):
                if u in fifth:
                    act.wait_ge(raw_landed[0], 16 * (u // 4) + 16)
                    nc.scalar.copy(fifth[u][1][:], fifth[u][0][:]).then_inc(hi_ready, 1)
                else:
                    hi(u, u % 4, u // 4, ksize(u))

            def after_wait(m):
                return slice(m, m + 1) if isinstance(m, int) else bass.ds(act.snap(m), 1)

            def x_hi(st, m):
                A(XH[:, m:m + 1, :], X[:, m:m + 1, :], ACT.Copy, scale=GAIN[:, st, m:m + 1]).then_inc(xh_ready, 1)

            def x_square(st, m):
                if KT_D * st + m >= 2:
                    act.wait_ge(ss_ready, m + (KT_D * st - 1))
                A(SQ[:, m % 2], X[:, m], ACT.Square).then_inc(sq_ready, 1)

            def x_tile(st, m, m_even=None):
                par = m % 2 if m_even is None else m_even
                if not isinstance(m, int) or KT_D * st + m >= 2:
                    act.wait_ge(ss_ready, m + (KT_D * st - 1))
                tile = after_wait(m)
                if st < 4:
                    A(XH[:, tile, :], X[:, tile, :], ACT.Copy, scale=GAIN[:, st, tile]).then_inc(xh_ready, 1)
                A(SQ[:, par:par + 1, :], X[:, tile, :], ACT.Square).then_inc(sq_ready, 1)

            def std(st):
                act.wait_ge(ms_done, st + 1)
                A(STD[:], PS[:, B4], ACT.Sqrt, bias=EPSC[:], scale=1.0 / D).then_inc(std_ready, 1)

            def ffn_step(layer, m, par, before=None, after=None):
                u, f = UP[layer] + 2 * m, FT * layer + m
                act.wait_ge(unit_evac, u + 1)
                tile = after_wait(m)
                A(CV[:, par], GS[:, par, 2:T + 2], ACT.Identity, bias=CONVB[:, layer, tile],
                  scale=CONVW[:, layer, tile, 2]).then_inc(c0_ready, 1)
                if after:
                    after()
                act.wait_ge(conv_ready, f + 1)
                A(CV[:, par], CV[:, par], ACT.Silu).then_inc(silu_ready, 1)
                act.wait_ge(unit_evac, u + 2)
                tile = after_wait(m)
                nc.scalar.copy(AH[:, tile, :], AC[:, par:par + 1, :]).then_inc(ah_ready, 1)

            def ffn(layer, st):
                u0, d0 = UP[layer], DOWN[layer]
                for j in range(2):
                    act.wait_ge(unit_evac, u0 - 1 + j)
                    x_tile(st, 6 + j)
                    hi_unit(u0 + 2 + j)
                std(st)
                with act.Fori(1, FT - 1, 2) as i:
                    for j in range(2):
                        s, landed = 2 * j, 8 * i + (4 * u0 + 24)
                        act.wait_ge(raw_landed[s], landed)
                        nc.scalar.copy(WH[:, s, 0:D], WRAW[:, s, 0:D]).then_inc(hi_ready, 1)

                        def second(s=s, landed=landed):
                            act.wait_ge(raw_landed[s + 1], landed)
                            nc.scalar.copy(WH[:, s + 1, 0:D], WRAW[:, s + 1, 0:D]).then_inc(hi_ready, 1)
                        ffn_step(layer, i + (j - 1), j, after=second)
                hi_unit(d0)
                ffn_step(layer, FT - 2, 0, after=lambda: hi_unit(d0 + 1))
                hi_unit(d0 + 2)
                ffn_step(layer, FT - 1, 1, after=lambda: hi_unit(d0 + 3))
                with act.Fori(1, KT_D - 1, 2) as i:
                    for j in range(2):
                        s, landed = 2 * j, 8 * i + (4 * d0 + 24)
                        act.wait_ge(raw_landed[s], landed)
                        nc.scalar.copy(WH[:, s], WRAW[:, s]).then_inc(hi_ready, 1)
                        act.wait_ge(unit_evac, 2 * i + (d0 + 2 * j))
                        x_tile(st + 1, i + (j - 1), j)
                        act.wait_ge(raw_landed[s + 1], landed)
                        nc.scalar.copy(WH[:, s + 1], WRAW[:, s + 1]).then_inc(hi_ready, 1)
                if d0 + 16 < DOWN1:
                    hi_unit(d0 + 16)
                act.wait_ge(unit_evac, d0 + 14)
                x_tile(st + 1, 6)
                if d0 + 16 < DOWN1:
                    hi_unit(d0 + 17)
                    hi_unit(d0 + 18)
                if st + 1 < 4:
                    act.wait_ge(unit_evac, d0 + 16)
                    x_tile(st + 1, 7)

            act.dma_start(GAIN[:], gains).then_inc(gain_landed, 16)
            act.dma_start(RB[0:32, :], rel_bias).then_inc(rel_landed, 16)
            act.dma_start(HOT[0:32, :], onehot).then_inc(rel_landed, 16)
            act.wait_ge(small_set, 1)
            nc.scalar.copy(WARM[:, 0:1], EPSC[:])
            hi_unit(0)
            act.wait_ge(gain_landed, 16)
            for m in range(KT_D):
                if m % 2 == 0:
                    act.wait_ge(x_landed[m // 2], 16)
                x_hi(0, m)
                if m in (3, 5):
                    x_square(0, (m - 3) // 2)
            hi_unit(1)
            for m in range(2, KT_D):
                x_square(0, m)
                if m == 3:
                    hi_unit(2)
                if m == 6:
                    hi_unit(3)
                if m == 5:
                    act.wait_ge(tb_done, 1)
                    nc.scalar.copy(TB[0:A_HEADS, :], PS[0:A_HEADS, B5, 0:REL]).then_inc(tb_ready, 1)
                    act.wait_ge(tb_ready, 1)
                    act.dma_start(bias_rows.rearrange("h (q r) -> h q r", q=64),
                                  TB[0:A_HEADS, :].rearrange("h (o r) -> h o r", o=1).to_broadcast([A_HEADS, 64, REL]))\
                       .then_inc(rows_out, 16)
            std(0)
            hi_unit(4)
            hi_unit(5)
            for dst, src in ((IDENT[:], ident), (CAUSAL[:], causal), (SINK[:], sinks), (CONVW[:], conv_w),
                             (CONVB[:], conv_b), (BNORM[:], b_norm), (WG[0:RANK, :], w_gate[0:RANK]),
                             (WG[RANK:RANK + 1, :], w_gate[RANK:RANK + 1]), (GARAW[:], w_ga)):
                act.dma_start(dst, src).then_inc(consts, 16)
            act.wait_ge(rows_out, 16)
            for hh in range(2):
                for half in range(2):
                    def stretch(first, n, hh=hh, half=half):
                        return bass.AP(tensor=bias_rows.tensor,
                                       offset=bias_rows.offset + (2 * hh + half) * 64 * REL + 63 + first,
                                       ap=[[REL - 1, 64], [4 * 64 * REL, KV], [1, n]])
                    rows = slice(64 * hh, 64 * hh + 64)
                    act.dma_start(BIAS[rows, :, 1, half, 0:64], stretch(64, 64)).then_inc(bias_in, 16)
                    act.dma_start(BIAS[rows, :, 1, half, 64:P], stretch(0, 64)).then_inc(bias_in, 16)
                    act.dma_start(BIAS[rows, :, 1, 2 + half], stretch(0, P)).then_inc(bias_in, 16)
            for g in range(KV):
                if g % 2 == 0:
                    act.wait_ge(unit_evac, g // 2 + 1)
                here, there = slice(64 * (g % 2), 64 * (g % 2) + 64), slice(64 - 64 * (g % 2), 128 - 64 * (g % 2))
                act.dma_start(KT[there, g, 1 - g % 2], KT[here, g, g % 2]).then_inc(k_dup, 16)
            hi_unit(6)
            act.wait_ge(vt_done, 1)
            for b in range(2):
                nc.scalar.copy(V[:, 0, 2 * b:2 * b + 2], PS[:, B5 + b].rearrange("p (t f) -> p t f", t=2)).then_inc(v_copied, 1)
            hi_unit(7)

            def softmax_exp(k):
                act.wait_ge(max_ready, k + 1)
                for i in range(4):
                    A(PB[:, k % 2, i], SB[:, k % 2, i], ACT.Exp, bias=NM[:, k % 2, i:i + 1],
                      accum_out=SUM[:, k % 2, i:i + 1])
                A(ES[:, k % 2], SM[:, k % 2], ACT.Exp).then_inc(exp_done, 1)

            def probs_copy(k):
                act.wait_ge(pt_done, k + 1)
                if k >= 2:
                    act.wait_ge(pv_done, k - 1)
                nc.scalar.copy(PT[:, k % 2], PS[:, B6].rearrange("p (i c) -> p i c", i=4)).then_inc(pt_ready, 1)

            def o_view(k):
                return PS[:, B7, 0:2 * P].rearrange("p (j a q) -> p a j q", j=2, a=2)

            def o_tiles(t, k):
                g, p = divmod(k, 4)
                return t[:, 2 * g:2 * g + 2, p * P:(p + 1) * P].rearrange("p a (j q) -> p a j q", j=2)

            def o_hi(k):
                act.wait_ge(pv_done, k + 1)
                nc.scalar.copy(o_tiles(OH, k), o_view(k)).then_inc(oh_ready, 1)

            for k in range(16):
                g, p = divmod(k, 4)
                if k >= 1:
                    probs_copy(k - 1)
                if k >= 2:
                    o_hi(k - 2)
                softmax_exp(k)
                if k % 2 == 0 and k <= 8:
                    hi_unit(8 + k // 2)
                elif 9 <= k <= 12 and k != 10:
                    hi_unit(k + 3 if k > 9 else 13)
                elif k == 14:
                    hi_unit(A_O + 4)
            probs_copy(15)
            o_hi(14)
            o_hi(15)
            for m in range(6):
                act.wait_ge(unit_evac, A_O + m + 1)
                x_tile(1, m)
                if m >= 1:
                    hi_unit(A_O + 4 + m)
            ffn(0, 1)

            std(2)

            def decays(h):
                act.wait_ge(cum_done, h + 1)
                nc.scalar.copy(EU[:, h], PS[:, B6 + h % 2]).then_inc(c_copied, 1)
                A(EP[:, h], PS[:, B6 + h % 2], ACT.Exp, scale=1.0 / GATE_NORM)
                A(EN[:, h], PS[:, B6 + h % 2], ACT.Exp, scale=-1.0 / GATE_NORM).then_inc(e_ready, 1)
                act.wait_ge(d_ready, h + 1)
                A(EU[:, h], EU[:, h], ACT.Exp, scale=1.0 / GATE_NORM)
                A(DEC[:, h], CL[:, h], ACT.Exp, scale=1.0 / GATE_NORM).then_inc(ln_ready, 1)

            def values_copy(j):
                act.wait_ge(vtt_done, j + 1)
                nc.scalar.copy(VV[:, :, j * P:(j + 1) * P], PS[:, B4 + j % 2].rearrange("p (t f) -> p t f", t=4))\
                   .then_inc(vv_ready, 1)

            def gates(t0):
                for t in (t0, t0 + 1):
                    act.wait_ge(z_done, t + 1)
                    A(GT[:, t, 0], PS[:, B6 + t % 2], ACT.Abs).then_inc(act_step, 1)
                for t in (t0, t0 + 1):
                    act.wait_ge(act_step, 3 * t0 + 2)
                    A(GT[:, t, 0], GT[:, t, 0], ACT.Exp, scale=-1.0).then_inc(act_step, 1)
                for t in (t0, t0 + 1):
                    act.wait_ge(act_step, 3 * t0 + 4)
                    A(GT[:, t, 1], GT[:, t, 0], ACT.Ln, bias=1.0).then_inc(act_step, 1)

            for j in range(16):
                hi_unit(B_V + j + 3)
                if 1 <= j <= 2:
                    gates(2 * j - 2)
                if j in (4, 6):
                    decays(j - 4)
                    decays(j - 3)
                if 2 <= j <= 9:
                    values_copy(j - 2)

            def head_keys(h):
                act.wait_ge(kut_done, h + 1)
                if h == 0:
                    act.wait_ge(am_zero, 1)
                for half in range(2):
                    rows = slice(64 * half, 64 * half + 64)
                    last = nc.scalar.copy(KUT[rows, half], PS[rows, B5].rearrange("p (i c) -> p i c", i=4))
                last.then_inc(kut_ready, 1)

            def head_outputs(h):
                for vt, o in ((0, EN), (1, EU)):
                    act.wait_ge(o_done, 2 * h + vt + 1)
                    nc.scalar.copy(o[:, h], PS[:, 2 + vt]).then_inc(act_step, 1)
                    if h >= 1 and vt == 0:
                        act.wait_ge(hms_done, h)
                    A(SQ[:, vt], PS[:, 2 + vt], ACT.Square).then_inc(o_ready, 1)

            def head_std(h):
                act.wait_ge(hms_done, h + 1)
                if h >= 1:
                    act.wait_ge(y_ready, 2 * h)
                A(STD[:], PS[:, B4], ACT.Sqrt, bias=EPSC[:], scale=1.0 / HV).then_inc(hstd_ready, 1)

            def silu(j):
                act.wait_ge(unit_evac, B_G + j + 1)
                A(SG[:, j], SG[:, j], ACT.Silu).then_inc(sg_ready, 1)

            def head_hi(h):
                for vt in range(2):
                    act.wait_ge(y_ready, 2 * h + vt + 1)
                    nc.scalar.copy(YH[:, 2 * h + vt], (EN if vt == 0 else EU)[:, h]).then_inc(yh_ready, 1)

            for h in range(BH):
                head_keys(h)
                u = B_G + 2 * h
                hi_unit(u + 3)
                if h >= 1:
                    head_std(h - 1)
                silu(2 * h)
                if h >= 1:
                    head_hi(h - 1)
                if h < 3:
                    hi_unit(u + 4)
                silu(2 * h + 1)
                head_outputs(h)
            hi_unit(B_O + 2)
            hi_unit(B_O + 3)
            head_std(3)
            head_hi(3)
            hi_unit(B_O + 4)
            for m in range(6):
                act.wait_ge(unit_evac, B_O + m + 1)
                x_tile(3, m)
                if m >= 1:
                    hi_unit(B_O + 4 + m)
            ffn(1, 3)
            A(WARM[:, 1:2], EPSC[:], ACT.Sqrt)
            act.wait_ge(ms_done, 5)
            A(RMS[:], PS[:, B4, 0:4], ACT.Sqrt, bias=EPSC[:], scale=1.0 / D).then_inc(std_ready, 1)
            act.wait_ge(last_sq_ready, 1)
            for m in range(KT_D - POOL_TILES, KT_D):
                nc.scalar.activation(X[:, m], X[:, m], ACT.Copy, scale=GAIN[:, 4, m:m + 1]).then_inc(gained, 1)

        @block.vector
        def _(dve):
            tt, stt, ts = nc.vector.tensor_tensor, nc.vector.scalar_tensor_tensor, nc.vector.tensor_scalar
            steps = [0]

            def link(instruction):
                steps[0] += 1
                instruction.then_inc(dve_step, 1)
                dve.wait_ge(dve_step, steps[0])

            def lo(u, s, k):
                dve.wait_ge(hi_ready, u + 1)
                tt(WL[:, s, 0:k * P], WRAW[:, s, 0:k * P], WH[:, s, 0:k * P].bitcast(F32), ALU.subtract).then_inc(lo_ready, 1)

            def lo_unit(u):
                if u in fifth:
                    raw, high, low = fifth[u]
                    dve.wait_ge(hi_ready, u + 1)
                    tt(low[:], raw[:], high[:].bitcast(F32), ALU.subtract).then_inc(lo_ready, 1)
                else:
                    lo(u, u % 4, ksize(u))

            def tile_of(m):
                return slice(m, m + 1) if isinstance(m, int) else bass.ds(m, 1)

            def x_lo(st, m):
                tile = tile_of(m)
                dve.wait_ge(xh_ready, m + (KT_D * st + 1))
                stt(XL[:, tile, :], X[:, tile, :], GAIN[:, st, tile], XH[:, tile, :].bitcast(F32),
                    ALU.mult, ALU.subtract).then_inc(xl_ready, 1)

            def x_add(u_last, m, bank, n=1):
                tile = tile_of(m)
                dve.wait_ge(unit_done, u_last + 1)
                tt(X[:, tile, :], PS[:, bank:bank + 1], X[:, tile, :], ALU.add).then_inc(unit_evac, n)

            def inverse_rms(st):
                dve.wait_ge(std_ready, st + 1)
                nc.vector.reciprocal(R[:], STD[:]).then_inc(r_ready, 1)
                dve.wait_ge(r_ready, st + 1)

            def ffn_step(layer, m, par, mid=None, after=None):
                u, f = UP[layer] + 2 * m, FT * layer + m
                tile = tile_of(m)
                gate, up = (0, 1) if par == 0 else (2, 3)
                dve.wait_ge(unit_done, u + 1)
                tt(GS[:, par, 2:T + 2], PS[:, gate], R[:], ALU.mult).then_inc(unit_evac, 1)
                if mid:
                    mid()
                dve.wait_ge(c0_ready, f + 1)
                stt(CV[:, par], GS[:, par, 1:T + 1], CONVW[:, layer, tile, 1], CV[:, par], ALU.mult, ALU.add)\
                    .then_inc(c1_ready, 1)
                dve.wait_ge(c1_ready, f + 1)
                stt(CV[:, par], GS[:, par, 0:T], CONVW[:, layer, tile, 0], CV[:, par], ALU.mult, ALU.add)\
                    .then_inc(conv_ready, 1)
                if after:
                    after()
                dve.wait_ge(unit_done, u + 2)
                dve.wait_ge(slr_ready, f + 1)
                tt(AC[:, par], PS[:, up], CV[:, par], ALU.mult).then_inc(unit_evac, 1)
                dve.wait_ge(ah_ready, f + 1)
                tt(AL[:, tile, :], AC[:, par:par + 1, :], AH[:, tile, :].bitcast(F32), ALU.subtract).then_inc(al_ready, 1)

            def ffn(layer, st):
                u0, d0 = UP[layer], DOWN[layer]
                for j in range(2):
                    x_add(u0 - 2 + j, 6 + j, 2 + j)
                    x_lo(st, 6 + j)
                    lo_unit(u0 + 2 + j)
                nc.vector.memset(GS[:, :, 0:2], 0.0)
                inverse_rms(st)
                with dve.Fori(1, FT - 1, 2) as i:
                    for j in range(2):
                        s = 2 * j
                        ffn_step(layer, i + (j - 1), j,
                                 mid=lambda: lo(2 * i + (u0 + 2 * j + 2), s, KT_D),
                                 after=lambda: lo(2 * i + (u0 + 2 * j + 3), s + 1, KT_D))
                ffn_step(layer, FT - 2, 0, mid=lambda: lo_unit(d0), after=lambda: lo_unit(d0 + 1))
                ffn_step(layer, FT - 1, 1, mid=lambda: lo_unit(d0 + 2), after=lambda: lo_unit(d0 + 3))
                with dve.Fori(1, KT_D - 1, 2) as i:
                    for j in range(2):
                        s = 2 * j
                        lo(2 * i + (d0 + 2 * j + 2), s, HALF)
                        x_add(2 * i + (d0 + 2 * j - 1), i + (j - 1), 2 * j, 2)
                        if st + 1 < 4:
                            x_lo(st + 1, i + (j - 1))
                        lo(2 * i + (d0 + 2 * j + 3), s + 1, HALF)
                for m in (6, 7):
                    if m == 6 and st + 1 < 4:
                        lo_unit(d0 + 16)
                    x_add(d0 + 2 * m + 1, m, 2 * (m % 2), 2)
                    if st + 1 < 4:
                        x_lo(st + 1, m)
                        lo_unit(d0 + 17 + (m - 6))

            lo_unit(0)
            dve.wait_ge(gain_landed, 16)
            for m in range(KT_D):
                if m % 2 == 0:
                    dve.wait_ge(x_landed[m // 2], 16)
                x_lo(0, m)
            for u in range(1, 4):
                lo_unit(u)
            inverse_rms(0)

            for t in range(2):
                dve.wait_ge(unit_done, A_K + t + 1)
                for half in range(2):
                    rows = slice(64 * half, 64 * half + 64)
                    last = tt(KT[rows, 2 * t + half, half], PS[rows, t], R[rows], ALU.mult)
                last.then_inc(unit_evac, 1)
                if t:
                    lo_unit(4)
            for t in range(2):
                dve.wait_ge(unit_done, A_V + t + 1)
                tt(VT[:, t], PS[:, 2 + t], R[:], ALU.mult).then_inc(unit_evac, 1)
                lo_unit(5 + t)

            def queries(u):
                dve.wait_ge(unit_done, u + 1)
                by_chunk = lambda t: t.rearrange("p (c q) -> p c q", q=CHUNK)
                a = CHUNK * (u % 2)
                tt(QT[:, (u - A_Q) // 2 % 2, :, a:a + CHUNK], by_chunk(PS[:, u % 4]), by_chunk(R[:]), ALU.mult)\
                    .then_inc(unit_evac, 1)

            dve.wait_ge(consts, 16 * CONSTS)
            queries(A_Q)
            lo_unit(7)
            queries(A_Q + 1)

            def softmax_max(k):
                g, p = divmod(k, 4)
                if p == 0:
                    dve.wait_ge(bias_ready, g + 1)
                dve.wait_ge(scores_done, k + 1)
                b = k % 2
                stt(SB[:, b].rearrange("p i c -> p (i c)"), PS[:, B4 + b], A_SCALE,
                    BIAS[:, g, min(p, 1)].rearrange("p i c -> p (i c)"), ALU.mult, ALU.add).then_inc(s_ready, 1)
                dve.wait_ge(s_ready, k + 1)
                link(nc.vector.tensor_reduce(MX[:, b], SB[:, b], AX.X, ALU.max))
                sink = SINK[:, g:g + 1, :].to_broadcast([P, 2, 2])
                two = lambda t: t[:, b].rearrange("p (j h) -> p j h", j=2)
                link(tt(two(MX), two(MX), sink, ALU.max))
                tt(two(SM), sink, two(MX), ALU.subtract)
                ts(NM[:, b], MX[:, b], -1.0, None, ALU.mult).then_inc(max_ready, 1)

            def softmax_divide(k):
                b = k % 2
                dve.wait_ge(exp_done, k + 1)
                link(tt(RD[:, b], SUM[:, b], ES[:, b], ALU.add))
                link(nc.vector.reciprocal(RD[:, b], RD[:, b]))
                tt(PB[:, b], PB[:, b], RD[:, b].unsqueeze(2).to_broadcast([P, 4, P]), ALU.mult).then_inc(p_ready, 1)

            def o_lo(k):
                g, p = divmod(k, 4)
                dve.wait_ge(oh_ready, k + 1)
                view = lambda t: t[:, 2 * g:2 * g + 2, p * P:(p + 1) * P].rearrange("p a (j q) -> p a j q", j=2)
                tt(view(OL), PS[:, B7, 0:2 * P].rearrange("p (j a q) -> p a j q", j=2, a=2), view(OH).bitcast(F32),
                   ALU.subtract).then_inc(ol_ready, 1)

            for k in range(16):
                g, p = divmod(k, 4)
                softmax_max(k)
                if g < 3 and k % 2 == 1:
                    queries(A_Q + 2 + k // 2)
                if k >= 2:
                    o_lo(k - 2)
                if k % 2 == 1 and k <= 9:
                    lo_unit(8 + k // 2)
                elif 10 <= k <= 13 and k != 11:
                    lo_unit(k + 2 if k > 10 else 13)
                elif k == 15:
                    lo_unit(A_O + 4)
                softmax_divide(k)
            o_lo(14)
            o_lo(15)
            for m in range(6):
                x_add(A_O + m, m, m % 4)
                x_lo(1, m)
                if m >= 1:
                    lo_unit(A_O + 4 + m)
            ffn(0, 1)

            inverse_rms(2)
            dve.wait_ge(ga_done, 1)
            dve.wait_ge(small_set, 3)
            tt(GAT[0:RANK, :], PS[0:RANK, B5], R[0:RANK], ALU.mult).then_inc(ga_ready, 1)

            def log_gates(t):
                dve.wait_ge(act_step, 3 * (t - t % 2) + t % 2 + 5)
                stt(GK[:, t], PS[:, B6 + t % 2], 0.0, GT[:, t, 1], ALU.min, ALU.subtract).then_inc(gk_ready, 1)

            def to_last(h):
                dve.wait_ge(c_copied, h + 1)
                chunks = EU[:, h].rearrange("p (c t) -> p c t", t=CHUNK)
                link(nc.vector.tensor_copy(CL[:, h], chunks[:, :, CHUNK - 1]))
                tt(chunks, CL[:, h].unsqueeze(2).to_broadcast([P, NCH, CHUNK]), chunks, ALU.subtract).then_inc(d_ready, 1)

            for j in range(16):
                u = B_V + j
                dve.wait_ge(unit_done, u + 1)
                if j < 8:
                    if j >= 2:
                        dve.wait_ge(vtt_done, j - 1)
                    tt(VTT[:, j % 2], PS[:, j % 4], R[:], ALU.mult).then_inc(unit_evac, 1)
                elif j < 12:
                    h = j - 8
                    dve.wait_ge(epr_ready, h + 1)
                    stt(EP[:, h], PS[:, j % 4], B_SCALE, EP[:, h], ALU.mult, ALU.mult).then_inc(unit_evac, 1)
                else:
                    h = j - 12
                    if h >= 2:
                        dve.wait_ge(ku_ready, h - 1)
                    tt(KS[:, h % 2], PS[:, j % 4], R[:], ALU.mult).then_inc(unit_evac, 1)
                    dve.wait_ge(unit_evac, u + 1)
                    dve.wait_ge(ln_ready, h + 1)
                    tt(EN[:, h], KS[:, h % 2], EN[:, h], ALU.mult).then_inc(kd_ready, 1)
                lo_unit(u + 3)
                if 1 <= j <= 2:
                    log_gates(2 * j - 2)
                    log_gates(2 * j - 1)
                if j in (4, 6):
                    to_last(j - 4)
                    to_last(j - 3)

            def mask(h):
                if h == 0:
                    dve.wait_ge(am_zero, 1)
                dve.wait_ge(a_done, h + 1)
                nc.vector.copy_predicated(AM[:, h % 2], CAUSAL[:].bitcast(U32).unsqueeze(1).to_broadcast([P, 4, P]),
                                          PS[:, B4].rearrange("p (i c) -> p i c", i=4)).then_inc(am_ready, 1)

            def states(h):
                for c in range(NCH - 1):
                    dve.wait_ge(u_done, (NCH - 1) * h + min(c | 1, NCH - 2) + 1)
                    u = PS[:, B6 + (c // 2) % 2, (c % 2) * HV:(c % 2 + 1) * HV]
                    if c == 0:
                        nc.vector.tensor_copy(S[:, 1], u).then_inc(st_ready, 1)
                    else:
                        dve.wait_ge(st_ready, (NCH - 1) * h + c)
                        stt(S[:, c + 1], S[:, c], DEC[:, h, c:c + 1], u, ALU.mult, ALU.add).then_inc(st_ready, 1)

            def head_norm(h):
                dve.wait_ge(hstd_ready, h + 1)
                link(nc.vector.reciprocal(STD[:], STD[:]))
                for vt, o in ((0, EN), (1, EU)):
                    link(stt(o[:, h], o[:, h], BNORM[:, vt:vt + 1], STD[:], ALU.mult, ALU.mult))
                    dve.wait_ge(sg_ready, 2 * h + vt + 1)
                    tt(o[:, h], o[:, h], SG[:, 2 * h + vt], ALU.mult).then_inc(y_ready, 1)

            def head_lo(h):
                for vt, o in ((0, EN), (1, EU)):
                    dve.wait_ge(yh_ready, 2 * h + vt + 1)
                    tt(YL[:, 2 * h + vt], o[:, h], YH[:, 2 * h + vt].bitcast(F32), ALU.subtract).then_inc(yl_ready, 1)

            for h in range(BH):
                u = B_G + 2 * h
                mask(h)
                lo_unit(u + 3)
                dve.wait_ge(unit_done, u + 1)
                tt(SG[:, 2 * h], PS[:, 0], R[:], ALU.mult).then_inc(unit_evac, 1)
                states(h)
                if h >= 1:
                    head_norm(h - 1)
                    head_lo(h - 1)
                if h < 3:
                    lo_unit(u + 4)
                dve.wait_ge(unit_done, u + 2)
                tt(SG[:, 2 * h + 1], PS[:, 1], R[:], ALU.mult).then_inc(unit_evac, 1)
            lo_unit(B_O + 2)
            lo_unit(B_O + 3)
            head_norm(3)
            head_lo(3)
            lo_unit(B_O + 4)
            for m in range(6):
                x_add(B_O + m, m, m % 4)
                x_lo(3, m)
                if m >= 1:
                    lo_unit(B_O + 4 + m)
            ffn(1, 3)
            dve.wait_ge(ss_ready, KT_D * 5 - 2)
            dve.wait_ge(unit_evac, DOWN1 + 16)
            tt(SQ[:, 1], X[:, 7], X[:, 7], ALU.mult).then_inc(last_sq_ready, 1)
            dve.wait_ge(std_ready, 5)
            link(nc.vector.reciprocal(RMS[:], RMS[:]))
            for t in range(4):
                ts(STD[:, t * P:(t + 1) * P], IDENT[:], RMS[:, t:t + 1], None, ALU.mult).then_inc(diag_ready, 1)
            dve.wait_ge(r_spread, 1)
            nc.vector.tensor_copy(R[:], PS[:, B5]).then_inc(r_ready, 1)
            dve.wait_ge(r_ready, 5)
            for m in range(KT_D - POOL_TILES):
                stt(X[:, m], X[:, m], GAIN[:, 4, m:m + 1], R[:], ALU.mult, ALU.mult).then_inc(fin_ready, 1)

        @block.gpsimd
        def _(pool):
            steps = [0]

            def link(instruction):
                steps[0] += 1
                instruction.then_inc(pool_step, 1)
                pool.wait_ge(pool_step, steps[0])

            def sum_square(st, m, par=None):
                par = m % 2 if par is None else par
                pool.wait_ge(sq_ready, m + (KT_D * st + 1))
                if isinstance(m, int) and m == 0:
                    if st:
                        pool.wait_ge(std_ready, st)
                    nc.gpsimd.tensor_copy(SS[:], SQ[:, 0]).then_inc(ss_ready, 1)
                    pool.wait_ge(ss_ready, KT_D * st + 1)
                else:
                    nc.gpsimd.tensor_tensor(SS[:], SS[:], SQ[:, par], ALU.add).then_inc(ss_ready, 1)
                    pool.wait_ge(ss_ready, m + (KT_D * st + 1))

            def ffn(layer, st):
                for j in range(2):
                    sum_square(st, 6 + j)
                pool.wait_ge(r_ready, st + 1)
                with pool.Fori(0, FT, 2) as i:
                    for j in range(2):
                        pool.wait_ge(silu_ready, i + (FT * layer + j + 1))
                        nc.gpsimd.tensor_tensor(CV[:, j], CV[:, j], R[:], ALU.mult).then_inc(slr_ready, 1)
                        pool.wait_ge(slr_ready, i + (FT * layer + j + 1))
                for m in range(KT_D if st + 1 < 4 else KT_D - 1):
                    sum_square(st + 1, m)

            link(nc.gpsimd.memset(EPSC[:], EPS))
            link(nc.gpsimd.memset(ONES[:], 1.0))
            for half in range(2):
                link(nc.gpsimd.memset(KT[64 - 64 * half:P - 64 * half, :, half], 0.0))
            nc.gpsimd.memset(V[64:P, 1, 0], 0.0).then_inc(small_set, 1)
            pool.wait_ge(small_set, 1)
            for m in range(KT_D):
                sum_square(0, m)
            pool.wait_ge(ss_ready, KT_D)
            pool.wait_ge(bias_in, 16 * 12)
            for g in range(KV):
                link(nc.gpsimd.tensor_copy(BIAS[:, g, 0], BIAS[:, g, 1]))
                nc.gpsimd.memset(BIAS[:, g, 0, 0:2, 64:P], NEG).then_inc(bias_ready, 1)
                pool.wait_ge(bias_ready, g + 1)
                if g == 0:
                    pool.wait_ge(v_copied, 2)
                    link(nc.gpsimd.tensor_copy(V[0:64, 1], V[0:64, 0]))
                    nc.gpsimd.tensor_copy(V[64:P, 1, 1:4], V[64:P, 0, 0:3]).then_inc(v_ready, 1)
                    pool.wait_ge(v_ready, 1)
            link(nc.gpsimd.memset(GAH[:].bitcast(F32), 0.0))
            link(nc.gpsimd.memset(GAL[:].bitcast(F32), 0.0))
            pool.wait_ge(consts, 16 * CONSTS)
            link(nc.gpsimd.tensor_copy(GAH[:, :, 0:RANK], GARAW[:]))
            nc.gpsimd.tensor_tensor(GAL[:, :, 0:RANK], GARAW[:], GAH[:, :, 0:RANK].bitcast(F32), ALU.subtract)\
                .then_inc(gal_ready, 1)
            pool.wait_ge(gal_ready, 1)
            for m in range(6):
                sum_square(1, m)
            ffn(0, 1)
            pool.wait_ge(unit_done, B_V)
            nc.gpsimd.memset(GAT[0:32, :], 1.0).then_inc(small_set, 2)
            pool.wait_ge(small_set, 3)
            for h in range(BH):
                pool.wait_ge(e_ready, h + 1)
                if h == 0:
                    pool.wait_ge(r_ready, 3)
                nc.gpsimd.tensor_tensor(EP[:, h], EP[:, h], R[:], ALU.mult).then_inc(epr_ready, 1)
                pool.wait_ge(epr_ready, h + 1)
            pool.wait_ge(ga_done, 1)
            link(nc.gpsimd.memset(KUT[:], 0.0))
            nc.gpsimd.memset(AM[:], 0.0).then_inc(am_zero, 1)
            pool.wait_ge(am_zero, 1)
            for h in range(BH):
                pool.wait_ge(unit_evac, B_K + h + 1)
                pool.wait_ge(ln_ready, h + 1)
                nc.gpsimd.tensor_tensor(EU[:, h], EU[:, h], KS[:, h % 2], ALU.mult).then_inc(ku_ready, 1)
                pool.wait_ge(ku_ready, h + 1)
            for m in range(6):
                sum_square(3, m)
            ffn(1, 3)
            pool.wait_ge(gained, POOL_TILES)
            pool.wait_ge(r_ready, 5)
            for i in range(POOL_TILES):
                m = KT_D - POOL_TILES + i
                nc.gpsimd.tensor_tensor(X[:, m], X[:, m], R[:], ALU.mult).then_inc(pool_fin, 1)
                pool.wait_ge(pool_fin, i + 1)


def _one_hot():
    rel = np.arange(REL) - 127
    half, exact = 16, 8
    n = np.abs(rel)
    large = exact + (np.log(np.maximum(n, 1).astype(np.float32) / exact) / np.log(128 / exact)
                     * (half - exact)).astype(np.int32)
    bucket = np.where(rel > 0, half, 0) + np.where(n < exact, n, np.minimum(large, half - 1))
    return (bucket[None, :] == np.arange(32)[:, None]).astype(np.float32)


def _causal():
    s, t = np.arange(P)[:, None], np.arange(P)[None, :]
    return ((s <= t) & (s // CHUNK == t // CHUNK)).astype(np.float32)


def _units(w, k):
    K, N = w.shape
    w = w.reshape(K // (k * P), k, P, N // P, P)
    return np.ascontiguousarray(w.transpose(3, 0, 2, 1, 4)).reshape(-1, P, k * P)


def _rows(v):
    return np.ascontiguousarray(np.moveaxis(v.reshape(*v.shape[:-1], -1, P), -1, 0))


def kernel(x, mix_norm, ffn_norm, final_norm, rel_bias, a_w_qkv, a_sinks, a_w_o, b_w_in, b_w_gate, b_gate_bias,
           b_norm, b_w_o, f_w_up, f_conv_w, f_conv_b, f_w_down):
    import concourse.bacc as bacc
    from concourse.bass_utils import run_bass_kernel_spmd

    x, mix_norm, ffn_norm, final_norm, rel_bias, a_w_qkv, a_sinks, a_w_o, b_w_in, b_w_gate, b_gate_bias, \
        b_norm, b_w_o, f_w_up, f_conv_w, f_conv_b, f_w_down = (
            np.asarray(a) for a in (x, mix_norm, ffn_norm, final_norm, rel_bias, a_w_qkv, a_sinks, a_w_o, b_w_in,
                                    b_w_gate, b_gate_bias, b_norm, b_w_o, f_w_up, f_conv_w, f_conv_b, f_w_down))
    w = a_w_qkv[0]
    nq, nk = A_HEADS * HD, KV * HD
    w_qkv = np.concatenate([w[:, nq:], w[:, :nq]], axis=1)
    w, dk, dv = b_w_in[0], BH * HK, BH * HV
    w_bin = np.concatenate([w[:, 2 * dk:2 * dk + dv], w[:, :2 * dk], w[:, 2 * dk + dv:2 * dk + 2 * dv]], axis=1)
    w_ga = w[:, 2 * dk + 2 * dv:].reshape(KT_D, P, RANK).transpose(1, 0, 2)
    w_up = np.stack([_units(f_w_up[n].reshape(D, 2, FT, P).transpose(0, 2, 1, 3).reshape(D, 2 * FF), KT_D)
                     for n in range(2)])
    sinks = np.repeat(a_sinks[0].reshape(KV, 2, 2).transpose(1, 0, 2), 64, axis=0)
    arrays = {
        "xT": x[0].T.reshape(KT_D, P, T).transpose(1, 0, 2),
        "gains": _rows(np.stack([mix_norm[0], ffn_norm[0], mix_norm[1], ffn_norm[1], final_norm])),
        "w_qkv": _units(w_qkv, KT_D), "sinks": sinks, "rel_bias": rel_bias, "w_o": _units(a_w_o[0], KT_D),
        "w_bin": _units(w_bin, KT_D), "w_ga": w_ga, "w_gate": np.concatenate([b_w_gate[0], b_gate_bias], axis=0),
        "b_norm": _rows(b_norm[0]), "w_bo": _units(b_w_o[0], KT_D), "w_up": w_up,
        "conv_w": f_conv_w.reshape(2, 3, FT, P).transpose(3, 0, 2, 1), "conv_b": _rows(f_conv_b),
        "w_down": np.stack([_units(f_w_down[n], HALF) for n in range(2)]),
        "onehot": _one_hot(), "ident": np.eye(P, dtype=np.float32), "causal": _causal(),
    }
    arrays = {k: np.ascontiguousarray(v) for k, v in arrays.items()}
    nc = bacc.Bacc("TRN2", target_bir_lowering=False, num_devices=1, dynamic_dma_scratch_size=1024)
    args = [nc.dram_tensor(k, v.shape, mybir.dt.from_np(v.dtype), kind="ExternalInput").ap() for k, v in arrays.items()]
    out = nc.dram_tensor("out", (P, KT_D, T), F32, kind="ExternalOutput").ap()
    bias_rows = nc.dram_tensor("bias_rows", (A_HEADS, 64 * REL), F32, kind="Internal").ap()
    trunk(nc, *args, out, bias_rows)
    got = run_bass_kernel_spmd(nc, [arrays], core_ids=[0]).results[0]["out"]
    return np.ascontiguousarray(np.asarray(got).transpose(2, 1, 0)).reshape(1, T, D)
```

```python
from contextlib import ExitStack

import numpy as np

import concourse.bass as bass
from concourse import mybir

F32, F32R, U32 = mybir.dt.float32, mybir.dt.float32r, mybir.dt.uint32
ALU, ACT, AX = mybir.AluOpType, mybir.ActivationFunctionType, mybir.AxisListType

P = 128
T = 512
D = 1024
KT_D = D // P
FF = 2816
FT = FF // P
HALF = FT // 2
CHUNK = 64
NCH = T // CHUNK
EPS = 1e-6
NEG = -1e30
A_HEADS, KV, HD = 16, 4, 64
A_SCALE = HD ** -0.5
BH, HK, HV = 4, 128, 256
B_SCALE = HK ** -0.5
RANK = 16
LO = 32
GATE_NORM = 16.0
REL = 2 * P - 64
SLOTS = 4
TH = T // 2
DVE_TILES = 6

A_K, A_V, A_Q, A_O = 0, 2, 4, 12
UP0, DOWN0 = 20, 64
B_V, B_Q, B_K, B_G, B_O = 80, 88, 92, 96, 104
UP1, DOWN1 = 112, 156
UP, DOWN = (UP0, UP1), (DOWN0, DOWN1)

END_BANKS = ((1, 4, 5), (3, 6, 7))
V_TILES = ((5, 0, 0), (5, 1, 128), (6, 0, 256), (6, 1, 384), (7, 0, 64), (7, 1, 192), (4, 0, 320))

B4, B5, B6, B7 = 4, 5, 6, 7


def trunk(nc, xT, gains, w_qkv, sinks, rel_bias, w_o, w_bin, w_ga, w_gate, b_norm, w_bo, w_up, conv_w, conv_b,
          w_down, onehot, ident, causal, causal_pair, out, bias_rows):
    with ExitStack() as ctx:
        place_at = [-(-nc.sbuf_base // 64) * 64]

        def place(name, shape, dt=F32, at=None):
            size = 4 * int(np.prod(shape[1:]))
            offset = place_at[0] if at is None else at
            if at is None:
                place_at[0] += -(-size // 64) * 64
            return nc.alloc_sbuf_tensor_at(name, shape, dt, offset=offset)

        def sem(name):
            return ctx.enter_context(nc.semaphore(name))

        X = place("X", [P, KT_D, T])
        XH = place("XH", [P, KT_D, T], F32R)
        XL = place("XL", [P, KT_D, T], F32R)
        WH = place("WH", [P, SLOTS, HALF * P], F32R)
        slots_at = place_at[0]
        WRAW = place("WRAW", [P, SLOTS, HALF * P])
        WL = place("WL", [P, SLOTS, HALF * P], F32R, at=slots_at)
        R = place("R", [P, T])
        STD = place("STD", [P, T])
        SS = place("SS", [P, T])
        SQ = place("SQ", [P, 2, T])
        ONES = place("ONES", [P, P])
        CONSTS = 11
        IDENT = place("IDENT", [P, P])
        CAUSAL = place("CAUSAL", [P, P])
        CAUSAL2 = place("CAUSAL2", [P, P])
        GAIN = place("GAIN", [P, 5, KT_D])
        CONVW = place("CONVW", [P, 2, FT, 3])
        CONVB = place("CONVB", [P, 2, FT])
        BNORM = place("BNORM", [P, 2])
        SINK = place("SINK", [P, KV, 2])
        EPSC = place("EPSC", [P, 1])
        WG = place("WG", [P, BH * HK])
        GARAW = place("GARAW", [P, KT_D, RANK])
        MX = place("MX", [P, 2, 4])
        NM = place("NM", [P, 2, 4])
        SM = place("SM", [P, 2, 4])
        ES = place("ES", [P, 2, 4])
        SUM = place("SUM", [P, 2, 4])
        RD = place("RD", [P, 2, 4])
        WARM = place("WARM", [P, 2])
        RMS = place("RMS", [P, 4])
        CL = place("CL", [P, BH, NCH])
        DEC = place("DEC", [P, BH, NCH])
        DEC2 = place("DEC2", [P, BH, NCH // 2])
        region = place_at[0]

        AH = place("AH", [P, FT, T], F32R)
        AL = place("AL", [P, FT, T], F32R)
        GS = place("GS", [P, 2, T + 2])
        CV = place("CV", [P, 2, T])
        AC = place("AC", [P, 2, T])
        end_ffn = place_at[0]

        place_at[0] = region
        KT = place("KT", [P, KV, 2, T])
        VT = place("VT", [P, 2, T])
        V = place("V", [P, 2, 4, KV * HD])
        QT = place("QT", [P, 2, NCH, 2 * CHUNK])
        SB = place("SB", [P, 2, 4, P])
        PB = place("PB", [P, 2, 4, P])
        PT = place("PT", [P, 2, 4, P])
        BIAS = place("BIAS", [P, KV, 4, P])
        TB = place("TB", [P, REL])
        HOT = place("HOT", [P, REL])
        RB = place("RB", [P, A_HEADS])
        OH = place("OH", [P, KT_D, T], F32R)
        OL = place("OL", [P, KT_D, T], F32R)
        fifth_raw_a = place("FIFTH_RAW_A", [P, D])
        fifth_lo_a = place("FIFTH_LO_A", [P, D], F32R, at=place_at[0] - 4 * D)
        fifth_hi_a = place("FIFTH_HI_A", [P, D], F32R)
        end_a = place_at[0]

        place_at[0] = region
        EP = place("EP", [P, BH, T])
        EN = place("EN", [P, BH, T])
        EU = place("EU", [P, BH, T])
        VV = place("VV", [P, 4, BH * HV])
        S = place("S", [P, NCH // 2, HV])
        SG = place("SG", [P, KT_D, T])
        y_at = place_at[0]
        YH = place("YH", [P, KT_D, T], F32R)
        YL = place("YL", [P, KT_D, T], F32R)
        GT = place("GT", [P, 4, 2, T], at=y_at)
        GK = place("GK", [P, 4, T], at=y_at + 16 * T * 2)
        vtt_at = place_at[0]
        VTT = place("VTT", [P, 2, T])
        KS = place("KS", [P, 2, T])
        GAT = place("GAT", [P, T])
        fifth_raw_b = nc.alloc_sbuf_tensor_at("FIFTH_RAW_B", [P, D], F32, offset=vtt_at)
        fifth_lo_b = nc.alloc_sbuf_tensor_at("FIFTH_LO_B", [P, D], F32R, offset=vtt_at)
        fifth_hi_b = nc.alloc_sbuf_tensor_at("FIFTH_HI_B", [P, D], F32R, offset=vtt_at + 4 * D)
        fifth = {A_O + 4: (fifth_raw_a, fifth_hi_a, fifth_lo_a), B_O + 4: (fifth_raw_b, fifth_hi_b, fifth_lo_b)}
        ga_at = max(end_a, end_ffn, place_at[0])
        GA = place("GA", [P, KT_D, P], F32R, at=ga_at)
        AM = place("AM", [P, 2, 4, P], at=ga_at)
        KUT = place("KUT", [P, 4, P], at=ga_at + 4 * 2 * 4 * P)
        assert ga_at + 8 * KT_D * P <= nc.sbuf_usable_end

        PS = ctx.enter_context(nc.psum_tensor("PS", [P, 8, T], F32))

        raw_landed = [sem(f"raw_landed{s}") for s in range(SLOTS)]
        hi_ready, lo_ready = sem("hi_ready"), sem("lo_ready")
        unit_done = sem("unit_done")
        unit_evac = sem("unit_evac")
        first_landed, first_hi, first_lo = sem("first_landed"), sem("first_hi"), sem("first_lo")
        x_landed = [sem(f"x_landed{i}") for i in range(4)]
        gain_landed, rel_landed, consts = sem("gain_landed"), sem("rel_landed"), sem("consts")
        ones_set, eps_set = sem("ones_set"), sem("eps_set")
        small_set = sem("small_set")
        xh_ready, xl_ready = sem("xh_ready"), sem("xl_ready")
        sq_ready, ss_ready = sem("sq_ready"), sem("ss_ready")
        ms_done, std_ready, r_ready = sem("ms_done"), sem("std_ready"), sem("r_ready")
        tb_done, tb_ready, rows_out, bias_in = sem("tb_done"), sem("tb_ready"), sem("rows_out"), sem("bias_in")
        bias_ready, k_dup = sem("bias_ready"), sem("k_dup")
        vt_done, v_copied = sem("vt_done"), sem("v_copied")
        scores_done, s_ready, max_ready = sem("scores_done"), sem("s_ready"), sem("max_ready")
        exp_done, p_ready, pt_done, pt_ready = sem("exp_done"), sem("p_ready"), sem("pt_done"), sem("pt_ready")
        pv_done, oh_ready, ol_ready = sem("pv_done"), sem("oh_ready"), sem("ol_ready")
        dve_step = sem("dve_step")
        pool_step = sem("pool_step")
        c0_ready, c1_ready, conv_ready = sem("c0_ready"), sem("c1_ready"), sem("conv_ready")
        silu_ready, slr_ready, ah_ready, al_ready = sem("silu_ready"), sem("slr_ready"), sem("ah_ready"), sem("al_ready")
        gal_ready, ga_done, ga_ready = sem("gal_ready"), sem("ga_done"), sem("ga_ready")
        z_done, ln_ready, gk_ready, cum_done = sem("z_done"), sem("ln_ready"), sem("gk_ready"), sem("cum_done")
        act_step = sem("act_step")
        c_copied, d_ready, e_ready, epr_ready = sem("c_copied"), sem("d_ready"), sem("e_ready"), sem("epr_ready")
        vtt_done, vv_ready = sem("vtt_done"), sem("vv_ready")
        kd_ready, ku_ready, am_zero = sem("kd_ready"), sem("ku_ready"), sem("am_zero")
        carried = sem("carried")
        a_done, am_ready, kut_done, kut_ready = sem("a_done"), sem("am_ready"), sem("kut_done"), sem("kut_ready")
        u_done, st_ready, o_done, o_ready = sem("u_done"), sem("st_ready"), sem("o_done"), sem("o_ready")
        hsum_ready, hms_done, hstd_ready = sem("hsum_ready"), sem("hms_done"), sem("hstd_ready")
        sg_ready, y_ready, yh_ready, yl_ready = sem("sg_ready"), sem("y_ready"), sem("yh_ready"), sem("yl_ready")
        last_done, last_sq_ready = sem("last_done"), sem("last_sq_ready")
        diag_ready, r_spread = sem("diag_ready"), sem("r_spread")
        gained, pool_fin = sem("gained"), sem("pool_fin")
        fin_ready, out_written = sem("fin_ready"), sem("out_written")

        block = ctx.enter_context(nc.Block())

        def ksize(u):
            return HALF if DOWN0 <= u < B_V or u >= DOWN1 else KT_D

        @block.sync
        def _(sp):
            def load(u, src, k, first=False):
                s = u % SLOTS if isinstance(u, int) else first
                if not isinstance(u, int) or u >= SLOTS:
                    sp.wait_ge(unit_done, u - SLOTS + 1)
                sp.dma_start(WRAW[:, s, 0:k * P], src).then_inc(raw_landed[s], 16)

            def load_fifth(u, src):
                sp.wait_ge(hi_ready, u - SLOTS + 1)
                sp.dma_start(fifth[u][0][:], src).then_inc(raw_landed[0], 16)

            def load_all(u0, src, n, k):
                with sp.Fori(0, n - SLOTS + 1, SLOTS) as i:
                    for s in range(SLOTS):
                        sp.wait_ge(unit_done, i + (u0 + s - SLOTS + 1))
                        sp.dma_start(WRAW[:, s, 0:k * P], src[bass.ds(i + s, 1)].rearrange("a p c -> p (a c)"))\
                          .then_inc(raw_landed[s], 16)

            sp.dma_start(WRAW[:, 0, 0:D // 2], w_qkv[0, :, 0:D // 2]).then_inc(first_landed, 16)
            sp.dma_start(X[:, 0:2], xT[:, 0:2]).then_inc(x_landed[0], 16)
            sp.dma_start(WRAW[:, 0, D // 2:D], w_qkv[0, :, D // 2:D]).then_inc(raw_landed[0], 16)
            sp.dma_start(X[:, 2:4], xT[:, 2:4]).then_inc(x_landed[1], 16)
            sp.dma_start(X[:, 4:6], xT[:, 4:6]).then_inc(x_landed[2], 16)
            sp.dma_start(X[:, 6:8], xT[:, 6:8]).then_inc(x_landed[3], 16)
            for u in range(1, A_O):
                load(u, w_qkv[u], KT_D)
            for u in range(A_O, A_O + 4):
                load(u, w_o[u - A_O], KT_D)
            load_fifth(A_O + 4, w_o[4])
            for u in range(A_O + 5, UP0):
                load(u, w_o[u - A_O], KT_D)
            load_all(UP0, w_up[0], 2 * FT, KT_D)
            load_all(DOWN0, w_down[0], 2 * KT_D, HALF)
            load_all(B_V, w_bin, 24, KT_D)
            for u in range(B_O, B_O + 4):
                load(u, w_bo[u - B_O], KT_D)
            sp.wait_ge(vtt_done, 8)
            sp.wait_ge(kd_ready, 4)
            sp.wait_ge(ku_ready, 4)
            load_fifth(B_O + 4, w_bo[4])
            for u in range(B_O + 5, UP1):
                load(u, w_bo[u - B_O], KT_D)
            load_all(UP1, w_up[1], 2 * FT, KT_D)
            load_all(DOWN1, w_down[1], 2 * KT_D, HALF)
            stores = 0
            for half, pieces in enumerate((((0, 3), (3, 5)), ((0, 1), (1, 3), (3, 5)))):
                tokens = slice(half * TH, (half + 1) * TH)
                for m0, m1 in pieces:
                    sp.wait_ge(fin_ready, DVE_TILES * half + m1)
                    sp.dma_start(out[:, m0:m1, tokens], X[:, m0:m1, tokens]).then_inc(out_written, 16)
                sp.wait_ge(pool_fin, (KT_D - DVE_TILES) * (half + 1))
                sp.dma_start(out[:, DVE_TILES:, tokens], X[:, DVE_TILES:, tokens]).then_inc(out_written, 16)
                sp.wait_ge(fin_ready, DVE_TILES * (half + 1))
                sp.dma_start(out[:, DVE_TILES - 1, tokens], X[:, DVE_TILES - 1, tokens]).then_inc(out_written, 16)
                stores += len(pieces) + 2
            sp.wait_ge(out_written, 16 * stores)

        @block.tensor
        def _(pe):
            mm = nc.tensor.matmul

            def product(s, bank, hi, lo, kbs, wkb, start=True, stop=True, part_ready=None, wh=None, wl=None):
                wh, wl = wh or WH[:, s], wl or WL[:, s]
                last = None
                for n, kb in enumerate(kbs):
                    if part_ready is not None:
                        pe.wait_ge(part_ready[0], part_ready[1] + kb + 1)
                    c = (wkb + n) * P
                    for w, x in ((wh, hi), (wh, lo), (wl, hi)):
                        last = mm(PS[:, bank], w[:, c:c + P], x[:, kb],
                                  start=start and n == 0 and w is wh and x is hi,
                                  stop=stop and n == len(kbs) - 1 and w is wl)
                return last

            def unit(u, s, hi, lo, bank=None, banks=4, **kw):
                pe.wait_ge(lo_ready, u + 1)
                if not isinstance(u, int) or u >= 4:
                    pe.wait_ge(unit_evac, u - banks + 1)
                product(s, s if bank is None else bank, hi, lo, range(KT_D), 0, **kw).then_inc(unit_done, 1)

            def mean_square(st):
                pe.wait_ge(ss_ready, KT_D * (st + 1))
                mm(PS[:, B4], ONES[:], SS[:], start=True, stop=True).then_inc(ms_done, 1)

            def up_phase(layer, st):
                u0 = UP[layer]
                for j in range(4):
                    unit(u0 + j, j, XH, XL, part_ready=(xl_ready, KT_D * st))
                    if j == 0:
                        mean_square(st)
                with pe.Fori(4, 2 * FT, 4) as i:
                    for s in range(SLOTS):
                        unit(i + (u0 + s), s, XH, XL)

            def down_unit(u, s, half):
                pe.wait_ge(lo_ready, u + 1)
                if half == 0:
                    pe.wait_ge(unit_evac, u - 3)
                return product(s, s & 2, AH, AL, range(half * HALF, half * HALF + HALF), 0,
                               start=half == 0, stop=half == 1)

            def down_phase(layer):
                u0 = DOWN[layer]
                for s in range(SLOTS):
                    if s == 0:
                        pe.wait_ge(al_ready, FT * layer + HALF)
                    if s == 1:
                        pe.wait_ge(lo_ready, u0 + 2)
                        last = None
                        for n in range(HALF):
                            kb = HALF + n
                            pe.wait_ge(al_ready, FT * layer + kb + 1)
                            for w, x in ((WH, AH), (WH, AL), (WL, AH)):
                                last = mm(PS[:, 0], w[:, 1, n * P:(n + 1) * P], x[:, kb], start=False,
                                          stop=n == HALF - 1 and w is WL)
                        last.then_inc(unit_done, 1)
                    else:
                        down_unit(u0 + s, s, s % 2).then_inc(unit_done, 1)
                with pe.Fori(4, 2 * KT_D - (4 if layer else 0), 4) as i:
                    for s in range(SLOTS):
                        down_unit(i + (u0 + s), s, s % 2).then_inc(unit_done, 1)

            pe.wait_ge(first_lo, 1)
            product(0, 0, XH, XL, range(0, 4), 0, stop=False, part_ready=(xl_ready, 0))
            pe.wait_ge(lo_ready, 1)
            product(0, 0, XH, XL, range(4, 8), 4, start=False, part_ready=(xl_ready, 0)).then_inc(unit_done, 1)
            pe.wait_ge(rel_landed, 32)
            mm(PS[0:A_HEADS, B5, 0:REL], RB[0:32, :], HOT[0:32, :], start=True, stop=True).then_inc(tb_done, 1)
            unit(1, 1, XH, XL)
            pe.wait_ge(lo_ready, 3)
            product(2, 2, XH, XL, range(0, 4), 0, stop=False)
            pe.wait_ge(ones_set, 1)
            mean_square(0)
            product(2, 2, XH, XL, range(4, 8), 4, start=False).then_inc(unit_done, 1)
            unit(3, 3, XH, XL)
            unit(4, 0, XH, XL)
            pe.wait_ge(consts, 16 * CONSTS)
            pe.wait_ge(unit_evac, A_V + 2)
            pe.wait_ge(tb_ready, 1)
            pe.wait_ge(std_ready, 1)
            for bank, half, first in V_TILES:
                for f in range(2):
                    c = half * 2 * P + f * P
                    last = nc.tensor.transpose(PS[:, bank, c:c + P], VT[:, f, first:first + P], IDENT[:])
            last.then_inc(vt_done, 1)
            unit(5, 1, XH, XL)

            def scores(k):
                g, p = divmod(k, 4)
                if k == 0:
                    pe.wait_ge(std_ready, 1)
                    pe.wait_ge(v_copied, 4)
                    pe.wait_ge(k_dup, 64)
                if k >= 2:
                    pe.wait_ge(s_ready, k - 1)
                if p == 0:
                    pe.wait_ge(unit_evac, A_Q + 2 * g + 2)
                for j in range(2):
                    for half in range(2):
                        q, keys = QT[:, g % 2, 2 * p + j], KT[:, g, half]
                        c = (2 * j + half) * P
                        first = max(2 * p - 1 + j, 0) * CHUNK
                        last = mm(PS[:, B4 + k % 2, c:c + P], q, keys[:, first:first + P], start=True, stop=True)
                last.then_inc(scores_done, 1)

            def turn_probs(k):
                pe.wait_ge(p_ready, k + 1)
                if k >= 1:
                    pe.wait_ge(pt_ready, k)
                for i in range(4):
                    last = nc.tensor.transpose(PS[:, B6, i * P:(i + 1) * P], PB[:, k % 2, i], IDENT[:])
                last.then_inc(pt_done, 1)

            def values(k):
                g, p = divmod(k, 4)
                pe.wait_ge(pt_ready, k + 1)
                if k >= 1:
                    pe.wait_ge(ol_ready, k)
                for j in range(2):
                    for half in range(2):
                        last = mm(PS[64 * half:64 * half + 64, B7, j * P:(j + 1) * P],
                                  V[:, 1 - j if p else 0, p, g * HD:(g + 1) * HD], PT[:, k % 2, 2 * j + half],
                                  start=True, stop=True)
                last.then_inc(pv_done, 1)

            def out_part(u, kbs, hi, lo, start, stop):
                return product(u % 4, u % 4, hi, lo, kbs, kbs[0], start=start, stop=stop)

            for k in range(16):
                g, p = divmod(k, 4)
                if g < 3:
                    u = A_Q + 2 + k // 2
                    if k % 2 == 0:
                        pe.wait_ge(lo_ready, u + 1)
                        pe.wait_ge(unit_evac, u - 3)
                    last = out_part(u, range(4 * (k % 2), 4 * (k % 2) + 4), XH, XL, k % 2 == 0, k % 2 == 1)
                    if k % 2 == 1:
                        last.then_inc(unit_done, 1)
                else:
                    u = A_O + p
                    pe.wait_ge(lo_ready, u + 1)
                    pe.wait_ge(unit_evac, u - 3)
                    pe.wait_ge(ol_ready, 8)
                    out_part(u, range(0, 4), OH, OL, True, False)
                scores(k)
                if k >= 2:
                    turn_probs(k - 2)
                if k >= 3:
                    values(k - 3)
            pe.wait_ge(ol_ready, 12)
            out_part(A_O, range(4, 6), OH, OL, False, False)
            turn_probs(14)
            values(13)
            out_part(A_O + 1, range(4, 6), OH, OL, False, False)
            turn_probs(15)
            values(14)
            out_part(A_O + 2, range(4, 6), OH, OL, False, False)
            values(15)
            out_part(A_O + 3, range(4, 6), OH, OL, False, False)
            pe.wait_ge(ol_ready, 16)
            for u in range(A_O, A_O + 4):
                out_part(u, range(6, 8), OH, OL, False, True).then_inc(unit_done, 1)
            unit(A_O + 4, 0, OH, OL, wh=fifth[A_O + 4][1], wl=fifth[A_O + 4][2])
            for u in range(A_O + 5, A_O + 8):
                unit(u, u % 4, OH, OL)

            up_phase(0, 1)
            down_phase(0)

            pe.wait_ge(gal_ready, 1)
            for kb in range(KT_D):
                pe.wait_ge(xl_ready, 2 * KT_D + kb + 1)
                for x in (XH, XL):
                    last = mm(PS[:, B5], GA[:, kb], x[:, kb], start=kb == 0 and x is XH,
                              stop=kb == KT_D - 1 and x is XL)
            last.then_inc(ga_done, 1)
            mean_square(2)

            def gate_logits(t):
                if t == 0:
                    pe.wait_ge(ga_ready, 1)
                if t >= 2:
                    pe.wait_ge(gk_ready, t - 1)
                mm(PS[:, B6 + t % 2], GAT[0:LO + RANK, t * P:(t + 1) * P], WG[0:LO + RANK, :],
                   start=True, stop=True).then_inc(z_done, 1)

            def cumulate(h):
                pe.wait_ge(gk_ready, 4)
                if h >= 2:
                    pe.wait_ge(e_ready, h - 1)
                for t in range(4):
                    last = mm(PS[:, B6 + h % 2, t * P:(t + 1) * P], GK[:, t, h * HK:(h + 1) * HK], CAUSAL[:],
                              start=True, stop=True)
                last.then_inc(cum_done, 1)

            def turn_values(j):
                pe.wait_ge(unit_evac, B_V + j + 1)
                if j == 0:
                    pe.wait_ge(std_ready, 3)
                if j == 1:
                    pe.wait_ge(ga_ready, 1)
                if j >= 2:
                    pe.wait_ge(vv_ready, j - 1)
                for t in range(4):
                    last = nc.tensor.transpose(PS[:, B4 + j % 2, t * P:(t + 1) * P],
                                               VTT[:, j % 2, t * P:(t + 1) * P], IDENT[:])
                last.then_inc(vtt_done, 1)

            for j in range(16):
                unit(B_V + j, j % 4, XH, XL)
                if 1 <= j <= 2:
                    gate_logits(2 * j - 2)
                    gate_logits(2 * j - 1)
                if j in (4, 6):
                    cumulate(j - 4)
                    cumulate(j - 3)
                if 2 <= j <= 9:
                    turn_values(j - 2)

            def head_scores(h):
                pe.wait_ge(kd_ready, h + 1)
                pe.wait_ge(ku_ready, h + 1)
                if h == 0:
                    pe.wait_ge(vv_ready, 8)
                if h >= 2:
                    pe.wait_ge(hstd_ready, h - 1)
                for p in range(4):
                    c = slice(p * P, (p + 1) * P)
                    mm(PS[:, B4, c], EN[:, h, c], EP[:, h, c], start=True, stop=True)
                    first, second = slice(p * P, p * P + CHUNK), slice(p * P + CHUNK, (p + 1) * P)
                    last = mm(PS[0:CHUNK, B4, second], EU[:, h, first], EP[:, h, second], start=True, stop=True)
                last.then_inc(a_done, 1)

            def head_keys(h):
                pe.wait_ge(carried, 2 * h + 1)
                for p in range(4):
                    c = slice(p * P, (p + 1) * P)
                    last = nc.tensor.transpose(PS[:, B5, c], EU[:, h, c], IDENT[:])
                last.then_inc(kut_done, 1)

            def state_updates(h):
                pe.wait_ge(kut_ready, h + 1)
                if h == 0:
                    pe.wait_ge(e_ready, 4)
                for p in range(3):
                    mm(PS[:, B6 + p // 2, (p % 2) * HV:(p % 2 + 1) * HV], KUT[:, p],
                       VV[:, p, h * HV:(h + 1) * HV], start=True, stop=True).then_inc(u_done, 1)

            def outputs(h):
                pe.wait_ge(am_ready, h + 1)
                pe.wait_ge(st_ready, 3 * (h + 1))
                pe.wait_ge(carried, 2 * h + 2)
                for vt in range(2):
                    v0 = h * HV + vt * P
                    if h >= 1:
                        pe.wait_ge(o_ready, 2 * (h - 1) + vt + 1)
                    for p in range(4):
                        c = slice(p * P, (p + 1) * P)
                        last = mm(PS[:, 2 + vt, c], VV[:, p, v0:v0 + P], AM[:, h % 2, p], start=True, stop=p == 0)
                        if p:
                            last = mm(PS[:, 2 + vt, c], S[:, p, vt * P:(vt + 1) * P], EP[:, h, c],
                                      start=False, stop=True)
                    last.then_inc(o_done, 1)

            def head_square(h):
                pe.wait_ge(hsum_ready, h + 1)
                if h < 3:
                    pe.wait_ge(am_ready, h + 2)
                mm(PS[:, B4], ONES[:], SQ[:, 0], start=True, stop=True).then_inc(hms_done, 1)

            for h in range(BH):
                head_scores(h)
                u = B_G + 2 * h
                if h == 0:
                    pe.wait_ge(unit_evac, B_G)
                unit(u, u % 4, XH, XL, bank=0, banks=2)
                head_keys(h)
                if h >= 1:
                    head_square(h - 1)
                pe.wait_ge(lo_ready, u + 2)
                pe.wait_ge(unit_evac, u)
                product((u + 1) % 4, 1, XH, XL, range(0, 4), 0, stop=False)
                state_updates(h)
                product((u + 1) % 4, 1, XH, XL, range(4, 8), 4, start=False).then_inc(unit_done, 1)
                outputs(h)
            for u in range(B_O, B_O + 4):
                pe.wait_ge(lo_ready, u + 1)
                if u == B_O:
                    pe.wait_ge(unit_evac, B_O)
                if u == B_O + 2:
                    head_square(3)
                    pe.wait_ge(o_ready, 8)
                pe.wait_ge(yl_ready, 4)
                out_part(u, range(0, 4), YH, YL, True, False)
            for u in range(B_O, B_O + 4):
                pe.wait_ge(yl_ready, 6)
                out_part(u, range(4, 6), YH, YL, False, False)
            for u in range(B_O, B_O + 4):
                pe.wait_ge(yl_ready, 8)
                out_part(u, range(6, 8), YH, YL, False, True).then_inc(unit_done, 1)
            unit(B_O + 4, 0, YH, YL, wh=fifth[B_O + 4][1], wl=fifth[B_O + 4][2])
            for u in range(B_O + 5, B_O + 8):
                unit(u, u % 4, YH, YL)

            up_phase(1, 3)
            down_phase(1)
            for s in range(2):
                down_unit(DOWN1 + 12 + s, s, s).then_inc(unit_done, 1)

            def last_tile(half, kbs):
                for kb in kbs:
                    s, c = 2 + kb // HALF, kb % HALF * P
                    for w, x in ((WH, AH), (WH, AL), (WL, AH)):
                        last = mm(PS[:, END_BANKS[half][0], 0:TH], w[:, s, c:c + P], x[:, kb, half * TH:(half + 1) * TH],
                                  start=kb == 0 and w is WH and x is AH, stop=kb == FT - 1 and w is WL)
                return last

            def sums(half):
                pe.wait_ge(ss_ready, KT_D * 5 - 1)
                pe.wait_ge(last_sq_ready, half + 1)
                for j in range(2):
                    tokens = slice((2 * half + j) * P, (2 * half + j + 1) * P)
                    for squares in (SS, SQ[:, 1]):
                        last = mm(PS[:, END_BANKS[half][1], j:j + 1], squares[:, tokens], ONES[:, 0:1],
                                  start=squares is SS, stop=squares is not SS)
                last.then_inc(ms_done, 1)

            def spread(half):
                for j in range(2):
                    t = 2 * half + j
                    pe.wait_ge(diag_ready, t + 1)
                    last = mm(PS[:, END_BANKS[half][2], j * P:(j + 1) * P], ONES[:], STD[:, t * P:(t + 1) * P],
                              start=True, stop=True)
                last.then_inc(r_spread, 1)

            pe.wait_ge(lo_ready, DOWN1 + 16)
            last_tile(0, range(FT)).then_inc(last_done, 1)
            last_tile(1, range(0, 5))
            sums(0)
            last_tile(1, range(5, 10))
            spread(0)
            last_tile(1, range(10, FT)).then_inc(last_done, 1)
            sums(1)
            spread(1)

        @block.scalar
        def _(act):
            A = nc.scalar.activation

            def hi(u, s, turn, k):
                act.wait_ge(raw_landed[s], 16 * turn + 16)
                nc.scalar.copy(WH[:, s, 0:k * P], WRAW[:, s, 0:k * P]).then_inc(hi_ready, 1)

            def hi_unit(u):
                if u in fifth:
                    act.wait_ge(raw_landed[0], 16 * (u // 4) + 16)
                    nc.scalar.copy(fifth[u][1][:], fifth[u][0][:]).then_inc(hi_ready, 1)
                else:
                    hi(u, u % 4, u // 4, ksize(u))

            def after_wait(m):
                return slice(m, m + 1) if isinstance(m, int) else bass.ds(act.snap(m), 1)

            def x_hi(st, m):
                A(XH[:, m:m + 1, :], X[:, m:m + 1, :], ACT.Copy, scale=GAIN[:, st, m:m + 1]).then_inc(xh_ready, 1)

            def x_square(st, m):
                if KT_D * st + m >= 2:
                    act.wait_ge(ss_ready, m + (KT_D * st - 1))
                A(SQ[:, m % 2], X[:, m], ACT.Square).then_inc(sq_ready, 1)

            def x_tile(st, m, m_even=None):
                par = m % 2 if m_even is None else m_even
                if not isinstance(m, int) or KT_D * st + m >= 2:
                    act.wait_ge(ss_ready, m + (KT_D * st - 1))
                tile = after_wait(m)
                if st < 4:
                    A(XH[:, tile, :], X[:, tile, :], ACT.Copy, scale=GAIN[:, st, tile]).then_inc(xh_ready, 1)
                A(SQ[:, par:par + 1, :], X[:, tile, :], ACT.Square).then_inc(sq_ready, 1)

            def std(st):
                act.wait_ge(ms_done, st + 1)
                A(STD[:], PS[:, B4], ACT.Sqrt, bias=EPSC[:], scale=1.0 / D).then_inc(std_ready, 1)

            def ffn_step(layer, m, par, before=None, after=None):
                u, f = UP[layer] + 2 * m, FT * layer + m
                act.wait_ge(unit_evac, u + 1)
                tile = after_wait(m)
                A(CV[:, par], GS[:, par, 2:T + 2], ACT.Identity, bias=CONVB[:, layer, tile],
                  scale=CONVW[:, layer, tile, 2]).then_inc(c0_ready, 1)
                if after:
                    after()
                act.wait_ge(conv_ready, f + 1)
                A(CV[:, par], CV[:, par], ACT.Silu).then_inc(silu_ready, 1)
                act.wait_ge(unit_evac, u + 2)
                tile = after_wait(m)
                nc.scalar.copy(AH[:, tile, :], AC[:, par:par + 1, :]).then_inc(ah_ready, 1)

            def ffn(layer, st):
                u0, d0 = UP[layer], DOWN[layer]
                for j in range(2):
                    act.wait_ge(unit_evac, u0 - 1 + j)
                    x_tile(st, 6 + j)
                    hi_unit(u0 + 2 + j)
                std(st)
                with act.Fori(1, FT - 1, 2) as i:
                    for j in range(2):
                        s, landed = 2 * j, 8 * i + (4 * u0 + 24)
                        act.wait_ge(raw_landed[s], landed)
                        nc.scalar.copy(WH[:, s, 0:D], WRAW[:, s, 0:D]).then_inc(hi_ready, 1)

                        def second(s=s, landed=landed):
                            act.wait_ge(raw_landed[s + 1], landed)
                            nc.scalar.copy(WH[:, s + 1, 0:D], WRAW[:, s + 1, 0:D]).then_inc(hi_ready, 1)
                        ffn_step(layer, i + (j - 1), j, after=second)
                hi_unit(d0)
                ffn_step(layer, FT - 2, 0, after=lambda: hi_unit(d0 + 1))
                hi_unit(d0 + 2)
                ffn_step(layer, FT - 1, 1, after=lambda: hi_unit(d0 + 3))
                with act.Fori(1, KT_D - 1, 2) as i:
                    for j in range(2):
                        s, landed = 2 * j, 8 * i + (4 * d0 + 24)
                        act.wait_ge(raw_landed[s], landed)
                        nc.scalar.copy(WH[:, s], WRAW[:, s]).then_inc(hi_ready, 1)
                        act.wait_ge(unit_evac, 2 * i + (d0 + 2 * j))
                        x_tile(st + 1, i + (j - 1), j)
                        act.wait_ge(raw_landed[s + 1], landed)
                        nc.scalar.copy(WH[:, s + 1], WRAW[:, s + 1]).then_inc(hi_ready, 1)
                if d0 + 16 < DOWN1:
                    hi_unit(d0 + 16)
                act.wait_ge(unit_evac, d0 + 14)
                x_tile(st + 1, 6)
                if d0 + 16 < DOWN1:
                    hi_unit(d0 + 17)
                    hi_unit(d0 + 18)
                if st + 1 < 4:
                    act.wait_ge(unit_evac, d0 + 16)
                    x_tile(st + 1, 7)

            act.dma_start(GAIN[:], gains).then_inc(gain_landed, 16)
            act.dma_start(RB[0:32, :], rel_bias).then_inc(rel_landed, 16)
            act.dma_start(HOT[0:32, :], onehot).then_inc(rel_landed, 16)
            act.wait_ge(eps_set, 1)
            nc.scalar.copy(WARM[:, 0:1], EPSC[:])
            act.wait_ge(first_landed, 16)
            nc.scalar.copy(WH[:, 0, 0:D // 2], WRAW[:, 0, 0:D // 2]).then_inc(first_hi, 1)
            act.wait_ge(gain_landed, 16)
            for m in range(KT_D):
                if m % 2 == 0:
                    act.wait_ge(x_landed[m // 2], 16)
                x_hi(0, m)
                if m == 1:
                    act.wait_ge(raw_landed[0], 16)
                    nc.scalar.copy(WH[:, 0, D // 2:D], WRAW[:, 0, D // 2:D]).then_inc(hi_ready, 1)
                if m in (3, 5):
                    x_square(0, (m - 3) // 2)
            hi_unit(1)
            for m in range(2, KT_D):
                x_square(0, m)
                if m == 3:
                    hi_unit(2)
                if m == 6:
                    hi_unit(3)
                if m == 5:
                    act.wait_ge(tb_done, 1)
                    nc.scalar.copy(TB[0:A_HEADS, :], PS[0:A_HEADS, B5, 0:REL]).then_inc(tb_ready, 1)
                    act.wait_ge(tb_ready, 1)
                    act.dma_start(bias_rows.rearrange("h (q r) -> h q r", q=64),
                                  TB[0:A_HEADS, :].rearrange("h (o r) -> h o r", o=1).to_broadcast([A_HEADS, 64, REL]))\
                       .then_inc(rows_out, 16)
            std(0)
            hi_unit(4)
            hi_unit(5)
            act.wait_ge(small_set, 1)
            for dst, src in ((IDENT[:], ident), (CAUSAL[:], causal), (CAUSAL2[:], causal_pair),
                             (SINK[:], sinks), (CONVW[:], conv_w),
                             (CONVB[:], conv_b), (BNORM[:], b_norm), (WG[0:RANK, :], w_gate[0:RANK]),
                             (WG[RANK:RANK + 1, :], w_gate[RANK:RANK + 1]),
                             (WG[LO:LO + RANK, :], w_gate[0:RANK]), (GARAW[:], w_ga)):
                act.dma_start(dst, src).then_inc(consts, 16)
            act.wait_ge(rows_out, 16)
            for hh in range(2):
                for half in range(2):
                    rows = slice(64 * hh, 64 * hh + 64)
                    act.dma_start(BIAS[rows, :, 2 + half],
                                  bass.AP(tensor=bias_rows.tensor,
                                          offset=bias_rows.offset + (2 * hh + half) * 64 * REL + 63,
                                          ap=[[REL - 1, 64], [4 * 64 * REL, KV], [1, P]])).then_inc(bias_in, 16)
            for g in range(KV):
                if g % 2 == 0:
                    act.wait_ge(unit_evac, g // 2 + 1)
                here, there = slice(64 * (g % 2), 64 * (g % 2) + 64), slice(64 - 64 * (g % 2), 128 - 64 * (g % 2))
                act.dma_start(KT[there, g, 1 - g % 2], KT[here, g, g % 2]).then_inc(k_dup, 16)
            hi_unit(6)
            act.wait_ge(vt_done, 1)
            for bank, tiles in ((B5, V[:, 0, 0:2]), (B6, V[:, 0, 2:4]), (B7, V[:, 1, 1:3]), (B4, V[:, 1, 3:4])):
                n = 2 if bank != B4 else 1
                nc.scalar.copy(tiles, PS[:, bank, 0:2 * P * n].rearrange("p (t f) -> p t f", t=n)).then_inc(v_copied, 1)
            hi_unit(7)

            def softmax_exp(k):
                act.wait_ge(max_ready, k + 1)
                if k >= 2:
                    act.wait_ge(pt_done, k - 1)
                for i in range(4):
                    A(PB[:, k % 2, i], SB[:, k % 2, i], ACT.Exp, bias=NM[:, k % 2, i:i + 1],
                      accum_out=SUM[:, k % 2, i:i + 1])
                A(ES[:, k % 2], SM[:, k % 2], ACT.Exp).then_inc(exp_done, 1)

            def probs_copy(k):
                act.wait_ge(pt_done, k + 1)
                if k >= 2:
                    act.wait_ge(pv_done, k - 1)
                nc.scalar.copy(PT[:, k % 2], PS[:, B6].rearrange("p (i c) -> p i c", i=4)).then_inc(pt_ready, 1)

            def o_view(k):
                return PS[:, B7, 0:2 * P].rearrange("p (j a q) -> p a j q", j=2, a=2)

            def o_tiles(t, k):
                g, p = divmod(k, 4)
                return t[:, 2 * g:2 * g + 2, p * P:(p + 1) * P].rearrange("p a (j q) -> p a j q", j=2)

            def o_hi(k):
                act.wait_ge(pv_done, k + 1)
                nc.scalar.copy(o_tiles(OH, k), o_view(k)).then_inc(oh_ready, 1)

            for k in range(16):
                g, p = divmod(k, 4)
                if k >= 2:
                    probs_copy(k - 2)
                if k >= 3:
                    o_hi(k - 3)
                softmax_exp(k)
                if k % 2 == 0 and k <= 8:
                    hi_unit(8 + k // 2)
                elif 9 <= k <= 12 and k != 10:
                    hi_unit(k + 3 if k > 9 else 13)
                elif k == 14:
                    hi_unit(A_O + 4)
            for k in range(14, 16):
                probs_copy(k)
                o_hi(k - 1)
            o_hi(15)
            for m in range(6):
                act.wait_ge(unit_evac, A_O + m + 1)
                x_tile(1, m)
                if m >= 1:
                    hi_unit(A_O + 4 + m)
            ffn(0, 1)

            std(2)

            def decays(h):
                act.wait_ge(cum_done, h + 1)
                nc.scalar.copy(EU[:, h], PS[:, B6 + h % 2]).then_inc(c_copied, 1)
                A(EP[:, h], PS[:, B6 + h % 2], ACT.Exp, scale=1.0 / GATE_NORM)
                A(EN[:, h], PS[:, B6 + h % 2], ACT.Exp, scale=-1.0 / GATE_NORM).then_inc(e_ready, 1)
                act.wait_ge(d_ready, h + 1)
                A(EU[:, h], EU[:, h], ACT.Exp, scale=1.0 / GATE_NORM)
                A(DEC[:, h], CL[:, h], ACT.Exp, scale=1.0 / GATE_NORM).then_inc(ln_ready, 1)

            def values_copy(j):
                act.wait_ge(vtt_done, j + 1)
                nc.scalar.copy(VV[:, :, j * P:(j + 1) * P], PS[:, B4 + j % 2].rearrange("p (t f) -> p t f", t=4))\
                   .then_inc(vv_ready, 1)

            def gates(t0):
                for t in (t0, t0 + 1):
                    act.wait_ge(z_done, t + 1)
                    A(GT[:, t, 0], PS[:, B6 + t % 2], ACT.Abs).then_inc(act_step, 1)
                for t in (t0, t0 + 1):
                    act.wait_ge(act_step, 3 * t0 + 2)
                    A(GT[:, t, 0], GT[:, t, 0], ACT.Exp, scale=-1.0).then_inc(act_step, 1)
                for t in (t0, t0 + 1):
                    act.wait_ge(act_step, 3 * t0 + 4)
                    A(GT[:, t, 1], GT[:, t, 0], ACT.Ln, bias=1.0).then_inc(act_step, 1)

            for j in range(16):
                hi_unit(B_V + j + 3)
                if 1 <= j <= 2:
                    gates(2 * j - 2)
                if j in (4, 6):
                    decays(j - 4)
                    decays(j - 3)
                if 2 <= j <= 9:
                    values_copy(j - 2)

            def head_keys(h):
                act.wait_ge(kut_done, h + 1)
                nc.scalar.copy(KUT[:], PS[:, B5].rearrange("p (i c) -> p i c", i=4)).then_inc(kut_ready, 1)

            def head_outputs(h):
                for vt, o in ((0, EN), (1, EU)):
                    act.wait_ge(o_done, 2 * h + vt + 1)
                    nc.scalar.copy(o[:, h], PS[:, 2 + vt]).then_inc(act_step, 1)
                    if h >= 1 and vt == 0:
                        act.wait_ge(hms_done, h)
                    A(SQ[:, vt], PS[:, 2 + vt], ACT.Square).then_inc(o_ready, 1)

            def head_std(h):
                act.wait_ge(hms_done, h + 1)
                if h >= 1:
                    act.wait_ge(y_ready, 2 * h)
                A(STD[:], PS[:, B4], ACT.Sqrt, bias=EPSC[:], scale=1.0 / HV).then_inc(hstd_ready, 1)

            def silu(j):
                act.wait_ge(unit_evac, B_G + j + 1)
                A(SG[:, j], SG[:, j], ACT.Silu).then_inc(sg_ready, 1)

            def head_hi(h):
                for vt in range(2):
                    act.wait_ge(y_ready, 2 * h + vt + 1)
                    nc.scalar.copy(YH[:, 2 * h + vt], (EN if vt == 0 else EU)[:, h]).then_inc(yh_ready, 1)

            for h in range(BH):
                u = B_G + 2 * h
                hi_unit(u + 3)
                if h >= 2:
                    head_hi(h - 2)
                silu(2 * h)
                head_keys(h)
                if h >= 1:
                    head_std(h - 1)
                hi_unit(u + 4)
                silu(2 * h + 1)
                head_outputs(h)
            head_hi(2)
            hi_unit(B_O + 3)
            head_std(3)
            head_hi(3)
            hi_unit(B_O + 4)
            for m in range(6):
                act.wait_ge(unit_evac, B_O + m + 1)
                x_tile(3, m)
                if m >= 1:
                    hi_unit(B_O + 4 + m)
            ffn(1, 3)
            A(WARM[:, 1:2], EPSC[:], ACT.Sqrt)
            last = KT_D - 1
            for m in range(DVE_TILES, last):
                A(X[:, m], X[:, m], ACT.Copy, scale=GAIN[:, 4, m:m + 1]).then_inc(gained, 1)
            for half in range(2):
                tokens = slice(half * TH, (half + 1) * TH)
                act.wait_ge(last_sq_ready, half + 1)
                A(X[:, last, tokens], X[:, last, tokens], ACT.Copy, scale=GAIN[:, 4, last:last + 1]).then_inc(gained, 1)
                act.wait_ge(ms_done, 5 + half)
                A(RMS[:, 2 * half:2 * half + 2], PS[:, END_BANKS[half][1], 0:2], ACT.Sqrt, bias=EPSC[:],
                  scale=1.0 / D).then_inc(std_ready, 1)

        @block.vector
        def _(dve):
            tt, stt, ts = nc.vector.tensor_tensor, nc.vector.scalar_tensor_tensor, nc.vector.tensor_scalar
            steps = [0]

            def link(instruction):
                steps[0] += 1
                instruction.then_inc(dve_step, 1)
                dve.wait_ge(dve_step, steps[0])

            def lo(u, s, k):
                dve.wait_ge(hi_ready, u + 1)
                tt(WL[:, s, 0:k * P], WRAW[:, s, 0:k * P], WH[:, s, 0:k * P].bitcast(F32), ALU.subtract)\
                    .then_inc(lo_ready, 1)

            def lo_unit(u):
                if u in fifth:
                    raw, high, low = fifth[u]
                    dve.wait_ge(hi_ready, u + 1)
                    tt(low[:], raw[:], high[:].bitcast(F32), ALU.subtract).then_inc(lo_ready, 1)
                else:
                    lo(u, u % 4, ksize(u))

            def tile_of(m):
                return slice(m, m + 1) if isinstance(m, int) else bass.ds(m, 1)

            def x_lo(st, m):
                tile = tile_of(m)
                dve.wait_ge(xh_ready, m + (KT_D * st + 1))
                stt(XL[:, tile, :], X[:, tile, :], GAIN[:, st, tile], XH[:, tile, :].bitcast(F32),
                    ALU.mult, ALU.subtract).then_inc(xl_ready, 1)

            def x_add(u_last, m, bank, n=1):
                tile = tile_of(m)
                dve.wait_ge(unit_done, u_last + 1)
                tt(X[:, tile, :], PS[:, bank:bank + 1], X[:, tile, :], ALU.add).then_inc(unit_evac, n)

            def inverse_rms(st):
                dve.wait_ge(std_ready, st + 1)
                nc.vector.reciprocal(R[:], STD[:]).then_inc(r_ready, 1)
                dve.wait_ge(r_ready, st + 1)

            def ffn_step(layer, m, par, mid=None, after=None):
                u, f = UP[layer] + 2 * m, FT * layer + m
                tile = tile_of(m)
                gate, up = (0, 1) if par == 0 else (2, 3)
                dve.wait_ge(unit_done, u + 1)
                tt(GS[:, par, 2:T + 2], PS[:, gate], R[:], ALU.mult).then_inc(unit_evac, 1)
                if mid:
                    mid()
                dve.wait_ge(c0_ready, f + 1)
                stt(CV[:, par], GS[:, par, 1:T + 1], CONVW[:, layer, tile, 1], CV[:, par], ALU.mult, ALU.add)\
                    .then_inc(c1_ready, 1)
                dve.wait_ge(c1_ready, f + 1)
                stt(CV[:, par], GS[:, par, 0:T], CONVW[:, layer, tile, 0], CV[:, par], ALU.mult, ALU.add)\
                    .then_inc(conv_ready, 1)
                if after:
                    after()
                dve.wait_ge(unit_done, u + 2)
                dve.wait_ge(slr_ready, f + 1)
                tt(AC[:, par], PS[:, up], CV[:, par], ALU.mult).then_inc(unit_evac, 1)
                dve.wait_ge(ah_ready, f + 1)
                tt(AL[:, tile, :], AC[:, par:par + 1, :], AH[:, tile, :].bitcast(F32), ALU.subtract).then_inc(al_ready, 1)

            def ffn(layer, st):
                u0, d0 = UP[layer], DOWN[layer]
                for j in range(2):
                    x_add(u0 - 2 + j, 6 + j, 2 + j)
                    x_lo(st, 6 + j)
                    lo_unit(u0 + 2 + j)
                nc.vector.memset(GS[:, :, 0:2], 0.0)
                inverse_rms(st)
                with dve.Fori(1, FT - 1, 2) as i:
                    for j in range(2):
                        s = 2 * j
                        ffn_step(layer, i + (j - 1), j,
                                 mid=lambda: lo(2 * i + (u0 + 2 * j + 2), s, KT_D),
                                 after=lambda: lo(2 * i + (u0 + 2 * j + 3), s + 1, KT_D))
                ffn_step(layer, FT - 2, 0, mid=lambda: lo_unit(d0), after=lambda: lo_unit(d0 + 1))
                ffn_step(layer, FT - 1, 1, mid=lambda: lo_unit(d0 + 2), after=lambda: lo_unit(d0 + 3))
                with dve.Fori(1, KT_D - 1, 2) as i:
                    for j in range(2):
                        s = 2 * j
                        lo(2 * i + (d0 + 2 * j + 2), s, HALF)
                        x_add(2 * i + (d0 + 2 * j - 1), i + (j - 1), 2 * j, 2)
                        if st + 1 < 4:
                            x_lo(st + 1, i + (j - 1))
                        lo(2 * i + (d0 + 2 * j + 3), s + 1, HALF)
                for m in (6, 7) if st + 1 < 4 else (6,):
                    if m == 6 and st + 1 < 4:
                        lo_unit(d0 + 16)
                    x_add(d0 + 2 * m + 1, m, 2 * (m % 2), 2)
                    if st + 1 < 4:
                        x_lo(st + 1, m)
                        lo_unit(d0 + 17 + (m - 6))

            first = slice(0, D // 2)
            dve.wait_ge(first_hi, 1)
            tt(WL[:, 0, first], WRAW[:, 0, first], WH[:, 0, first].bitcast(F32), ALU.subtract).then_inc(first_lo, 1)
            dve.wait_ge(gain_landed, 16)
            for m in range(KT_D):
                if m % 2 == 0:
                    dve.wait_ge(x_landed[m // 2], 16)
                x_lo(0, m)
                if m == 1:
                    rest = slice(D // 2, D)
                    dve.wait_ge(hi_ready, 1)
                    tt(WL[:, 0, rest], WRAW[:, 0, rest], WH[:, 0, rest].bitcast(F32), ALU.subtract).then_inc(lo_ready, 1)
            for u in range(1, 4):
                lo_unit(u)
            inverse_rms(0)

            for t in range(2):
                dve.wait_ge(unit_done, A_K + t + 1)
                for half in range(2):
                    rows = slice(64 * half, 64 * half + 64)
                    last = tt(KT[rows, 2 * t + half, half], PS[rows, t], R[rows], ALU.mult)
                last.then_inc(unit_evac, 1)
                if t:
                    lo_unit(4)
            for t in range(2):
                dve.wait_ge(unit_done, A_V + t + 1)
                tt(VT[:, t], PS[:, 2 + t], R[:], ALU.mult).then_inc(unit_evac, 1)
                lo_unit(5 + t)

            def queries(u):
                dve.wait_ge(unit_done, u + 1)
                by_chunk = lambda t: t.rearrange("p (c q) -> p c q", q=CHUNK)
                a = CHUNK * (u % 2)
                tt(QT[:, (u - A_Q) // 2 % 2, :, a:a + CHUNK], by_chunk(PS[:, u % 4]), by_chunk(R[:]), ALU.mult)\
                    .then_inc(unit_evac, 1)

            dve.wait_ge(consts, 16 * CONSTS)
            queries(A_Q)
            lo_unit(7)
            queries(A_Q + 1)

            def softmax_max(k):
                g, p = divmod(k, 4)
                if k == 0:
                    dve.wait_ge(bias_ready, 2)
                dve.wait_ge(scores_done, k + 1)
                b = k % 2
                items = lambda t: t.rearrange("p (j x) -> p j x", j=2)
                bias = BIAS[:, g].rearrange("p i c -> p (i c)")
                bias = items(bias) if p == 0 else bias[:, 2 * P:].unsqueeze(1).to_broadcast([P, 2, 2 * P])
                stt(items(SB[:, b].rearrange("p i c -> p (i c)")), items(PS[:, B4 + b]), A_SCALE, bias,
                    ALU.mult, ALU.add).then_inc(s_ready, 1)
                dve.wait_ge(s_ready, k + 1)
                link(nc.vector.tensor_reduce(MX[:, b], SB[:, b], AX.X, ALU.max))
                sink = SINK[:, g:g + 1, :].to_broadcast([P, 2, 2])
                two = lambda t: t[:, b].rearrange("p (j h) -> p j h", j=2)
                link(tt(two(MX), two(MX), sink, ALU.max))
                tt(two(SM), sink, two(MX), ALU.subtract)
                ts(NM[:, b], MX[:, b], -1.0, None, ALU.mult).then_inc(max_ready, 1)

            def softmax_divide(k):
                b = k % 2
                dve.wait_ge(exp_done, k + 1)
                link(tt(RD[:, b], SUM[:, b], ES[:, b], ALU.add))
                link(nc.vector.reciprocal(RD[:, b], RD[:, b]))
                tt(PB[:, b], PB[:, b], RD[:, b].unsqueeze(2).to_broadcast([P, 4, P]), ALU.mult).then_inc(p_ready, 1)

            def o_lo(k):
                g, p = divmod(k, 4)
                dve.wait_ge(oh_ready, k + 1)
                view = lambda t: t[:, 2 * g:2 * g + 2, p * P:(p + 1) * P].rearrange("p a (j q) -> p a j q", j=2)
                tt(view(OL), PS[:, B7, 0:2 * P].rearrange("p (j a q) -> p a j q", j=2, a=2), view(OH).bitcast(F32),
                   ALU.subtract).then_inc(ol_ready, 1)

            for k in range(16):
                g, p = divmod(k, 4)
                softmax_max(k)
                if g < 3 and k % 2 == 1:
                    queries(A_Q + 2 + k // 2)
                if k >= 3:
                    o_lo(k - 3)
                if k % 2 == 0 and 2 <= k <= 10:
                    lo_unit(7 + k // 2)
                elif 11 <= k <= 13:
                    lo_unit(k + 2)
                if k >= 1:
                    softmax_divide(k - 1)
            softmax_divide(15)
            o_lo(13)
            lo_unit(A_O + 4)
            o_lo(14)
            o_lo(15)
            for m in range(6):
                x_add(A_O + m, m, m % 4)
                x_lo(1, m)
                if m >= 1:
                    lo_unit(A_O + 4 + m)
            ffn(0, 1)

            inverse_rms(2)
            dve.wait_ge(ga_done, 1)
            dve.wait_ge(small_set, 3)
            for first in (0, LO):
                rows = slice(first, first + RANK)
                last = tt(GAT[rows, :], PS[rows, B5], R[rows], ALU.mult)
            last.then_inc(ga_ready, 1)

            def log_gates(t):
                dve.wait_ge(act_step, 3 * (t - t % 2) + t % 2 + 5)
                stt(GK[:, t], PS[:, B6 + t % 2], 0.0, GT[:, t, 1], ALU.min, ALU.subtract).then_inc(gk_ready, 1)

            def by_pair(decays):
                pairs = decays.rearrange("p (c j) -> p c j", j=2)
                return pairs[:, :, 0], pairs[:, :, 1]

            def to_last(h):
                dve.wait_ge(c_copied, h + 1)
                chunks = EU[:, h].rearrange("p (c t) -> p c t", t=CHUNK)
                link(nc.vector.tensor_copy(CL[:, h], chunks[:, :, CHUNK - 1]))
                tt(chunks, CL[:, h].unsqueeze(2).to_broadcast([P, NCH, CHUNK]), chunks, ALU.subtract).then_inc(d_ready, 1)

            for j in range(16):
                u = B_V + j
                dve.wait_ge(unit_done, u + 1)
                if j < 8:
                    if j >= 2:
                        dve.wait_ge(vtt_done, j - 1)
                    tt(VTT[:, j % 2], PS[:, j % 4], R[:], ALU.mult).then_inc(unit_evac, 1)
                elif j < 12:
                    h = j - 8
                    dve.wait_ge(epr_ready, h + 1)
                    stt(EP[:, h], PS[:, j % 4], B_SCALE, EP[:, h], ALU.mult, ALU.mult).then_inc(unit_evac, 1)
                else:
                    h = j - 12
                    if h >= 2:
                        dve.wait_ge(ku_ready, h - 1)
                    tt(KS[:, h % 2], PS[:, j % 4], R[:], ALU.mult).then_inc(unit_evac, 1)
                    dve.wait_ge(unit_evac, u + 1)
                    dve.wait_ge(ln_ready, h + 1)
                    tt(EN[:, h], KS[:, h % 2], EN[:, h], ALU.mult).then_inc(kd_ready, 1)
                    link(tt(DEC2[:, h], *by_pair(DEC[:, h]), ALU.mult))
                lo_unit(u + 3)
                if 1 <= j <= 2:
                    log_gates(2 * j - 2)
                    log_gates(2 * j - 1)
                if j in (4, 6):
                    to_last(j - 4)
                    to_last(j - 3)

            def mask(h):
                if h == 0:
                    dve.wait_ge(am_zero, 1)
                dve.wait_ge(a_done, h + 1)
                nc.vector.copy_predicated(AM[:, h % 2], CAUSAL2[:].bitcast(U32).unsqueeze(1).to_broadcast([P, 4, P]),
                                          PS[:, B4].rearrange("p (i c) -> p i c", i=4)).then_inc(am_ready, 1)

            def states(h):
                for p in range(3):
                    dve.wait_ge(u_done, 3 * h + max(p, 1) + 1)
                    u = PS[:, B6 + p // 2, (p % 2) * HV:(p % 2 + 1) * HV]
                    if p == 0:
                        nc.vector.tensor_copy(S[:, 1], u).then_inc(st_ready, 1)
                    else:
                        dve.wait_ge(st_ready, 3 * h + p)
                        stt(S[:, p + 1], S[:, p], DEC2[:, h, p:p + 1], u, ALU.mult, ALU.add).then_inc(st_ready, 1)

            def head_norm(h):
                dve.wait_ge(hstd_ready, h + 1)
                link(nc.vector.reciprocal(STD[:], STD[:]))
                for vt, o in ((0, EN), (1, EU)):
                    link(stt(o[:, h], o[:, h], BNORM[:, vt:vt + 1], STD[:], ALU.mult, ALU.mult))
                    dve.wait_ge(sg_ready, 2 * h + vt + 1)
                    tt(o[:, h], o[:, h], SG[:, 2 * h + vt], ALU.mult).then_inc(y_ready, 1)

            def head_lo(h):
                for vt, o in ((0, EN), (1, EU)):
                    dve.wait_ge(yh_ready, 2 * h + vt + 1)
                    tt(YL[:, 2 * h + vt], o[:, h], YH[:, 2 * h + vt].bitcast(F32), ALU.subtract).then_inc(yl_ready, 1)

            for h in range(BH):
                u = B_G + 2 * h
                mask(h)
                lo_unit(u + 3)
                if h >= 2:
                    head_lo(h - 2)
                dve.wait_ge(unit_done, u + 1)
                tt(SG[:, 2 * h], PS[:, 0], R[:], ALU.mult).then_inc(unit_evac, 1)
                states(h)
                dve.wait_ge(unit_done, u + 2)
                tt(SG[:, 2 * h + 1], PS[:, 1], R[:], ALU.mult).then_inc(unit_evac, 1)
                if h >= 1:
                    head_norm(h - 1)
                lo_unit(u + 4)
            head_lo(2)
            lo_unit(B_O + 3)
            head_norm(3)
            head_lo(3)
            lo_unit(B_O + 4)
            for m in range(6):
                x_add(B_O + m, m, m % 4)
                x_lo(3, m)
                if m >= 1:
                    lo_unit(B_O + 4 + m)
            ffn(1, 3)
            dve.wait_ge(ss_ready, KT_D * 5 - 2)
            for half in range(2):
                tokens = slice(half * TH, (half + 1) * TH)
                last = X[:, KT_D - 1, tokens]
                dve.wait_ge(last_done, half + 1)
                link(tt(last, PS[:, END_BANKS[half][0], 0:TH], last, ALU.add))
                tt(SQ[:, 1, tokens], last, last, ALU.mult).then_inc(last_sq_ready, 1)
                dve.wait_ge(std_ready, 5 + half)
                inverse = RMS[:, 2 * half:2 * half + 2]
                link(nc.vector.reciprocal(inverse, inverse))
                for t in (2 * half, 2 * half + 1):
                    ts(STD[:, t * P:(t + 1) * P], IDENT[:], RMS[:, t:t + 1], None, ALU.mult).then_inc(diag_ready, 1)
                dve.wait_ge(r_spread, half + 1)
                spread = PS[:, END_BANKS[half][2], 0:TH]
                for m in range(DVE_TILES):
                    if m == 1:
                        nc.vector.tensor_copy(R[:, tokens], spread).then_inc(r_ready, 1)
                        dve.wait_ge(r_ready, 5 + half)
                    stt(X[:, m, tokens], X[:, m, tokens], GAIN[:, 4, m:m + 1], R[:, tokens] if m else spread,
                        ALU.mult, ALU.mult).then_inc(fin_ready, 1)

        @block.gpsimd
        def _(pool):
            steps = [0]

            def link(instruction):
                steps[0] += 1
                instruction.then_inc(pool_step, 1)
                pool.wait_ge(pool_step, steps[0])

            def sum_square(st, m, par=None):
                par = m % 2 if par is None else par
                pool.wait_ge(sq_ready, m + (KT_D * st + 1))
                if isinstance(m, int) and m == 0:
                    if st:
                        pool.wait_ge(std_ready, st)
                    nc.gpsimd.tensor_copy(SS[:], SQ[:, 0]).then_inc(ss_ready, 1)
                    pool.wait_ge(ss_ready, KT_D * st + 1)
                else:
                    nc.gpsimd.tensor_tensor(SS[:], SS[:], SQ[:, par], ALU.add).then_inc(ss_ready, 1)
                    pool.wait_ge(ss_ready, m + (KT_D * st + 1))

            def ffn(layer, st):
                for j in range(2):
                    sum_square(st, 6 + j)
                pool.wait_ge(r_ready, st + 1)
                with pool.Fori(0, FT, 2) as i:
                    for j in range(2):
                        pool.wait_ge(silu_ready, i + (FT * layer + j + 1))
                        nc.gpsimd.tensor_tensor(CV[:, j], CV[:, j], R[:], ALU.mult).then_inc(slr_ready, 1)
                        pool.wait_ge(slr_ready, i + (FT * layer + j + 1))
                for m in range(KT_D if st + 1 < 4 else KT_D - 1):
                    sum_square(st + 1, m)

            nc.gpsimd.memset(ONES[:], 1.0).then_inc(ones_set, 1)
            pool.wait_ge(ones_set, 1)
            nc.gpsimd.memset(EPSC[:], EPS).then_inc(eps_set, 1)
            pool.wait_ge(eps_set, 1)
            link(nc.gpsimd.memset(WG[0:LO, :], 0.0))
            link(nc.gpsimd.memset(KT[64:P, :, 0], 0.0))
            nc.gpsimd.memset(KT[0:64, :, 1], 0.0).then_inc(small_set, 1)
            pool.wait_ge(small_set, 1)
            for m in range(KT_D):
                sum_square(0, m)
            pool.wait_ge(ss_ready, KT_D)
            pool.wait_ge(bias_in, 16 * 4)
            nc.gpsimd.memset(BIAS[:, :, 0:2, 64:P], NEG).then_inc(bias_ready, 1)
            pool.wait_ge(bias_ready, 1)
            nc.gpsimd.tensor_copy(BIAS[:, :, 0:2, 0:64], BIAS[:, :, 2:4, 64:P]).then_inc(bias_ready, 1)
            pool.wait_ge(bias_ready, 2)
            link(nc.gpsimd.memset(GA[:].bitcast(F32), 0.0))
            pool.wait_ge(consts, 16 * CONSTS)
            link(nc.gpsimd.tensor_copy(GA[:, :, 0:RANK], GARAW[:]))
            nc.gpsimd.tensor_tensor(GA[:, :, LO:LO + RANK], GARAW[:], GA[:, :, 0:RANK].bitcast(F32), ALU.subtract)\
                .then_inc(gal_ready, 1)
            pool.wait_ge(gal_ready, 1)
            for m in range(6):
                sum_square(1, m)
            ffn(0, 1)
            pool.wait_ge(unit_done, B_V)
            nc.gpsimd.memset(GAT[0:32, :], 1.0).then_inc(small_set, 2)
            pool.wait_ge(small_set, 3)
            for h in range(BH):
                pool.wait_ge(e_ready, h + 1)
                if h == 0:
                    pool.wait_ge(r_ready, 3)
                nc.gpsimd.tensor_tensor(EP[:, h], EP[:, h], R[:], ALU.mult).then_inc(epr_ready, 1)
                pool.wait_ge(epr_ready, h + 1)
            pool.wait_ge(ga_done, 1)
            nc.gpsimd.memset(AM[:], 0.0).then_inc(am_zero, 1)
            pool.wait_ge(am_zero, 1)
            for h in range(BH):
                pool.wait_ge(unit_evac, B_K + h + 1)
                pool.wait_ge(ln_ready, h + 1)
                nc.gpsimd.tensor_tensor(EU[:, h], EU[:, h], KS[:, h % 2], ALU.mult).then_inc(ku_ready, 1)
                pool.wait_ge(ku_ready, h + 1)
            def head_sum(h):
                pool.wait_ge(o_ready, 2 * h + 2)
                nc.gpsimd.tensor_tensor(SQ[:, 0], SQ[:, 0], SQ[:, 1], ALU.add).then_inc(hsum_ready, 1)
                pool.wait_ge(hsum_ready, h + 1)

            for h in range(BH):
                pool.wait_ge(a_done, h + 1)
                pairs = lambda t: t.rearrange("p (c j t) -> p c j t", j=2, t=CHUNK)
                decay = DEC[:, h].rearrange("p (c j) -> p c j", j=2)
                for n, (t, j) in enumerate(((EU, 0), (EP, 1))):
                    half = pairs(t[:, h])[:, :, j]
                    nc.gpsimd.tensor_tensor(half, half, decay[:, :, 1 - j:2 - j].to_broadcast([P, 4, CHUNK]), ALU.mult)\
                        .then_inc(carried, 1)
                    pool.wait_ge(carried, 2 * h + n + 1)
                if h >= 1:
                    head_sum(h - 1)
            head_sum(3)
            for m in range(6):
                sum_square(3, m)
            ffn(1, 3)
            for half in range(2):
                tokens = slice(half * TH, (half + 1) * TH)
                pool.wait_ge(gained, KT_D - DVE_TILES + half)
                pool.wait_ge(r_ready, 5 + half)
                for i, m in enumerate(range(DVE_TILES, KT_D)):
                    nc.gpsimd.tensor_tensor(X[:, m, tokens], X[:, m, tokens], R[:, tokens], ALU.mult).then_inc(pool_fin, 1)
                    pool.wait_ge(pool_fin, (KT_D - DVE_TILES) * half + i + 1)


def _one_hot():
    rel = np.arange(REL) - 127
    half, exact = 16, 8
    n = np.abs(rel)
    large = exact + (np.log(np.maximum(n, 1).astype(np.float32) / exact) / np.log(128 / exact)
                     * (half - exact)).astype(np.int32)
    bucket = np.where(rel > 0, half, 0) + np.where(n < exact, n, np.minimum(large, half - 1))
    return (bucket[None, :] == np.arange(32)[:, None]).astype(np.float32)


def _causal_pair():
    return np.triu(np.ones((P, P), np.float32))


def _causal():
    s, t = np.arange(P)[:, None], np.arange(P)[None, :]
    return ((s <= t) & (s // CHUNK == t // CHUNK)).astype(np.float32)


def _units(w, k):
    K, N = w.shape
    w = w.reshape(K // (k * P), k, P, N // P, P)
    return np.ascontiguousarray(w.transpose(3, 0, 2, 1, 4)).reshape(-1, P, k * P)


def _rows(v):
    return np.ascontiguousarray(np.moveaxis(v.reshape(*v.shape[:-1], -1, P), -1, 0))


def kernel(x, mix_norm, ffn_norm, final_norm, rel_bias, a_w_qkv, a_sinks, a_w_o, b_w_in, b_w_gate, b_gate_bias,
           b_norm, b_w_o, f_w_up, f_conv_w, f_conv_b, f_w_down):
    import concourse.bacc as bacc
    from concourse.bass_utils import run_bass_kernel_spmd

    x, mix_norm, ffn_norm, final_norm, rel_bias, a_w_qkv, a_sinks, a_w_o, b_w_in, b_w_gate, b_gate_bias, \
        b_norm, b_w_o, f_w_up, f_conv_w, f_conv_b, f_w_down = (
            np.asarray(a) for a in (x, mix_norm, ffn_norm, final_norm, rel_bias, a_w_qkv, a_sinks, a_w_o, b_w_in,
                                    b_w_gate, b_gate_bias, b_norm, b_w_o, f_w_up, f_conv_w, f_conv_b, f_w_down))
    w = a_w_qkv[0]
    nq, nk = A_HEADS * HD, KV * HD
    w_qkv = np.concatenate([w[:, nq:], w[:, :nq]], axis=1)
    w, dk, dv = b_w_in[0], BH * HK, BH * HV
    w_bin = np.concatenate([w[:, 2 * dk:2 * dk + dv], w[:, :2 * dk], w[:, 2 * dk + dv:2 * dk + 2 * dv]], axis=1)
    w_ga = w[:, 2 * dk + 2 * dv:].reshape(KT_D, P, RANK).transpose(1, 0, 2)
    w_up = np.stack([_units(f_w_up[n].reshape(D, 2, FT, P).transpose(0, 2, 1, 3).reshape(D, 2 * FF), KT_D)
                     for n in range(2)])
    sinks = np.repeat(a_sinks[0].reshape(KV, 2, 2).transpose(1, 0, 2), 64, axis=0)
    arrays = {
        "xT": x[0].T.reshape(KT_D, P, T).transpose(1, 0, 2),
        "gains": _rows(np.stack([mix_norm[0], ffn_norm[0], mix_norm[1], ffn_norm[1], final_norm])),
        "w_qkv": _units(w_qkv, KT_D), "sinks": sinks, "rel_bias": rel_bias, "w_o": _units(a_w_o[0], KT_D),
        "w_bin": _units(w_bin, KT_D), "w_ga": w_ga, "w_gate": np.concatenate([b_w_gate[0], b_gate_bias], axis=0),
        "b_norm": _rows(b_norm[0]), "w_bo": _units(b_w_o[0], KT_D), "w_up": w_up,
        "conv_w": f_conv_w.reshape(2, 3, FT, P).transpose(3, 0, 2, 1), "conv_b": _rows(f_conv_b),
        "w_down": np.stack([_units(f_w_down[n], HALF) for n in range(2)]),
        "onehot": _one_hot(), "ident": np.eye(P, dtype=np.float32), "causal": _causal(),
        "causal_pair": _causal_pair(),
    }
    arrays = {k: np.ascontiguousarray(v) for k, v in arrays.items()}
    nc = bacc.Bacc("TRN2", target_bir_lowering=False, num_devices=1, dynamic_dma_scratch_size=1024)
    args = [nc.dram_tensor(k, v.shape, mybir.dt.from_np(v.dtype), kind="ExternalInput").ap() for k, v in arrays.items()]
    out = nc.dram_tensor("out", (P, KT_D, T), F32, kind="ExternalOutput").ap()
    bias_rows = nc.dram_tensor("bias_rows", (A_HEADS, 64 * REL), F32, kind="Internal").ap()
    trunk(nc, *args, out, bias_rows)
    got = run_bass_kernel_spmd(nc, [arrays], core_ids=[0]).results[0]["out"]
    return np.ascontiguousarray(np.asarray(got).transpose(2, 1, 0)).reshape(1, T, D)
```
